# Optimizing a Trainium2 kernel written in Bass

```python
import jax
import jax.numpy as jnp
from jax import lax
import numpy as np
import math

D_MODEL = 1024
BATCH = 1
SEQ = 512
DEPTH = 2

N_A_LAYERS = DEPTH // 2
N_B_LAYERS = DEPTH - N_A_LAYERS
HEAD_DIM = 64
MIX_WIDTH = D_MODEL
MEM_HEADS = 4
MEM_WIDTH = MEM_HEADS * HEAD_DIM
MAIN_WIDTH = MIX_WIDTH - MEM_WIDTH
CHUNK = 128
A_GROUPS = 6
A_GROUP_DIM = MAIN_WIDTH // A_GROUPS
FOX_HEADS = MAIN_WIDTH // HEAD_DIM
Q_BLOCK = 128
N_MEM = 256
D_FF = -(-8 * D_MODEL // (3 * 256)) * 256
RMS_EPS = 1e-6
LN_EPS = 1e-5
FORGET_BIAS = 4.0


def rmsnorm(x, g):
    xf = x.astype(jnp.float32)
    y = xf * lax.rsqrt(jnp.mean(xf * xf, axis=-1, keepdims=True) + RMS_EPS)
    return (y * g.astype(jnp.float32)).astype(x.dtype)

def layernorm(x, g, b):
    xf = x.astype(jnp.float32)
    mu = jnp.mean(xf, axis=-1, keepdims=True)
    xc = xf - mu
    y = xc * lax.rsqrt(jnp.mean(xc * xc, axis=-1, keepdims=True) + LN_EPS)
    return (y * g.astype(jnp.float32) + b.astype(jnp.float32)).astype(x.dtype)

def memory_attention(q_mem, mem_n, w_mem_kv):
    B, S, _ = q_mem.shape
    M = mem_n.shape[1]
    k, v = jnp.split(mem_n @ w_mem_kv, 2, axis=-1)
    q = q_mem.reshape(B, S, MEM_HEADS, HEAD_DIM)
    k = k.reshape(B, M, MEM_HEADS, HEAD_DIM)
    v = v.reshape(B, M, MEM_HEADS, HEAD_DIM)
    logits = jnp.einsum('bshd,bmhd->bhsm', q, k).astype(jnp.float32) * (HEAD_DIM ** -0.5)
    p = jax.nn.softmax(logits, axis=-1).astype(v.dtype)
    o = jnp.einsum('bhsm,bmhd->bshd', p, v)
    return o.reshape(B, S, MEM_WIDTH)

def chunked_spatial_gating(u, v, w_s, b_s, ln_g, ln_b):
    B, S, _ = u.shape
    u = jax.nn.gelu(u)
    v = layernorm(jax.nn.gelu(v), ln_g, ln_b)
    nc = S // CHUNK
    vc = v.reshape(B, nc, CHUNK, A_GROUPS, A_GROUP_DIM)
    mask = jnp.tril(jnp.ones((CHUNK, CHUNK), dtype=bool))
    w = jnp.where(mask[None], w_s, jnp.zeros((), w_s.dtype))
    s = jnp.einsum('gts,bcsgd->bctgd', w, vc) + b_s.T[None, None, :, :, None]
    return u * s.reshape(B, S, MAIN_WIDTH)

def forgetting_attention(q, k, v, log_f):
    B, S, H, Dh = q.shape
    c = jnp.cumsum(log_f, axis=1)
    cT = c.transpose(0, 2, 1)
    nb = S // Q_BLOCK
    qb = q.reshape(B, nb, Q_BLOCK, H, Dh).transpose(1, 0, 2, 3, 4)
    cb = cT.reshape(B, H, nb, Q_BLOCK).transpose(2, 0, 1, 3)
    kpos = jnp.arange(S)
    scale = Dh ** -0.5

    def block(args):
        i, qi, ci = args
        qpos = i * Q_BLOCK + jnp.arange(Q_BLOCK)
        logits = jnp.einsum('bthd,bshd->bhts', qi, k).astype(jnp.float32) * scale
        logits = logits + ci[..., :, None] - cT[..., None, :]
        mask = kpos[None, :] <= qpos[:, None]
        logits = jnp.where(mask, logits, -jnp.inf)
        p = jax.nn.softmax(logits, axis=-1).astype(v.dtype)
        return jnp.einsum('bhts,bshd->bthd', p, v)

    o = lax.map(block, (jnp.arange(nb), qb, cb))
    return o.transpose(1, 0, 2, 3, 4).reshape(B, S, H * Dh)

def first_inputs(seed: int = 0) -> dict:
    key = jax.random.key(seed)
    ks = jax.random.split(key, 24)
    f32 = jnp.float32

    def dense(k, shape, fan_in):
        return jax.random.normal(k, shape, f32) * (fan_in ** -0.5)

    def gain(k, shape):
        return 1.0 + 0.05 * jax.random.normal(k, shape, f32)

    x = jax.random.normal(ks[0], (BATCH, SEQ, D_MODEL), f32)
    mem = jax.random.normal(ks[1], (BATCH, N_MEM, D_MODEL), f32)
    w_shared_kv = jnp.concatenate([
        dense(ks[19], (D_MODEL, 2 * MAIN_WIDTH), D_MODEL),
        0.1 * dense(ks[20], (D_MODEL, FOX_HEADS), D_MODEL)], axis=-1)
    return {
        'x': x,
        'mem': mem,
        'ln_mix_pre': gain(ks[2], (DEPTH, D_MODEL)),
        'ln_mix_post': gain(ks[3], (DEPTH, D_MODEL)),
        'ln_ffn_pre': gain(ks[4], (DEPTH, D_MODEL)),
        'ln_ffn_post': gain(ks[5], (DEPTH, D_MODEL)),
        'ln_mem': gain(ks[6], (DEPTH, D_MODEL)),
        'w_mem_kv': dense(ks[7], (DEPTH, D_MODEL, 2 * MEM_WIDTH), D_MODEL),
        'w_out': dense(ks[8], (DEPTH, MIX_WIDTH, D_MODEL), MIX_WIDTH),
        'w_ffn_gate': dense(ks[9], (DEPTH, D_MODEL, D_FF), D_MODEL),
        'w_ffn_up': dense(ks[10], (DEPTH, D_MODEL, D_FF), D_MODEL),
        'w_ffn_down': dense(ks[11], (DEPTH, D_FF, D_MODEL), D_FF),
        'w_in_a': dense(ks[12], (N_A_LAYERS, D_MODEL, 2 * MAIN_WIDTH + MEM_WIDTH), D_MODEL),
        'w_spatial': dense(ks[13], (N_A_LAYERS, A_GROUPS, CHUNK, CHUNK), CHUNK),
        'b_spatial': 1.0 + 0.05 * jax.random.normal(ks[14], (N_A_LAYERS, A_GROUPS, CHUNK), f32),
        'ln_v_g': gain(ks[15], (N_A_LAYERS, MAIN_WIDTH)),
        'ln_v_b': 0.02 * jax.random.normal(ks[16], (N_A_LAYERS, MAIN_WIDTH), f32),
        'ln_shared': gain(ks[17], (D_MODEL,)),
        'w_shared_kv': w_shared_kv,
        'b_forget': FORGET_BIAS + 0.1 * jax.random.normal(ks[18], (FOX_HEADS,), f32),
        'w_in_b': dense(ks[21], (N_B_LAYERS, D_MODEL, MAIN_WIDTH + MEM_WIDTH), D_MODEL),
    }

def first_block(x, mem, ln_mix_pre, ln_mix_post, ln_ffn_pre, ln_ffn_post, ln_mem,
              w_mem_kv, w_out, w_ffn_gate, w_ffn_up, w_ffn_down, w_in_a,
              w_spatial, b_spatial, ln_v_g, ln_v_b, ln_shared, w_shared_kv,
              b_forget, w_in_b):
    B, S, _ = x.shape
    h = x
    k_s = v_s = log_f_s = None
    for layer in range(DEPTH):
        a = rmsnorm(h, ln_mix_pre[layer])
        mem_n = rmsnorm(mem, ln_mem[layer])
        if layer < N_A_LAYERS:
            proj = a @ w_in_a[layer]
            u = proj[..., :MAIN_WIDTH]
            v = proj[..., MAIN_WIDTH:2 * MAIN_WIDTH]
            q_mem = proj[..., 2 * MAIN_WIDTH:]
            main = chunked_spatial_gating(u, v, w_spatial[layer], b_spatial[layer],
                                          ln_v_g[layer], ln_v_b[layer])
        else:
            if layer == N_A_LAYERS:
                s_in = rmsnorm(h, ln_shared)
                kvf = s_in @ w_shared_kv
                k_s = kvf[..., :MAIN_WIDTH].reshape(B, S, FOX_HEADS, HEAD_DIM)
                v_s = kvf[..., MAIN_WIDTH:2 * MAIN_WIDTH].reshape(B, S, FOX_HEADS, HEAD_DIM)
                log_f_s = jax.nn.log_sigmoid(kvf[..., 2 * MAIN_WIDTH:].astype(jnp.float32)
                                             + b_forget.astype(jnp.float32))
            proj = a @ w_in_b[layer - N_A_LAYERS]
            q = proj[..., :MAIN_WIDTH].reshape(B, S, FOX_HEADS, HEAD_DIM)
            q_mem = proj[..., MAIN_WIDTH:]
            main = forgetting_attention(q, k_s, v_s, log_f_s)
        mixed = jnp.concatenate([main, memory_attention(q_mem, mem_n, w_mem_kv[layer])], axis=-1)
        h = h + rmsnorm(mixed @ w_out[layer], ln_mix_post[layer])
        f = rmsnorm(h, ln_ffn_pre[layer])
        f = (jax.nn.silu(f @ w_ffn_gate[layer]) * (f @ w_ffn_up[layer])) @ w_ffn_down[layer]
        h = h + rmsnorm(f, ln_ffn_post[layer])
    return h


DEPTH_2 = 1

GRID_W = 64
CTX_LEN = 256

RWKV_WIDTH = 512
RWKV_HEAD = 64
RWKV_HEADS = RWKV_WIDTH // RWKV_HEAD
DECAY_LORA = 32
AAA_LORA = 32
GATE_LORA = 96
DIFF_WIDTH = D_MODEL - RWKV_WIDTH
DIFF_HEAD = 64
DIFF_HEADS = DIFF_WIDTH // (2 * DIFF_HEAD)
D_FF_2 = 2816
CONV_W = 3
ROPE_THETA = 10000.0
NORM_EPS = 1e-6
LN_X_EPS = 64e-5
SUBLN_EPS = 1e-5
ATTN_SCALE = DIFF_HEAD ** -0.5

RWKV_SPLITS = (RWKV_WIDTH, 2 * RWKV_WIDTH, 3 * RWKV_WIDTH,
               3 * RWKV_WIDTH + DECAY_LORA, 3 * RWKV_WIDTH + DECAY_LORA + AAA_LORA)
RWKV_COLS = 3 * RWKV_WIDTH + DECAY_LORA + AAA_LORA + GATE_LORA
DIFF_QK = DIFF_HEADS * 2 * DIFF_HEAD
DIFF_V = DIFF_HEADS * 2 * DIFF_HEAD
IN_COLS = RWKV_COLS + 2 * DIFF_QK + DIFF_V


def rmsnorm_2(x, g, eps=NORM_EPS):
    xf = x.astype(jnp.float32)
    y = xf * lax.rsqrt(jnp.mean(xf * xf, axis=-1, keepdims=True) + eps)
    return (y * g.astype(jnp.float32)).astype(x.dtype)

def modulate(h, shift, scale):
    return h * (1.0 + scale) + shift

def adaln(cond, w_mod, b_mod):
    return jax.nn.silu(cond) @ w_mod + b_mod

def dwconv(x, w):
    return lax.conv_general_dilated(
        x, w[:, None, :].astype(x.dtype), window_strides=(1,),
        padding=((CONV_W // 2, CONV_W // 2),),
        dimension_numbers=('NWC', 'WIO', 'NWC'),
        feature_group_count=x.shape[-1])

def axial_rope(rows):
    n_pair = DIFF_HEAD // 4
    row = jnp.repeat(jnp.arange(rows, dtype=jnp.float32), GRID_W)
    col = jnp.tile(jnp.arange(GRID_W, dtype=jnp.float32), rows)
    inv = ROPE_THETA ** (-jnp.arange(n_pair, dtype=jnp.float32) / n_pair)
    ang = jnp.concatenate([row[:, None] * inv, col[:, None] * inv], axis=-1)
    return jnp.cos(ang), jnp.sin(ang)

def apply_rope(x, cos, sin):
    half = DIFF_HEAD // 2
    x1, x2 = x[..., :half], x[..., half:]
    return jnp.concatenate([x1 * cos - x2 * sin, x1 * sin + x2 * cos], axis=-1).astype(x.dtype)

def rwkv_prepare(rw, p):
    B, T, _ = rw.shape
    heads = lambda t: t.reshape(B, T, RWKV_HEADS, RWKV_HEAD)
    r, k, v, wl, al, gl = jnp.split(rw, RWKV_SPLITS, axis=-1)
    kk = heads(k * p['k_k']).astype(jnp.float32)
    kk = kk / jnp.maximum(jnp.linalg.norm(kk, axis=-1, keepdims=True), 1e-12)
    w_lat = jnp.tanh(wl)
    dirs = []
    for w0, w2, a0, a2 in ((p['w0_fwd'], p['w2_fwd'], p['a0_fwd'], p['a2_fwd']),
                           (p['w0_bwd'], p['w2_bwd'], p['a0_bwd'], p['a2_bwd'])):
        w = -jax.nn.softplus(-(w0 + w_lat @ w2).astype(jnp.float32)) - 0.5
        decay = jnp.exp(-jnp.exp(w))
        a = jax.nn.sigmoid((a0 + al @ a2).astype(jnp.float32))
        k_dir = k * (1.0 + (a - 1.0) * p['k_a'])
        dirs.append((heads(decay), heads(k_dir), heads(a)))
    return heads(r), heads(v), kk, gl, dirs

def rwkv_scan(r, decay, k, v, kk, a, s0, reverse):
    tm = lambda t: jnp.swapaxes(t, 0, 1)

    def step(S, inp):
        r_t, w_t, k_t, v_t, kk_t, b_t = inp
        sa = jnp.einsum('bhvk,bhk->bhv', S, kk_t)
        S = (S * w_t[:, :, None, :] - sa[..., None] * b_t[:, :, None, :]
             + v_t[..., None] * k_t[:, :, None, :])
        return S, jnp.einsum('bhvk,bhk->bhv', S, r_t)

    s_fin, ys = lax.scan(step, s0, (tm(r), tm(decay), tm(k), tm(v), tm(kk), tm(kk * a)),
                         reverse=reverse)
    return tm(ys), s_fin

def rwkv_output(y, r, v, k_bonus, gl, p):
    B, T = y.shape[:2]
    mu = jnp.mean(y, axis=-1, keepdims=True)
    var = jnp.mean(jnp.square(y - mu), axis=-1, keepdims=True)
    yn = ((y - mu) * lax.rsqrt(var + LN_X_EPS)).reshape(B, T, RWKV_WIDTH) * p['ln_x_w'] + p['ln_x_b']
    bonus = (jnp.sum(r * k_bonus * p['r_k'], axis=-1, keepdims=True) * v).reshape(B, T, RWKV_WIDTH)
    g = jax.nn.sigmoid(gl) @ p['g2']
    return ((yn + bonus) * g).astype(r.dtype)

def rwkv_mixer(rw, rw_c, p, need_ctx):
    r, v, kk, gl, dirs = rwkv_prepare(rw, p)
    r_c, v_c, kk_c, gl_c, dirs_c = rwkv_prepare(rw_c, p)
    s0 = jnp.zeros((rw.shape[0], RWKV_HEADS, RWKV_HEAD, RWKV_HEAD), jnp.float32)
    ys, ys_c = [], []
    for d, reverse in enumerate((False, True)):
        dec_c, k_c, a_c = dirs_c[d]
        yd_c, s_ctx = rwkv_scan(r_c, dec_c, k_c, v_c, kk_c, a_c, s0, reverse)
        dec, k_d, a_d = dirs[d]
        yd, _ = rwkv_scan(r, dec, k_d, v, kk, a_d, s_ctx, reverse)
        ys.append(yd)
        ys_c.append(yd_c)
    out = rwkv_output(ys[0] + ys[1], r, v, 0.5 * (dirs[0][1] + dirs[1][1]), gl, p)
    out_c = (rwkv_output(ys_c[0] + ys_c[1], r_c, v_c, 0.5 * (dirs_c[0][1] + dirs_c[1][1]), gl_c, p)
             if need_ctx else None)
    return out, out_c

def diff_split(dq):
    B, T, _ = dq.shape
    q, k, v = jnp.split(dq, (DIFF_QK, 2 * DIFF_QK), axis=-1)
    qk = lambda t: t.reshape(B, T, DIFF_HEADS, 2, DIFF_HEAD).transpose(0, 2, 3, 1, 4)
    return qk(q), qk(k), v.reshape(B, T, DIFF_HEADS, 2 * DIFF_HEAD).transpose(0, 2, 1, 3)

def diff_attention(q, k_all, v_all, lam):
    s = jnp.einsum('bhmqd,bhmkd->bhmqk', q, k_all).astype(jnp.float32) * ATTN_SCALE
    pr = jax.nn.softmax(s, axis=-1)
    a = pr[:, :, 0] - lam * pr[:, :, 1]
    return jnp.einsum('bhqk,bhke->bhqe', a.astype(v_all.dtype), v_all)

def diff_post(o, p, lam_init):
    B, H, T, e = o.shape
    o = rmsnorm_2(o, p['subln_w'], SUBLN_EPS) * (1.0 - lam_init)
    return o.transpose(0, 2, 1, 3).reshape(B, T, H * e)

def diff_mixer(dq, dq_c, p, lam_init, cos, sin, need_ctx):
    q, k, v = diff_split(dq)
    q_c, k_c, v_c = diff_split(dq_c)
    q, k = apply_rope(q, cos, sin), apply_rope(k, cos, sin)
    f32 = lambda t: t.astype(jnp.float32)
    lam = (jnp.exp(jnp.sum(f32(p['lam_q1']) * f32(p['lam_k1'])))
           - jnp.exp(jnp.sum(f32(p['lam_q2']) * f32(p['lam_k2']))) + lam_init)
    k_all = jnp.concatenate([k_c, k], axis=3)
    v_all = jnp.concatenate([v_c, v], axis=2)
    B, H, _, T, d = q.shape
    nb = T // Q_BLOCK
    qb = q.reshape(B, H, 2, nb, Q_BLOCK, d).transpose(3, 0, 1, 2, 4, 5)
    o = lax.map(lambda qq: diff_attention(qq, k_all, v_all, lam), qb)
    o = o.transpose(1, 2, 0, 3, 4).reshape(B, H, T, 2 * d)
    out = diff_post(o, p, lam_init)
    out_c = diff_post(diff_attention(q_c, k_c, v_c, lam), p, lam_init) if need_ctx else None
    return out, out_c

def token_mixer(h, h_c, p, lam_init, cos, sin, need_ctx):
    parts = h @ p['w_in']
    parts_c = h_c @ p['w_in']
    rw = dwconv(parts[..., :RWKV_COLS], p['rwkv_conv'])
    rw_c = dwconv(parts_c[..., :RWKV_COLS], p['rwkv_conv'])
    y_r, y_r_c = rwkv_mixer(rw, rw_c, p, need_ctx)
    y_d, y_d_c = diff_mixer(parts[..., RWKV_COLS:], parts_c[..., RWKV_COLS:], p, lam_init,
                            cos, sin, need_ctx)
    out = jnp.concatenate([y_r, y_d], axis=-1) @ p['w_out']
    out_c = jnp.concatenate([y_r_c, y_d_c], axis=-1) @ p['w_out'] if need_ctx else None
    return out, out_c

def conv_ffn(h, p):
    u = dwconv(h @ p['w_up'], p['ffn_conv']) + p['ffn_conv_b']
    val, gate = jnp.split(u, 2, axis=-1)
    return (val * jax.nn.silu(gate)) @ p['w_down']

def second_inputs(seed: int = 0) -> dict:
    key = jax.random.key(seed)
    keys = jax.random.split(key, 36)
    L, D, Rw = DEPTH_2, D_MODEL, RWKV_WIDTH

    def nrm(i, shape, s):
        return s * jax.random.normal(keys[i], shape, jnp.float32)

    def uni(i, shape, lo, hi):
        return jax.random.uniform(keys[i], shape, jnp.float32, lo, hi)

    conv_base = jnp.array([0.25, 0.5, 0.25], jnp.float32)[None, :, None]
    return {
        'x': nrm(0, (BATCH, SEQ, D), 1.0),
        'c': nrm(1, (BATCH, D), 1.0),
        'ctx': nrm(2, (BATCH, CTX_LEN, D), 1.0),
        'c_ctx': nrm(3, (D,), 1.0),
        'w_mod': nrm(4, (L, D, 6 * D), 0.5 * D ** -0.5),
        'b_mod': nrm(5, (L, 6 * D), 0.02),
        'g_pre_mix': 1.0 + nrm(6, (L, D), 0.05),
        'g_post_mix': 1.0 + nrm(7, (L, D), 0.05),
        'g_pre_ffn': 1.0 + nrm(8, (L, D), 0.05),
        'g_post_ffn': 1.0 + nrm(9, (L, D), 0.05),
        'w_in': nrm(10, (L, D, IN_COLS), D ** -0.5),
        'rwkv_conv': conv_base + nrm(11, (L, CONV_W, RWKV_COLS), 0.1),
        'w0_fwd': uni(12, (L, Rw), -6.5, -1.5),
        'w2_fwd': nrm(13, (L, DECAY_LORA, Rw), 0.1),
        'a0_fwd': nrm(14, (L, Rw), 0.1),
        'a2_fwd': nrm(15, (L, AAA_LORA, Rw), 0.1),
        'w0_bwd': uni(16, (L, Rw), -6.5, -1.5),
        'w2_bwd': nrm(17, (L, DECAY_LORA, Rw), 0.1),
        'a0_bwd': nrm(18, (L, Rw), 0.1),
        'a2_bwd': nrm(19, (L, AAA_LORA, Rw), 0.1),
        'g2': nrm(20, (L, GATE_LORA, Rw), GATE_LORA ** -0.5),
        'k_k': 0.85 + nrm(21, (L, Rw), 0.05),
        'k_a': 1.0 + nrm(22, (L, Rw), 0.05),
        'r_k': nrm(23, (L, RWKV_HEADS, RWKV_HEAD), 0.1),
        'ln_x_w': 1.0 + nrm(24, (L, Rw), 0.05),
        'ln_x_b': nrm(25, (L, Rw), 0.02),
        'lam_q1': nrm(26, (L, DIFF_HEAD), 0.1),
        'lam_k1': nrm(27, (L, DIFF_HEAD), 0.1),
        'lam_q2': nrm(28, (L, DIFF_HEAD), 0.1),
        'lam_k2': nrm(29, (L, DIFF_HEAD), 0.1),
        'subln_w': 1.0 + nrm(30, (L, 2 * DIFF_HEAD), 0.05),
        'w_out': nrm(31, (L, D, D), D ** -0.5),
        'w_up': nrm(32, (L, D, 2 * D_FF_2), D ** -0.5),
        'ffn_conv': conv_base + nrm(33, (L, CONV_W, 2 * D_FF_2), 0.1),
        'ffn_conv_b': nrm(34, (L, 2 * D_FF_2), 0.02),
        'w_down': nrm(35, (L, D_FF_2, D), D_FF_2 ** -0.5),
    }

def second_block(x, c, ctx, c_ctx, w_mod, b_mod, g_pre_mix, g_post_mix, g_pre_ffn, g_post_ffn,
              w_in, rwkv_conv, w0_fwd, w2_fwd, a0_fwd, a2_fwd, w0_bwd, w2_bwd, a0_bwd, a2_bwd,
              g2, k_k, k_a, r_k, ln_x_w, ln_x_b, lam_q1, lam_k1, lam_q2, lam_k2, subln_w,
              w_out, w_up, ffn_conv, ffn_conv_b, w_down):
    n_tok = x.shape[1]
    ROWS = n_tok // GRID_W
    cos, sin = axial_rope(ROWS)
    for l in range(DEPTH_2):
        p = dict(g_pre_mix=g_pre_mix[l], g_post_mix=g_post_mix[l], g_pre_ffn=g_pre_ffn[l],
                 g_post_ffn=g_post_ffn[l], w_in=w_in[l], rwkv_conv=rwkv_conv[l],
                 w0_fwd=w0_fwd[l], w2_fwd=w2_fwd[l], a0_fwd=a0_fwd[l], a2_fwd=a2_fwd[l],
                 w0_bwd=w0_bwd[l], w2_bwd=w2_bwd[l], a0_bwd=a0_bwd[l], a2_bwd=a2_bwd[l],
                 g2=g2[l], k_k=k_k[l], k_a=k_a[l], r_k=r_k[l], ln_x_w=ln_x_w[l], ln_x_b=ln_x_b[l],
                 lam_q1=lam_q1[l], lam_k1=lam_k1[l], lam_q2=lam_q2[l], lam_k2=lam_k2[l],
                 subln_w=subln_w[l], w_out=w_out[l], w_up=w_up[l], ffn_conv=ffn_conv[l],
                 ffn_conv_b=ffn_conv_b[l], w_down=w_down[l])
        lam_init = 0.8 - 0.6 * math.exp(-0.3 * l)
        need_ctx = l + 1 < DEPTH_2
        mod = adaln(c, w_mod[l], b_mod[l])[:, None, :]
        mod_c = adaln(c_ctx[None, :], w_mod[l], b_mod[l])[:, None, :]
        sh1, sc1, gt1, sh2, sc2, gt2 = jnp.split(mod, 6, axis=-1)
        sh1c, sc1c, gt1c, sh2c, sc2c, gt2c = jnp.split(mod_c, 6, axis=-1)
        h = modulate(rmsnorm_2(x, p['g_pre_mix']), sh1, sc1)
        h_c = modulate(rmsnorm_2(ctx, p['g_pre_mix']), sh1c, sc1c)
        y, y_c = token_mixer(h, h_c, p, lam_init, cos, sin, need_ctx)
        x = x + gt1 * rmsnorm_2(y, p['g_post_mix'])
        h = modulate(rmsnorm_2(x, p['g_pre_ffn']), sh2, sc2)
        x = x + gt2 * rmsnorm_2(conv_ffn(h, p), p['g_post_ffn'])
        if need_ctx:
            ctx = ctx + gt1c * rmsnorm_2(y_c, p['g_post_mix'])
            h_c = modulate(rmsnorm_2(ctx, p['g_pre_ffn']), sh2c, sc2c)
            ctx = ctx + gt2c * rmsnorm_2(conv_ffn(h_c, p), p['g_post_ffn'])
    return x


def setup_inputs(seed=0):
    out = dict(first_inputs(seed))
    for name, value in second_inputs(seed + 1).items():
        if name != "x":
            out[name + "_2"] = value
    return out


def reference(
    x, mem, ln_mix_pre, ln_mix_post, ln_ffn_pre, ln_ffn_post, ln_mem, w_mem_kv, w_out,
    w_ffn_gate, w_ffn_up, w_ffn_down, w_in_a, w_spatial, b_spatial, ln_v_g, ln_v_b, ln_shared,
    w_shared_kv, b_forget, w_in_b, c_2, ctx_2, c_ctx_2, w_mod_2, b_mod_2, g_pre_mix_2,
    g_post_mix_2, g_pre_ffn_2, g_post_ffn_2, w_in_2, rwkv_conv_2, w0_fwd_2, w2_fwd_2, a0_fwd_2,
    a2_fwd_2, w0_bwd_2, w2_bwd_2, a0_bwd_2, a2_bwd_2, g2_2, k_k_2, k_a_2, r_k_2, ln_x_w_2,
    ln_x_b_2, lam_q1_2, lam_k1_2, lam_q2_2, lam_k2_2, subln_w_2, w_out_2, w_up_2, ffn_conv_2,
    ffn_conv_b_2, w_down_2,
):
    x = first_block(
        x, mem, ln_mix_pre, ln_mix_post, ln_ffn_pre, ln_ffn_post, ln_mem, w_mem_kv, w_out,
        w_ffn_gate, w_ffn_up, w_ffn_down, w_in_a, w_spatial, b_spatial, ln_v_g, ln_v_b,
        ln_shared, w_shared_kv, b_forget, w_in_b,
    )
    return second_block(
        x, c_2, ctx_2, c_ctx_2, w_mod_2, b_mod_2, g_pre_mix_2, g_post_mix_2, g_pre_ffn_2,
        g_post_ffn_2, w_in_2, rwkv_conv_2, w0_fwd_2, w2_fwd_2, a0_fwd_2, a2_fwd_2, w0_bwd_2,
        w2_bwd_2, a0_bwd_2, a2_bwd_2, g2_2, k_k_2, k_a_2, r_k_2, ln_x_w_2, ln_x_b_2, lam_q1_2,
        lam_k1_2, lam_q2_2, lam_k2_2, subln_w_2, w_out_2, w_up_2, ffn_conv_2, ffn_conv_b_2,
        w_down_2,
    )


_drawn_inputs = setup_inputs


def setup_inputs(seed=0):
    import zlib

    import numpy as np

    out = dict(_drawn_inputs(seed))
    spreads = {}
    factors = {'ln_mem': 5.145,
     'ln_v_b': 5.96,
     'b_forget': 28.248,
     'b_mod_2': 3.492,
     'g_pre_mix_2': 6.924,
     'g_post_mix_2': 8.0,
     'g_pre_ffn_2': 5.818,
     'g_post_ffn_2': 8.0,
     'w2_fwd_2': 43.373,
     'a0_fwd_2': 8.0,
     'a2_fwd_2': 5.32,
     'w2_bwd_2': 41.506,
     'a0_bwd_2': 8.0,
     'a2_bwd_2': 5.351,
     'k_a_2': 2.724,
     'r_k_2': 3.559,
     'ln_x_w_2': 200.0,
     'ln_x_b_2': 200.0,
     'lam_q1_2': 8.0,
     'lam_k1_2': 8.0,
     'lam_q2_2': 39.027,
     'lam_k2_2': 8.0,
     'subln_w_2': 200.0,
     'ffn_conv_b_2': 8.0,
     'ln_shared': 5.384,
     'c_ctx_2': 2.803,
     'w0_fwd_2': 6.923,
     'w0_bwd_2': 6.378,
     'k_k_2': 44.321}
    for name, (base, spread) in spreads.items():
        noise = np.random.default_rng([zlib.crc32(name.encode()), seed]).standard_normal(out[name].shape)
        drawn = base * np.exp(spread * noise) if base else spread * noise
        out[name] = jnp.asarray(drawn.astype(out[name].dtype))
    for name, factor in factors.items():
        out[name] = (out[name] * factor).astype(out[name].dtype)
    return out
```

```python
from contextlib import ExitStack

import numpy as np

import concourse.bass as bass
from concourse import mybir

F32 = mybir.dt.float32
ALU = mybir.AluOpType
ACT = mybir.ActivationFunctionType
AX_X = mybir.AxisListType.X

P = 128
D = 1024
KD = D // P
S = 512
NM = 256
NC_CTX = 256
D_FF = 2816
KF = D_FF // P
MAIN = 768
HEAD = 64
RMS_EPS = 1e-6
LN_EPS = 1e-5
SUBLN_EPS = 1e-5
NEG = -1e30
SLOTS = 4
SLOT_WORDS = 2048

O_H = 0
O_RING = O_H + KD * S
O_MEM = O_RING + SLOTS * SLOT_WORDS
O_CTX = O_MEM + KD * NM
O_VEC = O_CTX + KD * NC_CTX
O_CST = O_VEC + 512
O_MOD = O_CST + 512
O_SML = O_MOD + 256
O_ARENA = O_SML + 256
WORDS = 53100

ROWS = [
    [("ln_mix_pre", 16), ("ln_mix_post", 16), ("ln_ffn_pre", 16), ("ln_ffn_post", 16), ("ln_mem", 16),
     ("ln_shared", 8), ("c_2", 8), ("c_ctx_2", 8), ("g_pre_mix_2", 8), ("g_post_mix_2", 8), ("g_pre_ffn_2", 8)],
    [("g_post_ffn_2", 8), ("b_mod_2", 48), ("w0_fwd_2", 4), ("a0_fwd_2", 4), ("w0_bwd_2", 4), ("a0_bwd_2", 4),
     ("k_k_2", 4), ("k_a_2", 4), ("r_k_2", 4), ("ln_x_w_2", 4), ("ln_x_b_2", 4),
     ("rwkv_tap0", 12), ("rwkv_tap1", 12), ("rwkv_tap2", 12)],
    [("ffn_tap0", 44), ("ffn_tap1", 44)],
    [("ffn_tap2", 44), ("ffn_conv_b_2", 44), ("subln_w_2", 1), ("rwkv_wa_taps", 3), ("rwkv_g_taps", 3)],
]
VCOL = {}
for _t, _rows in enumerate(ROWS):
    _r = 0
    for _name, _n in _rows:
        VCOL[_name] = _t * P + _r
        _r += _n


class Chain:

    def __init__(self, eng, sem):
        self.eng, self.sem, self.count, self.per, self.i, self.k = eng, sem, 0, 0, None, 0

    def link(self, ins):
        ins.then_inc(self.sem, 1)
        if self.i is None:
            self.count += 1
            self.eng.wait_ge(self.sem, self.count)
        else:
            self.k += 1
            self.eng.wait_ge(self.sem, self.i * self.per + (self.count + self.k))

    def enter(self, i, per):
        self.i, self.per, self.k = i, per, 0

    def leave(self, trips):
        assert self.k == self.per, (self.k, self.per)
        self.count += trips * self.per
        self.i = None


class Stream:

    def __init__(self, k, eng):
        self.k, self.eng, self.n, self.i, self.per = k, eng, 0, None, 0

    def enter(self, i, per):
        assert per % SLOTS == 0
        self.i, self.per, self.start = i, per, self.n

    def leave(self, trips):
        assert self.n - self.start == self.per
        self.n = self.start + trips * self.per
        self.i = None

    def load(self, src, kc, cols):
        n, e = self.n, self.eng
        if n >= SLOTS:
            need = 2 * (n - SLOTS + 1)
            e.wait_ge(self.k.half_done, need if self.i is None else self.i * (2 * self.per) + need)
        e.dma_start(self.k.slot(n % SLOTS, kc, cols), src).then_inc(self.k.tile_landed[n % SLOTS], 16)
        self.n += 1

    def take(self, kc, cols):
        n = self.n
        need = 16 * (n // SLOTS + 1)
        if self.i is not None:
            need = self.i * (16 * (self.per // SLOTS)) + need
        self.eng.wait_ge(self.k.tile_landed[n % SLOTS], need)
        self.n += 1
        return self.k.slot(n % SLOTS, kc, cols)


class Kit:
    pass


def view(M, off, *dims):
    n = int(np.prod(dims))
    v = M[:, off:off + n]
    if len(dims) == 1:
        return v
    names = "abcde"[:len(dims)]
    return v.rearrange("p (" + " ".join(names) + ") -> p " + " ".join(names),
                       **{c: d for c, d in zip(names[1:], dims[1:])})


def col(k, name, j=0):
    c = O_VEC + VCOL[name] + j
    return k.M[:, c:c + 1]


A_XTOK = O_ARENA
A_MTOK = A_XTOK + 4 * D
A_CTOK = A_MTOK + 2 * D
A_ROWS = A_CTOK + 2 * D


def turns(k):
    M = k.M
    x, m, c, r = view(M, A_XTOK, 4, D), view(M, A_MTOK, 2, D), view(M, A_CTOK, 2, D), view(M, A_ROWS, 4, P)
    out = [([r[:, t, :] for t in range(4)], M[:, O_VEC:O_VEC + 512])]
    for f in range(KD):
        out.append(([x[:, t, f * P:(f + 1) * P] for t in range(4)], M[:, O_H + f * S:O_H + (f + 1) * S]))
    for f in range(0, KD, 2):
        out.append(([m[:, t, g * P:(g + 1) * P] for g in (f, f + 1) for t in range(2)],
                    M[:, O_MEM + f * NM:O_MEM + (f + 2) * NM]))
    for f in range(0, KD, 2):
        out.append(([c[:, t, g * P:(g + 1) * P] for g in (f, f + 1) for t in range(2)],
                    M[:, O_CTX + f * NM:O_CTX + (f + 2) * NM]))
    return out


def setup_sync(k, sp):
    M, a = k.M, k.a
    sp.dma_start(M[:, O_CST:O_CST + 512], a["const_base"]).then_inc(k.const_in, 16)
    sp.dma_start(view(M, A_XTOK, 4, D), a["x"][0].rearrange("(t p) d -> p t d", p=P)).then_inc(k.const_in, 16)
    rows = view(M, A_ROWS, 4, P)
    sp.wait_ge(k.rows_clear, 1)
    n = 0
    for name, (t, r, cnt, width, src) in k.row_sources.items():
        sp.dma_start(rows[r:r + cnt, t, 0:width], src).then_inc(k.rows_in, 16)
        n += 1
    assert n == k.n_rows
    sp.dma_start(view(M, A_MTOK, 2, D), a["mem"][0].rearrange("(t p) d -> p t d", p=P)).then_inc(k.tok_in, 16)
    sp.dma_start(view(M, A_CTOK, 2, D), a["ctx_2"][0].rearrange("(t p) d -> p t d", p=P)).then_inc(k.tok_in, 16)


def setup_tensor(k, pe):
    pe.wait_ge(k.const_in, 32)
    pe.wait_ge(k.rows_in, 16 * k.n_rows)
    for n, (blocks, _) in enumerate(turns(k)):
        if n == 1 + KD:
            pe.wait_ge(k.tok_in, 32)
        if n >= 4:
            pe.wait_ge(k.turn_read, n - 3)
        for j, b in enumerate(blocks):
            mm = pe.transpose(k.bank[n % 4][:, j * P:(j + 1) * P], b, k.ident)
        mm.then_inc(k.turned, 1)


def setup_vector(k, dve):
    dve.memset(view(k.M, A_ROWS, 512), 0.0).then_inc(k.rows_clear, 1)
    for n, (_, dst) in enumerate(turns(k)):
        dve.wait_ge(k.turned, n + 1)
        dve.tensor_copy(dst, k.bank[n % 4][:, :]).then_inc(k.turn_read, 1)


class Norm:
    def __init__(self, k, name, src, n, outs, scratch, post=None, then=None):
        self.src, self.n, self.outs, self.post = src, n, outs, post
        self.sq = view(k.M, scratch, 2, n)
        self.acc = view(k.M, scratch + 2 * n, n)
        self.rstd = view(k.M, scratch + 3 * n, n)
        self.tmp = view(k.M, scratch + 4 * n, 2, n)
        self.nth, k.norms = k.norms, k.norms + 1
        self.pth = k.posts
        s = k.norm_sems
        self.squared, self.added, self.summed, self.inverted = s["squared"], s["added"], s["summed"], s["inverted"]
        self.rooted, self.scaled, self.moved = s["rooted"], s["scaled"], s["moved"]


def norm_scalar(k, act, j, bank):
    for c in range(KD):
        if c >= 2:
            act.wait_ge(j.added, KD * j.nth + c - 1)
        if j.post == "chained":
            act.wait_ge(j.moved, KD * j.src_post + c + 1)
        act.activation(j.sq[:, c % 2, :], j.src[:, c, :], ACT.Square).then_inc(j.squared, 1)
    act.wait_ge(j.inverted, j.nth + 1)
    act.activation(j.rstd, j.rstd, ACT.Sqrt).then_inc(j.rooted, 1)


def norm_tensor(k, pe, j, bank):
    pe.wait_ge(j.added, KD * (j.nth + 1))
    pe.matmul(bank[:, :j.n], k.ones, j.acc, start=True, stop=True).then_inc(j.summed, 1)


def norm_sum_vector(k, dve, j, bank):
    for c in range(KD):
        dve.wait_ge(j.squared, KD * j.nth + c + 1)
        if c == 0:
            dve.tensor_copy(j.acc, j.sq[:, 0, :]).then_inc(j.added, 1)
        else:
            dve.wait_ge(j.added, KD * j.nth + c)
            dve.tensor_tensor(j.acc, j.acc, j.sq[:, c % 2, :], ALU.add).then_inc(j.added, 1)
    dve.wait_ge(j.summed, j.nth + 1)
    k.dve.link(dve.tensor_scalar(j.rstd, bank[:, :j.n], 1.0 / D, RMS_EPS, ALU.mult, ALU.add))
    dve.reciprocal(j.rstd, j.rstd).then_inc(j.inverted, 1)
    dve.wait_ge(j.rooted, j.nth + 1)


def norm_scale_vector(k, dve, j):
    for gain, dst, shift in j.outs:
        for c in range(KD):
            ins = dve.scalar_tensor_tensor(out=dst[:, c, :], in0=j.src[:, c, :], scalar=gain(c), in1=j.rstd,
                                           op0=ALU.mult, op1=ALU.mult)
            if shift is not None:
                k.dve.link(ins)
                dve.tensor_scalar(dst[:, c, :], dst[:, c, :], shift(c), None, ALU.add)


def post_scale_vector(k, dve, j, gain):
    for c in range(KD):
        if c >= 2:
            dve.wait_ge(j.moved, KD * j.pth + c - 1)
        dve.scalar_tensor_tensor(out=j.tmp[:, c % 2, :], in0=j.src[:, c, :], scalar=gain(c), in1=j.rstd,
                                 op0=ALU.mult, op1=ALU.mult).then_inc(j.scaled, 1)


def post_add_pool(k, pool, j):
    H = k.H
    for c in range(KD):
        pool.wait_ge(j.scaled, KD * j.pth + c + 1)
        pool.tensor_tensor(H[:, c, :], H[:, c, :], j.tmp[:, c % 2, :], ALU.add).then_inc(j.moved, 1)


class Phase:

    def __init__(self, name, sync=None, tensor=None, vector=None, scalar=None, pool=None):
        self.name, self.sync, self.tensor, self.vector, self.scalar, self.pool = name, sync, tensor, vector, scalar, pool


def block_feature(pe, bank, w, c0, m, rhs, kc, k0=0, start=True, stop=True):
    for q in range(kc):
        mm = pe.matmul(bank, w[:, q, c0:c0 + m], rhs(k0 + q), start=start and q == 0, stop=stop and q == kc - 1)
    return mm


def block_token(pe, bank, act_chunk, w, kc):
    for q in range(kc):
        mm = pe.matmul(bank, act_chunk(q), w[:, q, :], start=q == 0, stop=q == kc - 1)
    return mm


def build(nc, a, out, stop=None, consts=None):
    k = Kit()
    k.a = a
    with ExitStack() as ctx:
        k.M = ctx.enter_context(nc.sbuf_tensor("sbuf", [P, WORDS], F32))
        k.psum = ctx.enter_context(nc.psum_tensor("psum", [P, 8 * 512], F32))
        k.bank = [k.psum[:, 512 * i:512 * (i + 1)] for i in range(8)]
        names = []

        def sem(name):
            names.append(name)
            return ctx.enter_context(nc.semaphore(name))

        k.sem = sem
        M = k.M
        k.ident = M[:, O_CST:O_CST + P]
        k.ones = M[:, O_CST + P:O_CST + 2 * P]
        k.causal = M[:, O_CST + 2 * P:O_CST + 3 * P]
        k.lower = M[:, O_CST + 3 * P:O_CST + 4 * P]
        k.H = view(M, O_H, KD, S)
        k.memT = view(M, O_MEM, KD, NM)
        k.ctxT = view(M, O_CTX, KD, NC_CTX)
        k.slot = lambda n, kc, cols: view(M, O_RING + n * SLOT_WORDS, kc, cols)
        k.const_in, k.tok_in, k.rows_in, k.rows_clear = sem("const_in"), sem("tok_in"), sem("rows_in"), sem("rows_clear")
        k.turned, k.turn_read, k.out_sent, k.half_done = sem("turned"), sem("turn_read"), sem("out_sent"), sem("half_done")
        k.dve_steps, k.act_steps, k.pool_steps = sem("dve_steps"), sem("act_steps"), sem("pool_steps")
        k.norms, k.posts = 0, 0
        k.norm_sems = {s: sem(f"norm_{s}") for s in ("squared", "added", "summed", "inverted", "rooted", "scaled", "moved")}
        k.tile_landed = [sem(f"tile_landed{i}") for i in range(SLOTS)]
        k.phase_end = {e: sem(f"phase_end_{e}") for e in ("tensor", "vector", "scalar", "pool")}

        k.row_sources = {}
        for t, rows in enumerate(ROWS):
            r = 0
            for name, n in rows:
                w = P
                if name in a:
                    h = a[name]
                    src = h.rearrange(" ".join("abcd"[:len(h.shape)]) + " -> (" + " ".join("abcd"[:len(h.shape)]) + ")") if len(h.shape) > 1 else h
                    src = src.rearrange("(c p) -> c p", p=P)
                elif name.startswith("rwkv_tap"):
                    src = a["rwkv_conv_2"][0, int(name[-1]), 0:12 * P].rearrange("(c p) -> c p", p=P)
                elif name.startswith("ffn_tap"):
                    src = a["ffn_conv_2"][0, int(name[-1])].rearrange("(c p) -> c p", p=P)
                elif name == "rwkv_wa_taps":
                    src, w = a["rwkv_conv_2"][0, :, 1536:1600], 64
                else:
                    src, w = a["rwkv_conv_2"][0, :, 1600:1696], 96
                k.row_sources[name] = (t, r, n, w, src)
                r += n
        k.n_rows = len(k.row_sources)

        phases = [Phase("setup", sync=setup_sync, tensor=setup_tensor, vector=setup_vector)]
        phases += first_block_phases(k, stop)
        if stop is None or stop.endswith("2"):
            phases += second_block_phases(k, stop)
        k.phase_index = {p.name: n for n, p in enumerate(phases)}
        phases.append(final_phase(k, out))
        block = ctx.enter_context(nc.Block())

        def boundary(eng, me, n):
            eng.drain().then_inc(k.phase_end[me], 1)
            for other, s in k.phase_end.items():
                if other != me:
                    eng.wait_ge(s, n + 1)

        @block.sync
        def _(sp):
            k.sp_stream = Stream(k, sp)
            for ph in phases:
                if ph.sync:
                    ph.sync(k, sp)

        @block.tensor
        def _(pe):
            k.pe_stream = Stream(k, pe)
            for n, ph in enumerate(phases):
                if ph.tensor:
                    ph.tensor(k, pe)
                boundary(pe, "tensor", n)

        @block.vector
        def _(dve):
            k.dve = Chain(dve, k.dve_steps)
            for n, ph in enumerate(phases):
                if ph.vector:
                    ph.vector(k, dve)
                boundary(dve, "vector", n)

        @block.scalar
        def _(act):
            k.act = Chain(act, k.act_steps)
            for n, ph in enumerate(phases):
                if ph.scalar:
                    ph.scalar(k, act)
                boundary(act, "scalar", n)

        @block.gpsimd
        def _(pool):
            k.pool = Chain(pool, k.pool_steps)
            for n, ph in enumerate(phases):
                if ph.pool:
                    ph.pool(k, pool)
                boundary(pool, "pool", n)


A_A = O_ARENA
A_B = A_A + KD * S
A_MIX = A_B + KD * S
A_Y = A_MIX + KD * S
A_HID = A_Y + KD * S
A_SCR = A_HID + KF * S
A_TMP = A_SCR + 6 * S
assert A_TMP + 4 * S <= WORDS
A_MN = A_HID
A_KM = A_MN + KD * NM
A_VM = A_KM + 2 * NM
A_QM = A_VM + 2 * NM
A_V = A_QM + 2 * S
A_K = A_V + 4 * MAIN
assert A_K + 6 * S <= A_SCR
A_Q = A_Y
A_NEGC = A_Y + 6 * S
A_WS = A_Y
A_BC = A_Y + 2 * 6 * P
A_PT = A_A
A_PR = A_TMP


def norm_phase(k, name, jobs, post=None):

    def tensor(k, pe):
        if post:
            norm_tensor(k, pe, post[0], k.bank[7])
        for n, j in enumerate(jobs):
            norm_tensor(k, pe, j, k.bank[n])

    def scalar(k, act):
        if post:
            norm_scalar(k, act, post[0], k.bank[7])
        for n, j in enumerate(jobs):
            norm_scalar(k, act, j, k.bank[n])

    def vector(k, dve):
        if post:
            norm_sum_vector(k, dve, post[0], k.bank[7])
            post_scale_vector(k, dve, post[0], post[1])
        for n, j in enumerate(jobs):
            norm_sum_vector(k, dve, j, k.bank[n])
            norm_scale_vector(k, dve, j)

    def pool(k, pool):
        if post:
            post_add_pool(k, pool, post[0])

    return Phase(name, tensor=tensor, scalar=scalar, vector=vector, pool=pool)


def make_norm(k, name, src, n, outs, scratch, after=None):
    j = Norm(k, name, src, n, outs, scratch)
    if not outs:
        k.posts += 1
    if after is not None:
        j.post, j.src_post = "chained", after.pth
    return j


def mem_projection(k, L):
    t0 = k.plan
    k.plan += 2
    MN, KM, VM = view(k.M, A_MN, KD, NM), view(k.M, A_KM, 2, NM), view(k.M, A_VM, 2, NM)
    w = k.a["w_mem_kv"][L].rearrange("(c p) n -> p c n", p=P)

    def sync(k, sp):
        for t in range(2):
            k.sp_stream.load(w[:, :, t * 256:(t + 1) * 256], KD, 256)

    def tensor(k, pe):
        wk = k.pe_stream.take(KD, 256)
        for b in range(2):
            block_feature(pe, k.bank[b][:, :NM], wk, b * P, P, lambda q: MN[:, q, :], KD).then_inc(k.half_done, 1)
        wv = k.pe_stream.take(KD, 256)
        for t in range(2):
            block_token(pe, k.bank[2 + t][:, :NM], lambda q: MN[:, q, t * P:(t + 1) * P], wv, KD).then_inc(k.half_done, 1)

    def vector(k, dve):
        for b in range(4):
            dve.wait_ge(k.half_done, 2 * t0 + b + 1)
            dst = KM[:, b, :] if b < 2 else VM[:, b - 2, :]
            dve.tensor_copy(dst, k.bank[b][:, :NM])

    return Phase(f"mem_projection{L}", sync=sync, tensor=tensor, vector=vector)


def load_columns(k, w, c0, c1):
    for c in range(c0, c1, 256):
        k.sp_stream.load(w[:, :, c:min(c + 256, c1)], KD, min(256, c1 - c))


def input_projection_a(k):
    t0 = k.plan
    k.plan += 7
    M = k.M
    A, U, V, QM = view(M, A_A, KD, S), view(M, A_B, 6, S), view(M, A_V, 4, MAIN), view(M, A_QM, 2, S)
    w = k.a["w_in_a"][0].rearrange("(c p) n -> p c n", p=P)
    read = k.sem("in_a_read")
    halves = [("u", b) for b in range(6)] + [("v", c, t) for c in range(3) for t in range(2)] + [("q", b) for b in range(2)]

    def sync(k, sp):
        load_columns(k, w, 0, 1792)
        sp.dma_start(view(M, A_WS, 6, P), k.a["w_spatial"][0].rearrange("g t s -> t g s")).then_inc(k.ws_in, 16)
        for n, name in enumerate(("ln_v_g", "ln_v_b")):
            sp.dma_start(view(M, A_BC, 3, MAIN)[:, n, :], k.a[name].broadcast_to([P, MAIN])).then_inc(k.ws_in, 16)
        sp.dma_start(view(M, A_BC, 3, MAIN)[:, 2, :],
                     k.a["b_spatial"].rearrange("a g t -> a (g t)").broadcast_to([P, MAIN])).then_inc(k.ws_in, 16)

    def tensor(k, pe):
        for h, half in enumerate(halves):
            if h % 2 == 0:
                wt = k.pe_stream.take(KD, 256)
            if h >= 4:
                pe.wait_ge(read, h - 3)
            bank = k.bank[h % 4]
            if half[0] == "v":
                for t in range(2):
                    tok = 2 * half[2] + t
                    mm = block_token(pe, bank[:, t * 256:(t + 1) * 256], lambda q: A[:, q, tok * P:(tok + 1) * P], wt, KD)
            else:
                mm = block_feature(pe, bank[:, :], wt, (half[1] % 2) * P, P, lambda q: A[:, q, :], KD)
            mm.then_inc(k.half_done, 1)

    def scalar(k, act):
        for h, half in enumerate(halves):
            act.wait_ge(k.half_done, 2 * t0 + h + 1)
            bank = k.bank[h % 4][:, :]
            if half[0] == "u":
                act.activation(U[:, half[1], :], bank, ACT.Gelu_apprx_tanh).then_inc(read, 1)
            elif half[0] == "v":
                _, c, t = half
                act.activation(V[:, 2 * t:2 * t + 2, c * 256:(c + 1) * 256], bank.rearrange("p (a b) -> p a b", a=2),
                               ACT.Gelu_apprx_tanh).then_inc(read, 1)
            else:
                act.activation(QM[:, half[1], :], bank, ACT.Copy, scale=HEAD ** -0.5).then_inc(read, 1)

    return Phase("input_projection_a", sync=sync, tensor=tensor, scalar=scalar)


def spatial_prepare(k):
    M = k.M
    V, WS, BC = view(M, A_V, 4, MAIN), view(M, A_WS, 12, P), view(M, A_BC, 3, MAIN)
    turned, st = k.sem("ws_turned"), k.sem("v_stats")
    stats, mv = view(M, O_SML, 4, 12), view(M, O_SML + 48, 4, 2)
    rooted = k.sem("v_rooted")

    def tensor(k, pe):
        pe.wait_ge(k.ws_in, 64)
        for g in range(6):
            mm = pe.transpose(k.bank[g // 4][:, (g % 4) * P:(g % 4 + 1) * P], WS[:, g, :], k.ident)
        mm.then_inc(turned, 1)

    def vector(k, dve):
        for t in range(4):
            for n in range(2):
                ins = dve.bn_stats(stats[:, t, 6 * n:6 * n + 6], V[:, t, n * 384:(n + 1) * 384])
        k.dve.link(ins)
        for t in range(4):
            ins = dve.bn_aggr(mv[:, t, :], stats[:, t, :])
        k.dve.link(ins)
        k.dve.link(dve.tensor_scalar(mv[:, :, 1:2], mv[:, :, 1:2], LN_EPS, None, ALU.add))
        dve.reciprocal(mv[:, :, 1:2], mv[:, :, 1:2]).then_inc(st, 1)
        dve.wait_ge(turned, 1)
        dve.wait_ge(k.ws_in, 64)
        for g in range(6):
            dve.tensor_tensor(WS[:, 6 + g, :], k.bank[g // 4][:, (g % 4) * P:(g % 4 + 1) * P], k.lower, ALU.mult)
        dve.wait_ge(rooted, 1)
        for t in range(4):
            k.dve.link(dve.tensor_scalar(V[:, t, :], V[:, t, :], mv[:, t, 0:1], mv[:, t, 1:2], ALU.subtract, ALU.mult))
            k.dve.link(dve.tensor_tensor(V[:, t, :], V[:, t, :], BC[:, 0, :], ALU.mult))
            dve.tensor_tensor(V[:, t, :], V[:, t, :], BC[:, 1, :], ALU.add)

    def scalar(k, act):
        act.wait_ge(st, 1)
        act.activation(mv[:, :, 1:2], mv[:, :, 1:2], ACT.Sqrt).then_inc(rooted, 1)

    return Phase("spatial_prepare", tensor=tensor, vector=vector, scalar=scalar)


def spatial_gate(k):
    M = k.M
    V, WS, BC, U, MIX = (view(M, A_V, 4, MAIN), view(M, A_WS, 12, P), view(M, A_BC, 3, MAIN), view(M, A_B, 6, S),
                         view(M, A_MIX, KD, S))
    mixed, read = k.sem("spatial_mixed"), k.sem("spatial_read")

    def tensor(k, pe):
        for g in range(6):
            if g >= 4:
                pe.wait_ge(read, g - 3)
            for c in range(4):
                mm = pe.matmul(k.bank[g % 4][:, c * P:(c + 1) * P], V[:, c, g * P:(g + 1) * P], WS[:, 6 + g, :],
                               start=True, stop=True)
            mm.then_inc(mixed, 1)

    def vector(k, dve):
        for g in range(6):
            dve.wait_ge(mixed, g + 1)
            bias = BC[:, 2:3, g * P:(g + 1) * P].broadcast_to([P, 4, P])
            ins = dve.tensor_tensor(MIX[:, g, :].rearrange("p (c t) -> p c t", c=4),
                                    k.bank[g % 4][:, :].rearrange("p (c t) -> p c t", c=4), bias, ALU.add)
            ins.then_inc(read, 1)
            dve.wait_ge(read, g + 1)
            dve.tensor_tensor(MIX[:, g, :], MIX[:, g, :], U[:, g, :], ALU.mult)

    return Phase("spatial_gate", tensor=tensor, vector=vector)


class Attention:

    def __init__(self, name, heads, keys, q, key, value, out, negc=None):
        self.name, self.heads, self.keys, self.q, self.key, self.value, self.out, self.negc = \
            name, heads, keys, q, key, value, out, negc


def attention_phase(k, s):
    M = k.M
    NJ = 4
    pt = view(M, A_PT, 2, NJ, S)
    pr = view(M, A_PR, 3, S)
    small = view(M, O_SML, 4, 2)
    scored, maxed, raised, summed_inv, ready, turned, copied, valued, taken = (
        k.sem(f"{s.name}_{x}") for x in ("scored", "maxed", "raised", "inv", "ready", "turned", "copied", "valued", "taken"))
    units = [(h, i) for h in range(s.heads) for i in range(4)]
    nk = [s.keys(i) for i in range(4)]
    rows = lambda h: slice(64 * (h % 2), 64 * (h % 2) + 64)
    last_unit = lambda h: 4 * h + 3

    def tensor(k, pe):
        for u in range(len(units) + 2):
            if u < len(units):
                h, i = units[u]
                bank = k.bank[u % 3][:, :nk[i]]
                if u >= 3:
                    pe.wait_ge(raised, u - 2)
                if s.negc is not None:
                    pe.matmul(bank, k.ident[:, h:h + 1].broadcast_to([P, P]), s.negc[:, :nk[i]], start=True, stop=False)
                    pe.matmul(bank[:, i * P:], k.ident, k.causal, start=False, stop=False)
                pe.matmul(bank, s.q(h, i), s.key(h, nk[i]), start=s.negc is None, stop=True).then_inc(scored, 1)
            if u >= 2:
                v = u - 2
                h, i = units[v]
                pe.wait_ge(ready, v + 1)
                if v >= 2:
                    pe.wait_ge(copied, v - 1)
                for j in range(nk[i] // P):
                    mm = pe.transpose(k.bank[3 + v % 2][:, j * P:(j + 1) * P], pr[:, v % 3, j * P:(j + 1) * P], k.ident)
                mm.then_inc(turned, 1)
                if i == 3 and h >= 1:
                    values(pe, h - 1)
        values(pe, s.heads - 1)

    def values(pe, h):
        pe.wait_ge(copied, last_unit(h) + 1)
        if h >= 2:
            pe.wait_ge(taken, h - 1)
        out = k.bank[5 + h % 2][rows(h), :]
        n = nk[3] // P
        for j in range(n):
            q0 = j * P if s.negc is not None else 0
            mm = pe.matmul(out[:, q0:], s.value(h, j), pt[:, h % 2, j, q0:], start=j == 0, stop=j == n - 1)
        mm.then_inc(valued, 1)

    def vector(k, dve):
        for u in range(len(units) + 1):
            if u < len(units):
                h, i = units[u]
                dve.wait_ge(scored, u + 1)
                k.dve.link(dve.tensor_reduce(small[:, u % 4, 0:1], k.bank[u % 3][:, :nk[i]], AX_X, ALU.max))
                dve.tensor_scalar(small[:, u % 4, 0:1], small[:, u % 4, 0:1], -1.0, None, ALU.mult).then_inc(maxed, 1)
            if u >= 1:
                v = u - 1
                h, i = units[v]
                dve.wait_ge(raised, v + 1)
                k.dve.link(dve.reciprocal(small[:, v % 4, 1:2], small[:, v % 4, 1:2]))
                dve.tensor_scalar(pr[:, v % 3, :nk[i]], pr[:, v % 3, :nk[i]], small[:, v % 4, 1:2], None,
                                  ALU.mult).then_inc(ready, 1)
                if i == 0 and h >= 2:
                    take(dve, h - 2)
        take(dve, s.heads - 2)
        take(dve, s.heads - 1)

    def take(dve, h):
        dve.wait_ge(valued, h + 1)
        dve.tensor_copy(s.out(h), k.bank[5 + h % 2][rows(h), :]).then_inc(taken, 1)

    def scalar(k, act):
        for u in range(len(units) + 3):
            if u < len(units):
                h, i = units[u]
                act.wait_ge(maxed, u + 1)
                if u >= 3:
                    act.wait_ge(turned, u - 2)
                act.activation(pr[:, u % 3, :nk[i]], k.bank[u % 3][:, :nk[i]], ACT.Exp, bias=small[:, u % 4, 0:1],
                               accum_out=small[:, u % 4, 1:2]).then_inc(raised, 1)
            if u >= 3:
                v = u - 3
                h, i = units[v]
                act.wait_ge(turned, v + 1)
                if h >= 2:
                    act.wait_ge(valued, h - 1)
                n = nk[i] // P
                act.activation(pt[:, h % 2, 0:n, i * P:(i + 1) * P],
                               k.bank[3 + v % 2][:, :nk[i]].rearrange("p (j q) -> p j q", q=P), ACT.Copy).then_inc(copied, 1)

    return Phase(s.name, tensor=tensor, vector=vector, scalar=scalar)


def mem_attention(k, L):
    M = k.M
    QM, KM, VM, MIX = view(M, A_QM, 2, S), view(M, A_KM, 2, NM), view(M, A_VM, 2, NM), view(M, A_MIX, KD, S)
    r = lambda h: slice(64 * (h % 2), 64 * (h % 2) + 64)
    return attention_phase(k, Attention(
        f"mem_attention{L}", 4, lambda i: NM,
        q=lambda h, i: QM[r(h), h // 2, i * P:(i + 1) * P],
        key=lambda h, n: KM[r(h), h // 2, :n],
        value=lambda h, j: VM[:, j, h * HEAD:(h + 1) * HEAD],
        out=lambda h: MIX[r(h), 6 + h // 2, :]))


def fox_attention(k):
    M = k.M
    Q, K, V, MIX = view(M, A_Q, 6, S), view(M, A_K, 6, S), view(M, A_V, 4, MAIN), view(M, A_MIX, KD, S)
    r = lambda h: slice(64 * (h % 2), 64 * (h % 2) + 64)
    return attention_phase(k, Attention(
        "fox_attention", 12, lambda i: P * (i + 1),
        q=lambda h, i: Q[r(h), h // 2, i * P:(i + 1) * P],
        key=lambda h, n: K[r(h), h // 2, :n],
        value=lambda h, j: V[:, j, h * HEAD:(h + 1) * HEAD],
        out=lambda h: MIX[r(h), h // 2, :],
        negc=view(M, A_NEGC, S)))


def input_projection_b(k):
    t0 = k.plan
    k.plan += 11
    M = k.M
    A, B = view(M, A_A, KD, S), view(M, A_B, KD, S)
    Q, K, V, QM, NEGC = view(M, A_Q, 6, S), view(M, A_K, 6, S), view(M, A_V, 4, MAIN), view(M, A_QM, 2, S), view(M, A_NEGC, S)
    wkv = k.a["w_shared_kv"].rearrange("(c p) n -> p c n", p=P)
    wb = k.a["w_in_b"][0].rearrange("(c p) n -> p c n", p=P)
    read, cleared = k.sem("in_b_read"), k.sem("in_b_cleared")
    halves = ([("k", b) for b in range(6)] + [("v", c, t) for c in range(3) for t in range(2)] + [("f", 0), ("f", 1)]
              + [("q", b) for b in range(6)] + [("m", b) for b in range(2)])

    def sync(k, sp):
        load_columns(k, wkv, 0, 1536)
        sp.dma_start(k.bf, k.a["b_forget"].rearrange("(h o) -> h o", o=1)).then_inc(k.bf_in, 16)
        load_columns(k, wkv, 1536, 1548)
        load_columns(k, wb, 0, 1024)

    def tensor(k, pe):
        for h, half in enumerate(halves):
            if h % 2 == 0:
                wt = k.pe_stream.take(KD, 12 if half[0] == "f" else 256)
            if h >= 4:
                pe.wait_ge(read, h - 3)
            bank = k.bank[h % 4]
            X = B if half[0] in "kvf" else A
            if half[0] == "v":
                for t in range(2):
                    tok = 2 * half[2] + t
                    mm = block_token(pe, bank[:, t * 256:(t + 1) * 256], lambda q: X[:, q, tok * P:(tok + 1) * P], wt, KD)
            elif half[0] == "f":
                bank = k.bank[4]
                mm = block_feature(pe, bank[0:12, :], Shift(wt, 4 * half[1]), 0, 12, lambda q: X[:, q, :], 4, 4 * half[1],
                                   start=half[1] == 0, stop=half[1] == 1)
            else:
                mm = block_feature(pe, bank[:, :], wt, (half[1] % 2) * P, P, lambda q: X[:, q, :], KD)
            mm.then_inc(k.half_done, 1)

    def scalar(k, act):
        for h, half in enumerate(halves):
            act.wait_ge(k.half_done, 2 * t0 + h + 1)
            bank = k.bank[h % 4][:, :]
            if half[0] == "v":
                _, c, t = half
                act.activation(V[:, 2 * t:2 * t + 2, c * 256:(c + 1) * 256], bank.rearrange("p (a b) -> p a b", a=2),
                               ACT.Copy).then_inc(read, 1)
            elif half[0] == "f":
                if half[1] == 0:
                    act.wait_ge(cleared, 1)
                    act.activation(k.scrap, k.scrap, ACT.Copy).then_inc(read, 1)
                else:
                    act.activation(NEGC[0:12, :], k.bank[4][0:12, :], ACT.Copy).then_inc(read, 1)
            else:
                dst = {"k": K, "q": Q, "m": QM}[half[0]][:, half[1], :]
                act.activation(dst, bank, ACT.Copy, scale=1.0 if half[0] == "k" else HEAD ** -0.5).then_inc(read, 1)

    def vector(k, dve):
        k.dve.link(dve.memset(k.scrap, 0.0))
        dve.memset(NEGC, 0.0).then_inc(cleared, 1)

    return Phase("input_projection_b", sync=sync, tensor=tensor, scalar=scalar, vector=vector)


class Shift:

    def __init__(self, w, first):
        self.w, self.first = w, first

    def __getitem__(self, key):
        a, q, c = key
        return self.w[a, q + self.first, c]


def forget_phase(k):
    M = k.M
    Z = view(M, A_NEGC, S)
    E, R = view(M, A_SCR, S), view(M, A_SCR + S, S)
    a, b = k.sem("forget_abs"), k.sem("forget_log")

    def vector(k, dve):
        dve.wait_ge(k.bf_in, 16)
        k.dve.link(dve.tensor_scalar(R[0:12, :], Z[0:12, :], k.bf, -1.0, ALU.add, ALU.mult))
        k.dve.link(dve.tensor_scalar(E[0:12, :], R[0:12, :], -1.0, None, ALU.mult))
        k.dve.link(dve.tensor_tensor(E[0:12, :], E[0:12, :], R[0:12, :], ALU.max))
        dve.tensor_scalar(R[0:12, :], R[0:12, :], 0.0, None, ALU.max).then_inc(a, 1)
        dve.wait_ge(b, 1)
        k.dve.link(dve.tensor_tensor(R[0:12, :], R[0:12, :], E[0:12, :], ALU.add))
        k.dve.link(dve.memset(E[0:12, :], 1.0))
        k.dve.link(dve.tensor_tensor_scan(Z[0:12, :], E[0:12, :], R[0:12, :], 0.0, ALU.mult, ALU.add))

    def scalar(k, act):
        act.wait_ge(a, 1)
        k.act.link(act.activation(E[0:12, :], E[0:12, :], ACT.Exp, scale=-1.0))
        act.activation(E[0:12, :], E[0:12, :], ACT.Ln, bias=1.0).then_inc(b, 1)

    return Phase("forget", vector=vector, scalar=scalar)


def output_projection(k, name, w):
    t0 = k.plan
    k.plan += 4
    MIX, Y = view(k.M, A_MIX, KD, S), view(k.M, A_Y, KD, S)
    read = k.sem(f"{name}_read")
    w = w.rearrange("(c p) n -> p c n", p=P)

    def sync(k, sp):
        load_columns(k, w, 0, D)

    def tensor(k, pe):
        for b in range(KD):
            if b % 2 == 0:
                wt = k.pe_stream.take(KD, 256)
            if b >= 4:
                pe.wait_ge(read, b - 3)
            block_feature(pe, k.bank[b % 4][:, :], wt, (b % 2) * P, P, lambda q: MIX[:, q, :], KD).then_inc(k.half_done, 1)

    def vector(k, dve):
        for b in range(KD):
            dve.wait_ge(k.half_done, 2 * t0 + b + 1)
            dve.tensor_copy(Y[:, b, :], k.bank[b % 4][:, :]).then_inc(read, 1)

    return Phase(name, sync=sync, tensor=tensor, vector=vector)


def paired_units(k, eng, chains, unit):
    trips = KF // 4
    with eng.Fori(0, trips) as i:
        for c, n in chains:
            c.enter(i, n)
        for u in range(2):
            unit(i, u)
    for c, n in chains:
        c.leave(trips)
    unit(None, 2 * trips)


def at(i, per, off):
    return off if i is None else i * per + off


def ffn_up(k, name, w1, w2, c1, c2, tmp, conv=None):
    t0 = k.plan
    k.plan += KF
    M = k.M
    A, HID, T = view(M, A_A, KD, S), view(M, A_HID, KF, S), view(M, tmp, 4, S)
    w1 = w1.rearrange("(c p) n -> p c n", p=P)
    w2 = w2.rearrange("(c p) n -> p c n", p=P)
    free, gated, centred, tapped = (k.sem(f"{name}_{x}") for x in ("banks_free", "gated", "centred", "tapped"))

    def sync(k, sp):
        def unit(i, u):
            for w, c in ((w1, c1), (w2, c2)):
                k.sp_stream.load(w[:, :, c + 256 * u:][:, :, bass.ds(at(i, 512, 0), 256)], KD, 256)
        paired_units(k, sp, [(k.sp_stream, 4)], unit)

    def tensor(k, pe):
        pe.sem_inc(free, 2)

        def unit(i, u):
            pe.wait_ge(free, at(i, 2, u + 1))
            for g in range(2):
                wt = k.pe_stream.take(KD, 256)
                for b in range(2):
                    block_feature(pe, k.bank[4 * (u % 2) + 2 * g + b][:, :], wt, b * P, P, lambda q: A[:, q, :],
                                  KD).then_inc(k.half_done, 1)
        paired_units(k, pe, [(k.pe_stream, 4)], unit)

    def scalar(k, act):
        def unit(i, u):
            for b in range(2):
                act.wait_ge(k.half_done, at(i, 8, 2 * t0 + 4 * u + b + 1))
                if b == 0:
                    act.wait_ge(free, at(i, 2, u + 1))
                act.activation(T[:, 2 * (u % 2) + b, :], k.bank[4 * (u % 2) + b][:, :], ACT.Silu).then_inc(gated, 1)
        paired_units(k, act, [], unit)

    def vector(k, dve):
        def unit(i, u):
            for b in range(2):
                dve.wait_ge(k.half_done, at(i, 8, 2 * t0 + 4 * u + 2 + b + 1))
                dve.wait_ge(gated, at(i, 4, 2 * u + b + 1))
                bank = k.bank[4 * (u % 2) + 2 + b][:, :]
                dst = HID[:, bass.ds(at(i, 4, 2 * u + b), 1), :].rearrange("p a b -> p (a b)")
                ins = dve.tensor_tensor(dst, bank, T[:, 2 * (u % 2) + b, :], ALU.mult)
            ins.then_inc(free, 1)
        paired_units(k, dve, [], unit)

    def vec(i, u, b, half, what):
        return M[:, bass.ds(at(i, 4, O_VEC + conv[half][what] + 2 * u + b), 1)]

    def conv_scalar(k, act):
        def unit(i, u):
            for half in range(2):
                for b in range(2):
                    act.wait_ge(k.half_done, at(i, 8, 2 * t0 + 4 * u + 2 * half + b + 1))
                    if half == 0 and b == 0:
                        act.wait_ge(free, at(i, 2, u + 2))
                    act.activation(T[:, 2 * half + b, :], k.bank[4 * (u % 2) + 2 * half + b][:, :], ACT.Identity,
                                   scale=vec(i, u, b, half, "tap1"), bias=vec(i, u, b, half, "bias")).then_inc(centred, 1)
            for b in range(2):
                act.wait_ge(tapped, at(i, 4, 2 * u + b + 1))
                act.activation(T[:, 2 + b, :], T[:, 2 + b, :], ACT.Silu).then_inc(gated, 1)
        paired_units(k, act, [], unit)

    def conv_vector(k, dve):
        def unit(i, u):
            for half in range(2):
                for b in range(2):
                    dve.wait_ge(centred, at(i, 8, 4 * u + 2 * half + b + 1))
                    bank, t = k.bank[4 * (u % 2) + 2 * half + b], T[:, 2 * half + b, :]
                    k.dve.link(dve.scalar_tensor_tensor(out=t[:, 1:S], in0=bank[:, 0:S - 1], scalar=vec(i, u, b, half, "tap0"),
                                                        in1=t[:, 1:S], op0=ALU.mult, op1=ALU.add))
                    ins = dve.scalar_tensor_tensor(out=t[:, 0:S - 1], in0=bank[:, 1:S], scalar=vec(i, u, b, half, "tap2"),
                                                   in1=t[:, 0:S - 1], op0=ALU.mult, op1=ALU.add)
                    if half == 1:
                        ins.then_inc(tapped, 1)
                    else:
                        k.dve.link(ins)
            for b in range(2):
                dve.wait_ge(gated, at(i, 4, 2 * u + b + 1))
                dst = HID[:, bass.ds(at(i, 4, 2 * u + b), 1), :].rearrange("p a b -> p (a b)")
                ins = dve.tensor_tensor(dst, T[:, b, :], T[:, 2 + b, :], ALU.mult)
            ins.then_inc(free, 1)
        paired_units(k, dve, [(k.dve, 12)], unit)

    return Phase(name, sync=sync, tensor=tensor, vector=conv_vector if conv else vector,
                 scalar=conv_scalar if conv else scalar)


def ffn_down(k, name, w):
    t0 = k.plan
    k.plan += 16
    HID, Y = view(k.M, A_HID, KF, S), view(k.M, A_Y, KD, S)
    w = w.rearrange("(h c p) n -> p h c n", h=2, p=P)
    free = k.sem(f"{name}_free")
    KH = KF // 2

    def sync(k, sp):
        with sp.Fori(0, KD // 2) as i:
            k.sp_stream.enter(i, 4)
            for b in range(2):
                for h in range(2):
                    k.sp_stream.load(w[:, h, :, b * P:][:, :, bass.ds(i * 256, P)], KH, P)
        k.sp_stream.leave(KD // 2)

    def tensor(k, pe):
        pe.sem_inc(free, 2)
        with pe.Fori(0, KD // 2) as i:
            k.pe_stream.enter(i, 4)
            for b in range(2):
                pe.wait_ge(free, i * 2 + (b + 1))
                for h in range(2):
                    wt = k.pe_stream.take(KH, P)
                    for q in range(KH):
                        mm = pe.matmul(k.bank[b][:, :], wt[:, q, :], HID[:, KH * h + q, :],
                                       start=h == 0 and q == 0, stop=h == 1 and q == KH - 1)
                        if q in (5, KH - 1):
                            mm.then_inc(k.half_done, 1)
        k.pe_stream.leave(KD // 2)

    def vector(k, dve):
        with dve.Fori(0, KD // 2) as i:
            for b in range(2):
                dve.wait_ge(k.half_done, i * 8 + (2 * t0 + 4 * b + 4))
                dve.tensor_copy(Y[:, bass.ds(i * 2 + b, 1), :].rearrange("p a b -> p (a b)"),
                                k.bank[b][:, :]).then_inc(free, 1)

    return Phase(name, sync=sync, tensor=tensor, vector=vector)


def first_block_phases(k, stop):
    M = k.M
    k.plan = 0
    k.ws_in, k.bf_in = k.sem("spatial_in"), k.sem("b_forget_in")
    k.bf = M[0:12, O_SML + 200:O_SML + 201]
    k.scrap = M[0:1, O_SML + 202:O_SML + 203]
    A, B, Y, MN = view(M, A_A, KD, S), view(M, A_B, KD, S), view(M, A_Y, KD, S), view(M, A_MN, KD, NM)
    g = lambda name, base: (lambda c: col(k, name, base + c))

    ph = []
    for L in range(2):
        norms = []
        if L == 0:
            norms.append(make_norm(k, "mix_norm0", k.H, S, [(g("ln_mix_pre", 0), A, None)], A_SCR))
        norms.append(make_norm(k, f"mem_norm{L}", k.memT, NM, [(g("ln_mem", 8 * L), MN, None)], A_TMP))
        ph.append(norm_phase(k, f"input_norms{L}", norms))
        ph.append(mem_projection(k, L))
        if L == 0:
            ph += [input_projection_a(k), spatial_prepare(k), spatial_gate(k)]
        else:
            ph += [input_projection_b(k), forget_phase(k), fox_attention(k)]
        ph.append(mem_attention(k, L))
        if stop == f"mix{L}":
            return ph
        ph.append(output_projection(k, f"output_projection{L}", k.a["w_out"][L]))
        post = make_norm(k, f"mix_post{L}", Y, S, [], A_SCR)
        pre = make_norm(k, f"ffn_pre{L}", k.H, S, [(g("ln_ffn_pre", 8 * L), A, None)], A_HID, after=post)
        ph.append(norm_phase(k, f"ffn_norm{L}", [pre], post=(post, g("ln_mix_post", 8 * L))))
        if stop == f"hmix{L}":
            return ph
        ph.append(ffn_up(k, f"ffn_up{L}", k.a["w_ffn_gate"][L], k.a["w_ffn_up"][L], 0, 0, A_TMP))
        ph.append(ffn_down(k, f"ffn_down{L}", k.a["w_ffn_down"][L]))
        post = make_norm(k, f"ffn_post{L}", Y, S, [], A_SCR)
        nxt = []
        if L == 0:
            nxt = [make_norm(k, "mix_norm1", k.H, S, [(g("ln_mix_pre", 8), A, None), (g("ln_shared", 0), B, None)],
                             A_HID, after=post)]
        ph.append(norm_phase(k, f"layer_norm{L}", nxt, post=(post, g("ln_ffn_post", 8 * L))))
        if stop == f"h{L}":
            return ph
    return ph


T_ALL = NC_CTX + S
TT = T_ALL // P
LAM_INIT = 0.8 - 0.6 * 1.0
LN_X_EPS = 64e-5
CH = 64
NPAIR = 8
DECAY = -float(np.exp(-0.5))

A_C = A_B
D_Q = A_Y
D_K = D_Q + 4 * S
D_V = D_K + 4 * T_ALL
D_ROPE = D_V + TT * 512
D_PT = D_ROPE + P + 2 * S
D_P = D_PT + 2 * TT * S
D_LAM = D_P + 4 * T_ALL
assert D_LAM + 256 <= WORDS
R_R = A_Y
R_K = R_R + 4 * T_ALL
R_V = R_K + 4 * T_ALL
R_KK = R_V + 4 * T_ALL
R_WA = R_KK + 4 * T_ALL
R_GL = R_WA + T_ALL
R_YB = R_GL + S
R_TMP = R_YB + 4 * S
R_ABD = A_A
R_BBD, R_KBD, R_VBD = R_ABD + 1024, R_ABD + 2048, R_ABD + 3072
R_ATK = R_ABD + 4096
R_BTK, R_KTK, R_VTK = R_ATK + 1024, R_ATK + 2048, R_ATK + 3072
assert R_VTK + 1024 <= A_MIX
R_ABAR, R_SABD, R_S0BD = R_ABD, R_BBD, R_KBD
R_AR = O_MEM
R_B, R_VST, R_QK, R_QB, R_LT, R_KV = (O_MEM + 1024 + 512 * n for n in range(6))
R_SIG = R_TMP
R_EXP = R_SIG + 1024
R_G = R_EXP + 1536
R_XY, R_YBD, R_T, R_TBD = R_TMP, R_TMP + 1024, R_TMP + 2048, R_TMP + 2560
R_KTBD = R_TMP + 3584
R_LOFF = R_KTBD + 1024
R_SA, R_S, R_S0 = R_LOFF + 1024, R_LOFF + 1536, R_LOFF + 2048
assert R_G + 1024 <= R_KTBD and R_S0 + 512 <= WORDS
R_MASK = O_RING
MASKS = {}
_off = 0
for _n, _w in (("head", 2), ("eye", CH), ("x1", 2 * CH), ("y1", 2 * CH), ("incl", 2 * CH), ("neg", 2 * CH),
               ("strict", 2 * P), ("level", 5 * 2 * P), ("reset", 512), ("headsum", P)):
    MASKS[_n] = _off
    _off += _w
N_MASK = _off
R_W2 = R_MASK + N_MASK
R_G2 = R_W2 + 1024
R_KD = R_G2 + 512
R_A2 = R_KD + 1024
R_AL = R_A2 + 1024
assert R_AL + T_ALL <= O_MEM

MOD_DERIVED = ("gx", "gc", "gf", "pm", "pf")


def adaptive_phase(k):
    t0 = k.plan
    k.plan += 24
    M = k.M
    COND = view(M, A_SCR, KD, 2)
    SIL = view(M, A_SCR + 16, KD, 2)
    MOD = view(M, O_MOD, 48, 2)
    w = k.a["w_mod_2"][0].rearrange("(c p) n -> p c n", p=P)
    ready, silu = k.sem("cond_ready"), k.sem("cond_silu")

    def sync(k, sp):
        with sp.Fori(0, 6) as i:
            k.sp_stream.enter(i, 4)
            for t in range(4):
                k.sp_stream.load(w[:, :, 256 * t:][:, :, bass.ds(i * 1024, 256)], KD, 256)
        k.sp_stream.leave(6)

    def tensor(k, pe):
        pe.wait_ge(silu, 1)
        out = k.bank[0][:, 0:96].rearrange("p (n two) -> p n two", two=2)
        with pe.Fori(0, 6) as i:
            k.pe_stream.enter(i, 4)
            for t in range(4):
                wt = k.pe_stream.take(KD, 256)
                for b in range(2):
                    dst = out[:, bass.ds(i * 8 + (2 * t + b), 1), :].rearrange("p a b -> p (a b)")
                    block_feature(pe, dst, wt, b * P, P, lambda q: SIL[:, q, :], KD).then_inc(k.half_done, 1)
        k.pe_stream.leave(6)

    def scalar(k, act):
        for n, name in enumerate(("c_2", "c_ctx_2")):
            ins = act.activation(SIL[:, :, n:n + 1], M[:, O_VEC + VCOL[name]:O_VEC + VCOL[name] + KD].rearrange(
                "p (c o) -> p c o", o=1), ACT.Silu)
        ins.then_inc(silu, 1)

    def vector(k, dve):
        dve.wait_ge(k.half_done, 2 * (t0 + 24))
        vec = lambda name, n=KD: M[:, O_VEC + VCOL[name]:O_VEC + VCOL[name] + n].rearrange("p (c o) -> p c o", o=1)
        k.dve.link(dve.tensor_tensor(MOD, k.bank[0][:, 0:96].rearrange("p (n two) -> p n two", two=2),
                                     vec("b_mod_2", 48).broadcast_to([P, 48, 2]), ALU.add))
        for name, (v, c, which, plus) in (("gx", ("g_pre_mix_2", 8, 0, 1.0)), ("gc", ("g_pre_mix_2", 8, 1, 1.0)),
                                          ("gf", ("g_pre_ffn_2", 32, 0, 1.0)), ("pm", ("g_post_mix_2", 16, 0, 0.0)),
                                          ("pf", ("g_post_ffn_2", 40, 0, 0.0))):
            o = O_MOD + 96 + 8 * MOD_DERIVED.index(name)
            dve.scalar_tensor_tensor(out=M[:, o:o + KD].rearrange("p (c o) -> p c o", o=1), in0=MOD[:, c:c + KD, which:which + 1],
                                     scalar=plus, in1=vec(v), op0=ALU.add, op1=ALU.mult)

    return Phase("adaptive", sync=sync, tensor=tensor, scalar=scalar, vector=vector)


def mod_col(k, c, which=0):
    o = O_MOD + 2 * c + which
    return k.M[:, o:o + 1]


def derived_col(k, name, c):
    o = O_MOD + 96 + 8 * MOD_DERIVED.index(name) + c
    return k.M[:, o:o + 1]


def diff_projection(k):
    t0 = k.plan
    k.plan += 6
    M = k.M
    A, C = view(M, A_A, KD, S), view(M, A_C, KD, NC_CTX)
    Q, K, V = view(M, D_Q, 4, S), view(M, D_K, 4, T_ALL), view(M, D_V, TT, 512)
    w = k.a["w_in_2"][0].rearrange("(c p) n -> p c n", p=P)
    read = k.sem("diff_read")
    halves = [("q", b) for b in range(4)] + [("k", b) for b in range(4)] + [("v", c, t) for c in range(2) for t in range(2)]
    tok = lambda t: (lambda q: C[:, q, t * P:(t + 1) * P]) if t < 2 else (lambda q: A[:, q, (t - 2) * P:(t - 1) * P])

    def sync(k, sp):
        load_columns(k, w, 1696, 3232)
        for s in k.phase_end.values():
            sp.wait_ge(s, k.phase_index["second_norms"] + 1)
        sp.dma_start(M[:, D_ROPE:D_ROPE + P + 2 * S], k.a["const_rope"]).then_inc(k.rope_in, 16)
        for n, name in enumerate(("lam_q1_2", "lam_k1_2", "lam_q2_2", "lam_k2_2")):
            sp.dma_start(view(M, D_LAM, 4, HEAD)[:, n, :], k.a[name].broadcast_to([P, HEAD])).then_inc(k.rope_in, 16)

    def tensor(k, pe):
        for h, half in enumerate(halves):
            if h % 2 == 0:
                wt = k.pe_stream.take(KD, 256)
            if h >= 4:
                pe.wait_ge(read, h - 3)
            two = [k.bank[2 * (h % 4)], k.bank[2 * (h % 4) + 1]]
            if half[0] == "v":
                for n in range(3):
                    dst = two[n // 2][:, (n % 2) * 256:(n % 2 + 1) * 256]
                    mm = block_token(pe, dst, tok(3 * half[2] + n), wt, KD)
            else:
                c0 = (half[1] % 2) * P
                if half[0] == "k":
                    block_feature(pe, two[1][:, :NC_CTX], wt, c0, P, lambda q: C[:, q, :], KD)
                mm = block_feature(pe, two[0], wt, c0, P, lambda q: A[:, q, :], KD)
            mm.then_inc(k.half_done, 1)

    def vector(k, dve):
        for h, half in enumerate(halves):
            dve.wait_ge(k.half_done, 2 * t0 + h + 1)
            o = 1024 * (h % 4)
            if half[0] == "q":
                ins = dve.tensor_scalar(Q[:, half[1], :], k.psum[:, o:o + S], HEAD ** -0.5, None, ALU.mult)
            elif half[0] == "k":
                dve.tensor_copy(K[:, half[1], NC_CTX:], k.psum[:, o:o + S])
                ins = dve.tensor_copy(K[:, half[1], :NC_CTX], k.psum[:, o + S:o + S + NC_CTX])
            else:
                _, c, t = half
                ins = dve.tensor_copy(V[:, 3 * t:3 * t + 3, c * 256:(c + 1) * 256],
                                      k.psum[:, o:o + 768].rearrange("p (a b) -> p a b", a=3))
            ins.then_inc(read, 1)

    return Phase("diff_projection", sync=sync, tensor=tensor, vector=vector)


def rope_phase(k):
    M = k.M
    Q, K = view(M, D_Q, 4, S), view(M, D_K, 4, T_ALL)
    rot, cos, sin = M[:, D_ROPE:D_ROPE + P], M[:, D_ROPE + P:D_ROPE + P + S], M[:, D_ROPE + P + S:D_ROPE + P + 2 * S]
    T = view(M, D_PT, 8, S)
    L = view(M, D_LAM, 4, HEAD)
    prod = view(M, D_P, 2, HEAD)
    lam = view(M, O_SML + 100, 4)
    turned, dots, exps = k.sem("rotated"), k.sem("lam_dots"), k.sem("lam_exps")
    blocks = [Q[:, n, :] for n in range(4)] + [K[:, n, NC_CTX:] for n in range(4)]
    k.lam = lam[:, 3:4]

    def tensor(k, pe):
        pe.wait_ge(k.rope_in, 16 * 5)
        for n, x in enumerate(blocks):
            pe.matmul(k.bank[n], rot, x, start=True, stop=True).then_inc(turned, 1)

    def vector(k, dve):
        dve.wait_ge(k.rope_in, 16 * 5)
        for n in range(2):
            k.dve.link(dve.tensor_tensor(prod[:, n, :], L[:, 2 * n, :], L[:, 2 * n + 1, :], ALU.mult))
        dve.tensor_reduce(lam[:, 0:2], prod, AX_X, ALU.add).then_inc(dots, 1)
        for n, x in enumerate(blocks):
            dve.wait_ge(turned, n + 1)
            k.dve.link(dve.tensor_tensor(T[:, n, :], k.bank[n], sin, ALU.mult))
            k.dve.link(dve.tensor_tensor(x, x, cos, ALU.mult))
            dve.tensor_tensor(x, x, T[:, n, :], ALU.add)
        dve.wait_ge(exps, 1)
        k.dve.link(dve.tensor_tensor(lam[:, 2:3], lam[:, 0:1], lam[:, 1:2], ALU.subtract))
        dve.tensor_scalar(lam[:, 3:4], lam[:, 2:3], LAM_INIT, None, ALU.add)

    def scalar(k, act):
        act.wait_ge(dots, 1)
        act.activation(lam[:, 0:2], lam[:, 0:2], ACT.Exp).then_inc(exps, 1)

    return Phase("rope", tensor=tensor, vector=vector, scalar=scalar)


def diff_attention(k):
    M = k.M
    Q, K, V = view(M, D_Q, 4, S), view(M, D_K, 4, T_ALL), view(M, D_V, TT, 512)
    MIX = view(M, A_MIX, KD, S)
    PT, PR = view(M, D_PT, 2, TT, S), view(M, D_P, 2, 2, T_ALL)
    small = view(M, O_SML, 2, 2, 2)
    units = [(h, i) for h in range(4) for i in range(4)]
    scored, maxed, raised, ready, turned, copied, valued, taken = (
        k.sem(f"diff_{x}") for x in ("scored", "maxed", "raised", "ready", "turned", "copied", "valued", "taken"))
    score = lambda m: k.psum[:, 1024 * m:1024 * m + T_ALL]
    TURN = 4

    def values(pe, h):
        pe.wait_ge(copied, 4 * h + 4)
        if h >= 2:
            pe.wait_ge(taken, h - 1)
        for j in range(TT):
            mm = pe.matmul(k.bank[6 + h % 2], V[:, j, h * P:(h + 1) * P], PT[:, h % 2, j, :], start=j == 0, stop=j == TT - 1)
        mm.then_inc(valued, 1)

    def tensor(k, pe):
        for u in range(len(units) + 1):
            if u < len(units):
                h, i = units[u]
                for m in range(2):
                    if u >= 1:
                        pe.wait_ge(raised, 2 * u - 1 + m)
                    r = slice(64 * m, 64 * m + 64)
                    pe.matmul(k.bank[2 * m], Q[r, h, i * P:(i + 1) * P], K[r, h, 0:512], start=True, stop=True)
                    pe.matmul(k.bank[2 * m + 1][:, :256], Q[r, h, i * P:(i + 1) * P], K[r, h, 512:768], start=True,
                              stop=True).then_inc(scored, 1)
            if u >= 1:
                v = u - 1
                h, i = units[v]
                pe.wait_ge(ready, v + 1)
                if v >= 1:
                    pe.wait_ge(copied, v)
                for j in range(TT):
                    mm = pe.transpose(k.bank[TURN + j // 4][:, (j % 4) * P:(j % 4 + 1) * P],
                                      PR[:, v % 2, 0, j * P:(j + 1) * P], k.ident)
                mm.then_inc(turned, 1)
                if i == 1 and h >= 1:
                    values(pe, h - 1)
        values(pe, 3)

    def vector(k, dve):
        for u in range(len(units) + 1):
            if u < len(units):
                for m in range(2):
                    dve.wait_ge(scored, 2 * u + m + 1)
                    k.dve.link(dve.tensor_reduce(small[:, u % 2, m, 0:1], score(m), AX_X, ALU.max))
                    dve.tensor_scalar(small[:, u % 2, m, 0:1], small[:, u % 2, m, 0:1], -1.0, None, ALU.mult).then_inc(maxed, 1)
            if u >= 1:
                v = u - 1
                h, i = units[v]
                sm, pr = small[:, v % 2], PR[:, v % 2]
                dve.wait_ge(raised, 2 * v + 2)
                k.dve.link(dve.reciprocal(sm[:, :, 1:2], sm[:, :, 1:2]))
                k.dve.link(dve.tensor_tensor(sm[:, 1, 1:2], sm[:, 1, 1:2], k.lam, ALU.mult))
                k.dve.link(dve.tensor_scalar(pr[:, 1, :], pr[:, 1, :], sm[:, 1, 1:2], None, ALU.mult))
                dve.scalar_tensor_tensor(out=pr[:, 0, :], in0=pr[:, 0, :], scalar=sm[:, 0, 1:2], in1=pr[:, 1, :],
                                         op0=ALU.mult, op1=ALU.subtract).then_inc(ready, 1)
                if i == 3 and h >= 1:
                    take(dve, h - 1)
        take(dve, 3)

    def take(dve, h):
        dve.wait_ge(valued, h + 1)
        dve.tensor_copy(MIX[:, 4 + h, :], k.bank[6 + h % 2]).then_inc(taken, 1)

    def scalar(k, act):
        for u in range(len(units) + 2):
            if u < len(units):
                if u >= 2:
                    act.wait_ge(turned, u - 1)
                for m in range(2):
                    act.wait_ge(maxed, 2 * u + m + 1)
                    act.activation(PR[:, u % 2, m, :], score(m), ACT.Exp, bias=small[:, u % 2, m, 0:1],
                                   accum_out=small[:, u % 2, m, 1:2]).then_inc(raised, 1)
            if u >= 1 and u - 1 < len(units):
                v = u - 1
                h, i = units[v]
                act.wait_ge(turned, v + 1)
                if h >= 2:
                    act.wait_ge(valued, h - 1)
                act.activation(PT[:, h % 2, :, i * P:(i + 1) * P],
                               k.psum[:, 512 * TURN:512 * TURN + T_ALL].rearrange("p (j q) -> p j q", q=P),
                               ACT.Copy).then_inc(copied, 1)

    return Phase("diff_attention", tensor=tensor, vector=vector, scalar=scalar)


def diff_post(k):
    M = k.M
    O = view(M, A_MIX, KD, S)[:, 4:8, :]
    SQ = view(M, D_PT, 4, S)
    squared, summed, inv, rooted = (k.sem(f"diffpost_{x}") for x in ("squared", "summed", "inverted", "rooted"))
    g = M[:, O_SML + 110:O_SML + 111]

    def scalar(k, act):
        act.activation(SQ, O, ACT.Square).then_inc(squared, 1)
        act.wait_ge(inv, 1)
        act.activation(SQ, SQ, ACT.Sqrt).then_inc(rooted, 1)

    def tensor(k, pe):
        pe.wait_ge(squared, 1)
        for n in range(4):
            mm = pe.matmul(k.bank[n], k.ones, SQ[:, n, :], start=True, stop=True)
        mm.then_inc(summed, 1)

    def vector(k, dve):
        dve.tensor_scalar(g, col(k, "subln_w_2"), 1.0 - LAM_INIT, None, ALU.mult)
        dve.wait_ge(summed, 1)
        k.dve.link(dve.tensor_scalar(SQ, k.psum[:, 0:4 * S].rearrange("p (a b) -> p a b", a=4), 1.0 / P, SUBLN_EPS,
                                     ALU.mult, ALU.add))
        dve.reciprocal(SQ, SQ).then_inc(inv, 1)
        dve.wait_ge(rooted, 1)
        dve.scalar_tensor_tensor(out=O, in0=O, scalar=g, in1=SQ, op0=ALU.mult, op1=ALU.mult)

    return Phase("diff_post", tensor=tensor, vector=vector, scalar=scalar)


def rwkv_projection(k):
    t0 = k.plan
    k.plan += 7
    M = k.M
    A, C = view(M, A_A, KD, S), view(M, A_C, KD, NC_CTX)
    RKV = view(M, R_R, 12, T_ALL)
    WA, GL = view(M, R_WA, T_ALL), view(M, R_GL, S)
    w = k.a["w_in_2"][0].rearrange("(c p) n -> p c n", p=P)
    free, centred = k.sem("rwkv_bank_free"), k.sem("rwkv_centred")

    def part(h):
        if h < 12:
            return RKV[:, h, :], [col(k, f"rwkv_tap{t}", h) for t in range(3)], P, (h % 2) * P
        name, m, c0, dst = (("rwkv_wa_taps", 64, 0, WA), ("rwkv_g_taps", 96, 64, GL))[h - 12]
        return dst[0:m, :], [col(k, name, t)[0:m, :] for t in range(3)], m, c0

    def segments(h):
        o = 1024 * (h % 4)
        return [(o, 0, S)] if h == 13 else [(o, NC_CTX, S), (o + S, 0, NC_CTX)]

    def sync(k, sp):
        load_columns(k, w, 0, 1536)
        load_columns(k, w, 1536, 1696)

    def tensor(k, pe):
        for h in range(14):
            if h % 2 == 0:
                wt = k.pe_stream.take(KD, 256 if h < 12 else 160)
            if h >= 4:
                pe.wait_ge(free, h - 3)
            _, _, m, c0 = part(h)
            two = [k.bank[2 * (h % 4)], k.bank[2 * (h % 4) + 1]]
            if h != 13:
                block_feature(pe, two[1][0:m, :NC_CTX], wt, c0, m, lambda q: C[:, q, :], KD)
            block_feature(pe, two[0][0:m, :], wt, c0, m, lambda q: A[:, q, :], KD).then_inc(k.half_done, 1)

    def scalar(k, act):
        for h in range(14):
            act.wait_ge(k.half_done, 2 * t0 + h + 1)
            dst, taps, m, _ = part(h)
            for o, d0, n in segments(h):
                ins = act.activation(dst[:, d0:d0 + n], k.psum[0:m, o:o + n], ACT.Copy, scale=taps[1])
            ins.then_inc(centred, 1)

    def vector(k, dve):
        for h in range(14):
            dve.wait_ge(centred, h + 1)
            dst, taps, m, _ = part(h)
            for n, (o, d0, cnt) in enumerate(segments(h)):
                x, y = k.psum[0:m, o:o + cnt], dst[:, d0:d0 + cnt]
                k.dve.link(dve.scalar_tensor_tensor(out=y[:, 1:cnt], in0=x[:, 0:cnt - 1], scalar=taps[0], in1=y[:, 1:cnt],
                                                    op0=ALU.mult, op1=ALU.add))
                ins = dve.scalar_tensor_tensor(out=y[:, 0:cnt - 1], in0=x[:, 1:cnt], scalar=taps[2], in1=y[:, 0:cnt - 1],
                                               op0=ALU.mult, op1=ALU.add)
            ins.then_inc(free, 1)

    return Phase("rwkv_projection", sync=sync, tensor=tensor, vector=vector, scalar=scalar)


def mask(k, name, off=0, n=None):
    o = R_MASK + MASKS[name] + off
    return k.M[:, o:o + n]


def rwkv_prepare(k):
    M = k.M
    K, KK = view(M, R_K, 4, T_ALL), view(M, R_KK, 4, T_ALL)
    WA = view(M, R_WA, T_ALL)
    SQ = view(M, R_ABD, 2, T_ALL)
    N = view(M, R_ABD + 2 * T_ALL, 2, T_ALL)
    scaled, squared, summed, rooted, floored = (k.sem(f"kk_{x}") for x in ("scaled", "squared", "summed", "rooted", "done"))

    def sync(k, sp):
        for s in k.phase_end.values():
            sp.wait_ge(s, k.phase_index["rwkv_projection"] + 1)
        sp.dma_start(M[:, R_MASK:R_MASK + N_MASK], k.a["const_rwkv"]).then_inc(k.rwkv_in, 16)
        for d, s in enumerate(("fwd", "bwd")):
            sp.dma_start(view(M, R_W2, 2, 512)[0:32, d, :], k.a[f"w2_{s}_2"][0]).then_inc(k.rwkv_in, 16)
            sp.dma_start(view(M, R_A2, 2, 512)[0:32, d, :], k.a[f"a2_{s}_2"][0]).then_inc(k.rwkv_in, 16)
        sp.dma_start(M[0:96, R_G2:R_G2 + 512], k.a["g2_2"][0]).then_inc(k.rwkv_in, 16)

    def scalar(k, act):
        for f in range(4):
            act.wait_ge(scaled, f + 1)
            if f >= 2:
                act.wait_ge(summed, f - 1)
            act.activation(SQ[:, f % 2, :], KK[:, f, :], ACT.Square).then_inc(squared, 1)
            if f >= 1:
                root(act, f - 1)
        root(act, 3)
        act.activation(WA[0:32, :], WA[0:32, :], ACT.Tanh)

    def root(act, f):
        act.wait_ge(summed, f + 1)
        if f >= 2:
            act.wait_ge(floored, f - 1)
        act.activation(N[:, f % 2, :], k.psum[:, 1024 * (f % 2):1024 * (f % 2) + T_ALL], ACT.Sqrt).then_inc(rooted, 1)

    def tensor(k, pe):
        pe.wait_ge(k.rwkv_in, 16 * 6)
        for f in range(4):
            pe.wait_ge(squared, f + 1)
            if f >= 2:
                pe.wait_ge(rooted, f - 1)
            b = k.bank[2 * (f % 2):2 * (f % 2) + 2]
            pe.matmul(b[0], mask(k, "headsum", 0, P), SQ[:, f % 2, 0:512], start=True, stop=True)
            pe.matmul(b[1][:, :256], mask(k, "headsum", 0, P), SQ[:, f % 2, 512:768], start=True, stop=True).then_inc(summed, 1)

    def vector(k, dve):
        dve.tensor_copy(M[0:32, R_AL:R_AL + T_ALL], WA[32:64, :])
        for f in range(4):
            dve.tensor_scalar(KK[:, f, :], K[:, f, :], col(k, "k_k_2", f), None, ALU.mult).then_inc(scaled, 1)
        for f in range(4):
            dve.wait_ge(rooted, f + 1)
            n = N[:, f % 2, :]
            k.dve.link(dve.tensor_scalar(n, n, 1e-12, None, ALU.max))
            k.dve.link(dve.reciprocal(n, n))
            dve.tensor_tensor(KK[:, f, :], KK[:, f, :], n, ALU.mult).then_inc(floored, 1)

    return Phase("rwkv_prepare", sync=sync, tensor=tensor, vector=vector, scalar=scalar)


LEVELS = 5
MAIN_ONLY = ("ydone", "yout", "s0bd", "sabd")


def rwkv_loop(k):
    M = k.M
    v4 = lambda o, *d: view(M, o, *d)
    half = lambda ap, d: ap[:, 4 * d:4 * d + 4]
    src = {n: v4(o, 4, T_ALL) for n, o in (("R", R_R), ("K", R_K), ("V", R_V), ("KK", R_KK))}
    latent, factor = (v4(R_WA, T_ALL), v4(R_AL, T_ALL)), (v4(R_W2, 2, 512), v4(R_A2, 2, 512))
    SIG, EXP, G = v4(R_SIG, 2, NPAIR, CH), v4(R_EXP, 3, NPAIR, CH), v4(R_G, 2, NPAIR, CH)
    KD_, KKA = v4(R_KD, NPAIR, CH), v4(R_KD + 512, NPAIR, CH)
    TH = v4(O_SML + 120, NPAIR)
    PH = v4(O_SML + 128, NPAIR)
    AR, B_ = v4(R_AR, NPAIR, 2, CH), v4(R_B, NPAIR, CH)
    ABD, BBD, KBD, VBD = (v4(o, NPAIR, 2, CH) for o in (R_ABD, R_BBD, R_KBD, R_VBD))
    ATK, BTK, KTK, VTK = (v4(o, NPAIR, P) for o in (R_ATK, R_BTK, R_KTK, R_VTK))
    VST, QK, QB, LT, KV = (v4(o, NPAIR, CH) for o in (R_VST, R_QK, R_QB, R_LT, R_KV))
    XY, YBD, T_, TBD = v4(R_XY, NPAIR, 2, CH), v4(R_YBD, NPAIR, 2, CH), v4(R_T, NPAIR, CH), v4(R_TBD, NPAIR, 2, CH)
    KTBD, LOFF = v4(R_KTBD, NPAIR, 2, CH), v4(R_LOFF, NPAIR, 2, CH)
    ABAR, SABD, S0BD = (v4(o, NPAIR, 2, CH) for o in (R_ABAR, R_SABD, R_S0BD))
    SA, ST, S0 = v4(R_SA, NPAIR, CH), v4(R_S, NPAIR, CH), v4(R_S0, NPAIR, CH)
    YF, YB = v4(A_MIX, KD, S), v4(R_YB, 4, S)
    flat = lambda ap: ap.rearrange("p a b -> p (a b)")
    bd = lambda ap, p: ap[:, p].rearrange("p a b -> p (a b)")
    wide = lambda ap: ap.unsqueeze(2)
    m3 = lambda name, d, w: k.M[:, R_MASK + MASKS[name] + d * w:R_MASK + MASKS[name] + (d + 1) * w]
    sems = {n: k.sem(f"rwkv_{n}") for n in (
        "latents", "shifted", "sigmoid", "summed", "exps", "bd_ab", "bd_kv", "grams", "gram2", "lt", "xy0", "ybd",
        "kq", "turned", "tcopied", "vst", "loff", "tdone", "tst", "tbd", "xydone", "xy", "kvdone", "kvst", "abar",
        "abarbd", "s0bd", "sadone", "sast", "sabd", "sdone", "s", "ydone", "yout")}

    def body(i, first, main):
        def wait(eng, name, per=1, nth=1):
            eng.wait_ge(sems[name], at(i, per, per * (first if name not in MAIN_ONLY else 0) + nth))

        def prior(eng, name):
            eng.wait_ge(sems[name], at(i, 1, (first if name not in MAIN_ONLY else 0) + 1))

        def tokens(d):
            if not main:
                return bass.ds(i * CH if d == 0 else i * -CH + (NC_CTX - CH), CH)
            return bass.ds(i * CH + NC_CTX if d == 0 else i * -CH + (T_ALL - CH), CH)

        def out_tokens(d):
            return bass.ds(i * CH if d == 0 else i * -CH + (S - CH), CH)

        return wait, prior, tokens, out_tokens

    def tensor(k, pe):
        for trips, first, main in ((4, 0, False), (8, 4, True)):
            with pe.Fori(0, trips) as i:
                wait, prior, tokens, out_tokens = body(i, first, main)
                n_ar = 2 if main else 1
                prior(pe, "s")
                for which in range(2):
                    for d in range(2):
                        for f in range(4):
                            mm = pe.matmul(k.bank[which][:, (4 * d + f) * CH:(4 * d + f + 1) * CH],
                                           factor[which][0:32, d, f * P:(f + 1) * P], latent[which][0:32, tokens(d)], start=True, stop=True)
                mm.then_inc(sems["latents"], 1)
                wait(pe, "bd_ab")
                for p in range(NPAIR):
                    pe.matmul(k.bank[2 + p // 4][:, (p % 4) * P:(p % 4) * P + n_ar * CH], bd(BBD, p),
                              AR[:, p, 0:n_ar, :].rearrange("p a b -> p (a b)"), start=True, stop=True)
                for p in range(NPAIR):
                    mm = pe.matmul(k.bank[6][:, p * CH:(p + 1) * CH], bd(ABD, p), B_[:, p, :], start=True, stop=True)
                mm.then_inc(sems["grams"], 1)
                wait(pe, "bd_kv")
                if main:
                    prior(pe, "yout")
                for p in range(NPAIR):
                    mm = pe.matmul(k.bank[4 + p // 4][:, (p % 4) * P:(p % 4) * P + n_ar * CH], bd(KBD, p),
                                   AR[:, p, 0:n_ar, :].rearrange("p a b -> p (a b)"), start=True, stop=True)
                mm.then_inc(sems["gram2"], 1)

                def turn(n, what):
                    if n > 0:
                        wait(pe, "tcopied", 4, n)
                    for p in range(NPAIR):
                        mm = pe.transpose(k.bank[p // 4][:, (p % 4) * P:(p % 4 + 1) * P], bd(what, p), k.ident)
                    mm.then_inc(sems["turned"], 1)

                turn(0, VBD)
                for lv in range(LEVELS):
                    for d in range(2):
                        if lv == 0:
                            if d == 0:
                                wait(pe, "lt")
                                wait(pe, "xy0")
                        wait(pe, "loff", 2 * LEVELS, 2 * lv + d + 1)
                        if lv > 0:
                            wait(pe, "xy", 2 * (LEVELS + 0), 2 * (lv - 1) + d + 1)
                        for p in range(4 * d, 4 * d + 4):
                            mm = pe.matmul(k.bank[2 + d][:, (p % 4) * CH:(p % 4 + 1) * CH], bd(LOFF, p), XY[:, p, 0, :],
                                           start=True, stop=True)
                        mm.then_inc(sems["tdone"], 1)
                    if lv < 3:
                        turn(lv + 1, (ABD, BBD, KBD)[lv])
                    if lv == 3:
                        wait(pe, "kq")
                        wait(pe, "vst")
                        for p in range(NPAIR):
                            mm = pe.matmul(k.bank[4][:, p * CH:(p + 1) * CH], bd(KTBD, p), VST[:, p, :], start=True, stop=True)
                        mm.then_inc(sems["kvdone"], 1)
                    for d in range(2):
                        wait(pe, "tst", 2 * LEVELS, 2 * lv + d + 1)
                        wait(pe, "tbd", 2 * LEVELS, 2 * lv + d + 1)
                        wait(pe, "ybd", 2 * (LEVELS + 1), 2 * lv + d + 1)
                        for p in range(4 * d, 4 * d + 4):
                            o = (p % 4) * P
                            pe.matmul(k.bank[6 + d][:, o:o + CH], bd(YBD, p), T_[:, p, :], start=True, stop=True)
                            mm = pe.matmul(k.bank[6 + d][:, o + CH:o + P], bd(TBD, p), XY[:, p, 1, :], start=True, stop=True)
                        mm.then_inc(sems["xydone"], 1)
                wait(pe, "tcopied", 4, 4)
                wait(pe, "xy", 2 * LEVELS, 2 * LEVELS)
                for p in range(NPAIR):
                    mm = pe.matmul(k.bank[5][:, p * CH:(p + 1) * CH], ATK[:, p, :], XY[:, p, 1, :], start=True, stop=True)
                mm.then_inc(sems["abar"], 1)
                wait(pe, "abarbd")
                wait(pe, "ybd", 2 * (LEVELS + 1), 2 * (LEVELS + 1))
                wait(pe, "kvst")
                for p in range(NPAIR):
                    pe.matmul(k.bank[0][:, p * CH:(p + 1) * CH], bd(YBD, p), KV[:, p, :], start=True, stop=False)
                    mm = pe.matmul(k.bank[0][:, p * CH:(p + 1) * CH], bd(ABAR, p), S0[:, p, :], start=False, stop=True)
                mm.then_inc(sems["sadone"], 1)
                wait(pe, "sast")
                for p in range(NPAIR):
                    pe.matmul(k.bank[1][:, p * CH:(p + 1) * CH], KTK[:, p, :], VST[:, p, :], start=True, stop=False)
                    mm = pe.matmul(k.bank[1][:, p * CH:(p + 1) * CH], BTK[:, p, :], SA[:, p, :], start=False, stop=True)
                mm.then_inc(sems["sdone"], 1)
                if main:
                    wait(pe, "s0bd")
                    wait(pe, "sabd")
                    for p in range(NPAIR):
                        o = k.bank[4][:, p * CH:(p + 1) * CH]
                        pe.matmul(o, bd(S0BD, p), AR[:, p, 1, :], start=True, stop=False)
                        pe.matmul(o, VTK[:, p, :], QK[:, p, :], start=False, stop=False)
                        mm = pe.matmul(o, bd(SABD, p), QB[:, p, :], start=False, stop=True)
                    mm.then_inc(sems["ydone"], 1)

    def scalar(k, act):
        act.sem_inc(sems["yout"], 1)
        for trips, first, main in ((4, 0, False), (8, 4, True)):
            with act.Fori(0, trips) as i:
                wait, prior, tokens, out_tokens = body(i, first, main)
                wait(act, "shifted")
                act.activation(SIG, SIG, ACT.Sigmoid).then_inc(sems["sigmoid"], 1)
                wait(act, "summed")
                for n, (fwd, bwd) in enumerate((((1, 1), (0, -1)), ((0, -1), (1, 1)), ((0, 1), (1, -1)))):
                    if n == 2 and not main:
                        continue
                    for d, (g, sign) in enumerate((fwd, bwd)):
                        act.activation(half(EXP[:, n], d), half(G[:, g], d), ACT.Exp, scale=sign * DECAY)
                act.activation(PH, TH, ACT.Exp, scale=DECAY).then_inc(sems["exps"], 1)

                def ybd(d):
                    for h in range(2):
                        ins = act.activation(half(YBD, d)[:, :, h, :], half(XY, d)[:, :, 1, :], ACT.Copy,
                                             scale=m3("head", 0, 2)[:, h:h + 1])
                    ins.then_inc(sems["ybd"], 1)

                def copied(n, dst, scale):
                    wait(act, "turned", 4, n + 1)
                    ins = act.activation(dst.rearrange("p a b -> p (a b)"), k.psum[:, 0:1024], ACT.Copy, scale=scale)
                    ins.then_inc(sems["tcopied"], 1)

                wait(act, "xy0")
                for d in range(2):
                    ybd(d)
                copied(0, VTK, 1.0)
                for lv in range(LEVELS):
                    for d in range(2):
                        wait(act, "tdone", 2 * LEVELS, 2 * lv + d + 1)
                        act.activation(half(T_, d), k.bank[2 + d][:, 0:4 * CH].rearrange("p (a b) -> p a b", a=4),
                                       ACT.Copy).then_inc(sems["tst"], 1)
                    if lv < 3:
                        copied(lv + 1, (ATK, BTK, KTK)[lv], -1.0 if lv == 1 else 1.0)
                    if lv == 3:
                        wait(act, "kvdone")
                        act.activation(KV, k.bank[4][:, :].rearrange("p (a b) -> p a b", a=NPAIR), ACT.Copy).then_inc(sems["kvst"], 1)
                    for d in range(2):
                        wait(act, "xy", 2 * LEVELS, 2 * lv + d + 1)
                        ybd(d)
                wait(act, "sadone")
                act.activation(SA, k.bank[0][:, :].rearrange("p (a b) -> p a b", a=NPAIR), ACT.Copy).then_inc(sems["sast"], 1)
                if main:
                    wait(act, "ydone")
                    for d, Y in enumerate((YF, YB)):
                        ins = act.activation(Y[:, 0:4, out_tokens(d)],
                                             k.bank[4][:, 256 * d:256 * d + 256].rearrange("p (a b) -> p a b", a=4), ACT.Copy)
                    ins.then_inc(sems["yout"], 1)

    def vector(k, dve):
        dve.memset(ST, 0.0).then_inc(sems["s"], 1)
        dve.wait_ge(sems["s"], 1)
        for trips, first, main in ((4, 0, False), (8, 4, True)):
            with dve.Fori(0, trips) as i:
                k.dve.enter(i, 10)
                wait, prior, tokens, out_tokens = body(i, first, main)
                offs = M[:, O_VEC + VCOL["w0_fwd_2"]:O_VEC + VCOL["w0_fwd_2"] + 16].rearrange("p (d w f o) -> p w d f o", d=2, w=2, o=1)
                wait(dve, "latents")
                for w in range(2):
                    for d in range(2):
                        ins = dve.tensor_tensor(half(SIG[:, w], d), k.bank[w][:, 256 * d:256 * d + 256].rearrange("p (a b) -> p a b", a=4),
                                                offs[:, w, d].broadcast_to([P, 4, CH]), ALU.add)
                ins.then_inc(sems["shifted"], 1)
                wait(dve, "sigmoid")
                pre, x = G[:, 0], SIG[:, 0]
                k.dve.link(dve.tensor_tensor_scan(flat(pre), mask(k, "reset", 0, 512), flat(x), 0.0, ALU.mult, ALU.add))
                k.dve.link(dve.tensor_scalar(TH.unsqueeze(2), pre[:, :, CH - 1:CH], 0.5, None, ALU.mult))
                k.dve.link(dve.tensor_tensor(pre, pre, TH.unsqueeze(2).broadcast_to([P, NPAIR, CH]), ALU.subtract))
                dve.tensor_tensor(G[:, 1], pre, x, ALU.subtract).then_inc(sems["summed"], 1)
                ka = M[:, O_VEC + VCOL["k_a_2"]:O_VEC + VCOL["k_a_2"] + 4].unsqueeze(2).broadcast_to([P, 4, CH])
                for d in range(2):
                    dve.tensor_tensor(half(KKA, d), src["KK"][:, :, tokens(d)], half(SIG[:, 1], d), ALU.mult)
                    ins = dve.scalar_tensor_tensor(out=half(KD_, d), in0=half(SIG[:, 1], d), scalar=-1.0, in1=ka, op0=ALU.add, op1=ALU.mult)
                k.dve.link(ins)
                for d in range(2):
                    ins = dve.scalar_tensor_tensor(out=half(KD_, d), in0=half(KD_, d), scalar=1.0, in1=src["K"][:, :, tokens(d)],
                                                   op0=ALU.add, op1=ALU.mult)
                k.dve.link(ins)
                wait(dve, "exps")
                for d in range(2):
                    ins = dve.tensor_tensor(half(AR, d)[:, :, 0, :], src["KK"][:, :, tokens(d)], half(EXP[:, 0], d), ALU.mult)
                    if main:
                        dve.tensor_tensor(half(AR, d)[:, :, 1, :], src["R"][:, :, tokens(d)], half(EXP[:, 2], d), ALU.mult)
                k.dve.link(dve.tensor_tensor(B_, KKA, EXP[:, 1], ALU.mult))
                head = m3("head", 0, 2).unsqueeze(1).unsqueeze(3)
                full = [P, NPAIR, 2, CH]
                dve.tensor_tensor(ABD, AR[:, :, 0:1, :].broadcast_to(full), head.broadcast_to(full), ALU.mult)
                dve.tensor_tensor(BBD, wide(B_).broadcast_to(full), head.broadcast_to(full), ALU.mult).then_inc(sems["bd_ab"], 1)
                k.dve.link(dve.tensor_tensor(KD_, KD_, EXP[:, 1], ALU.mult))
                dve.tensor_tensor(KBD, wide(KD_).broadcast_to(full), head.broadcast_to(full), ALU.mult)
                hfull = [P, 4, 2, CH]
                for d in range(2):
                    ins = dve.tensor_tensor(half(VBD, d), wide(src["V"][:, :, tokens(d)]).broadcast_to(hfull), head.broadcast_to(hfull), ALU.mult)
                ins.then_inc(sems["bd_kv"], 1)
                half_total = PH.unsqueeze(2).broadcast_to([P, NPAIR, CH])
                k.dve.link(dve.tensor_tensor(S0, ST, half_total, ALU.mult))
                wait(dve, "grams")
                gram = lambda b, w: k.psum[:, 512 * b:512 * b + 512].rearrange("p (a w t) -> p a w t", a=4, w=2)[:, :, w, :]
                row = lambda name, d: m3(name, d, CH).unsqueeze(1).broadcast_to([P, 4, CH])
                for d in range(2):
                    ins = dve.tensor_copy(half(LT, d), gram(2 + d, 0))
                ins.then_inc(sems["lt"], 1)
                for d in range(2):
                    dve.tensor_tensor(half(XY, d)[:, :, 0, :], k.bank[6][:, 256 * d:256 * d + 256].rearrange("p (a b) -> p a b", a=4),
                                      row("x1", d), ALU.mult)
                    ins = dve.tensor_tensor(half(XY, d)[:, :, 1, :], gram(2 + d, 0), row("y1", d), ALU.mult)
                    if main:
                        ins = dve.tensor_tensor(half(QB, d), gram(2 + d, 1), row("neg", d), ALU.mult)
                k.dve.link(ins)
                flatxy = XY.rearrange("p a w t -> p (a w) t")
                dve.tensor_tensor(flatxy, flatxy, m3("eye", 0, CH).unsqueeze(1).broadcast_to([P, 2 * NPAIR, CH]), ALU.add).then_inc(sems["xy0"], 1)
                wait(dve, "xy0")
                wait(dve, "gram2")
                for d in range(2):
                    if main:
                        dve.tensor_tensor(half(QK, d), gram(4 + d, 1), row("incl", d), ALU.mult)
                    st = m3("strict", d, P).rearrange("p (h t) -> p h t", h=2).unsqueeze(1).broadcast_to(hfull)
                    ins = dve.tensor_tensor(half(KTBD, d), gram(4 + d, 0).unsqueeze(2).broadcast_to(hfull), st, ALU.mult)
                ins.then_inc(sems["kq"], 1)
                for lv in range(LEVELS):
                    for d in range(2):
                        wait(dve, "tst", 2 * LEVELS, 2 * lv + d + 1)
                        dve.tensor_tensor(half(TBD, d), wide(half(T_, d)).broadcast_to(hfull), head.broadcast_to(hfull),
                                          ALU.mult).then_inc(sems["tbd"], 1)
                    for d in range(2):
                        wait(dve, "xydone", 2 * LEVELS, 2 * lv + d + 1)
                        xy = half(XY, d).rearrange("p a w t -> p (a w t)")
                        dve.tensor_tensor(xy, xy, k.bank[6 + d], ALU.subtract).then_inc(sems["xy"], 1)
                wait(dve, "abar")
                dve.tensor_tensor(ABAR, wide(k.bank[5][:, :].rearrange("p (a b) -> p a b", a=NPAIR)).broadcast_to(full),
                                  head.broadcast_to(full), ALU.mult).then_inc(sems["abarbd"], 1)
                wait(dve, "abarbd")
                if main:
                    dve.tensor_tensor(S0BD, wide(S0).broadcast_to(full), head.broadcast_to(full), ALU.mult).then_inc(sems["s0bd"], 1)
                    wait(dve, "sast")
                    dve.tensor_tensor(SABD, wide(SA).broadcast_to(full), head.broadcast_to(full), ALU.mult).then_inc(sems["sabd"], 1)
                wait(dve, "sdone")
                k.dve.link(dve.tensor_tensor(ST, S0, k.bank[1][:, :].rearrange("p (a b) -> p a b", a=NPAIR), ALU.add))
                if main:
                    wait(dve, "ydone")
                dve.tensor_tensor(ST, ST, half_total, ALU.mult).then_inc(sems["s"], 1)
                wait(dve, "s", 1, 2)
            k.dve.leave(trips)

    def pool(k, pool):
        for trips, first, main in ((4, 0, False), (8, 4, True)):
            with pool.Fori(0, trips) as i:
                wait, prior, tokens, out_tokens = body(i, first, main)
                hfull = [P, 4, 2, CH]

                def loff(lv, d):
                    m = m3("level", 2 * lv + d, P).rearrange("p (h t) -> p h t", h=2).unsqueeze(1).broadcast_to(hfull)
                    pool.tensor_tensor(half(LOFF, d), wide(half(LT, d)).broadcast_to(hfull), m, ALU.mult).then_inc(sems["loff"], 1)

                wait(pool, "lt")
                for d in range(2):
                    loff(0, d)
                wait(pool, "tcopied", 4, 1)
                pool.tensor_tensor(VST, VTK[:, :, 0:CH], VTK[:, :, CH:P], ALU.add).then_inc(sems["vst"], 1)
                for lv in range(1, LEVELS):
                    for d in range(2):
                        wait(pool, "tdone", 2 * LEVELS, 2 * (lv - 1) + d + 1)
                        loff(lv, d)

    return Phase("rwkv_loop", tensor=tensor, vector=vector, scalar=scalar, pool=pool)


def rwkv_output(k):
    M = k.M
    R, K, V = view(M, R_R, 4, T_ALL), view(M, R_K, 4, T_ALL), view(M, R_V, 4, T_ALL)
    AL, GL, A2 = view(M, R_AL, T_ALL), view(M, R_GL, S), view(M, R_A2, 2, 512)
    Y, YB = view(M, A_MIX, 4, S), view(M, R_YB, 4, S)
    SQ, AF, AB, T = view(M, A_A, 4, S), view(M, A_A + 2048, 4, S), view(M, A_A + 4096, 4, S), view(M, A_A + 6144, 4, S)
    G2 = M[0:96, R_G2:R_G2 + 512]
    lo, hi = k.psum[:, 0:2048].rearrange("p (a b) -> p a b", a=4), k.psum[:, 2048:4096].rearrange("p (a b) -> p a b", a=4)
    a, b = k.sem("rwkv_out_product"), k.sem("rwkv_out_vector")
    c = k.sem("rwkv_out_scalar")
    cc = lambda name, f: col(k, name, f)

    def tensor(k, pe):
        headsum = mask(k, "headsum", 0, P)

        def each(base, lhsT, rhs):
            for f in range(4):
                mm = pe.matmul(k.bank[base + f], lhsT(f), rhs(f), start=True, stop=True)
            mm.then_inc(a, 1)

        each(4, lambda f: A2[0:32, 0, f * P:(f + 1) * P], lambda f: AL[0:32, NC_CTX:])
        pe.wait_ge(b, 1)
        each(0, lambda f: headsum, lambda f: Y[:, f, :])
        pe.wait_ge(c, 1)
        each(4, lambda f: A2[0:32, 1, f * P:(f + 1) * P], lambda f: AL[0:32, NC_CTX:])
        pe.wait_ge(b, 2)
        pe.wait_ge(c, 3)
        each(0, lambda f: headsum, lambda f: SQ[:, f, :])
        pe.wait_ge(b, 3)
        each(4, lambda f: headsum, lambda f: T[:, f, :])
        pe.wait_ge(b, 4)
        pe.wait_ge(c, 4)
        each(0, lambda f: G2[:, f * P:(f + 1) * P], lambda f: GL[0:96, :])

    def scalar(k, act):
        def rate(dst, name):
            for f in range(4):
                ins = act.activation(dst[:, f, :], k.bank[4 + f], ACT.Sigmoid, bias=cc(name, f))
            ins.then_inc(c, 1)

        act.wait_ge(a, 1)
        rate(AF, "a0_fwd_2")
        act.wait_ge(a, 3)
        rate(AB, "a0_bwd_2")
        act.wait_ge(b, 2)
        act.activation(SQ, Y, ACT.Square).then_inc(c, 1)
        act.activation(GL[0:96, :], GL[0:96, :], ACT.Sigmoid).then_inc(c, 1)
        act.wait_ge(b, 5)
        act.activation(SQ, SQ, ACT.Sqrt).then_inc(c, 1)

    def vector(k, dve):
        dve.tensor_tensor(Y, Y, YB, ALU.add).then_inc(b, 1)
        dve.wait_ge(b, 1)
        dve.wait_ge(a, 2)
        dve.scalar_tensor_tensor(out=Y, in0=lo, scalar=-1.0 / HEAD, in1=Y, op0=ALU.mult, op1=ALU.add).then_inc(b, 1)
        dve.wait_ge(c, 2)
        k.dve.link(dve.tensor_tensor(AF, AF, AB, ALU.add))
        k.dve.link(dve.tensor_scalar(AF, AF, 0.5, -1.0, ALU.mult, ALU.add))
        for f in range(4):
            ins = dve.tensor_scalar(AF[:, f, :], AF[:, f, :], cc("k_a_2", f), 1.0, ALU.mult, ALU.add)
        k.dve.link(ins)
        k.dve.link(dve.tensor_tensor(AF, AF, K[:, :, NC_CTX:], ALU.mult))
        for f in range(4):
            ins = dve.scalar_tensor_tensor(out=T[:, f, :], in0=R[:, f, NC_CTX:], scalar=cc("r_k_2", f), in1=AF[:, f, :],
                                           op0=ALU.mult, op1=ALU.mult)
        ins.then_inc(b, 1)
        dve.wait_ge(a, 4)
        dve.tensor_scalar(SQ, lo, 1.0 / HEAD, LN_X_EPS, ALU.mult, ALU.add).then_inc(b, 1)
        dve.wait_ge(b, 4)
        dve.reciprocal(SQ, SQ).then_inc(b, 1)
        dve.wait_ge(a, 5)
        k.dve.link(dve.tensor_tensor(AB, hi, V[:, :, NC_CTX:], ALU.mult))
        dve.wait_ge(c, 5)
        for f in range(4):
            ins = dve.scalar_tensor_tensor(out=Y[:, f, :], in0=Y[:, f, :], scalar=cc("ln_x_w_2", f), in1=SQ[:, f, :],
                                           op0=ALU.mult, op1=ALU.mult)
        k.dve.link(ins)
        for f in range(4):
            ins = dve.scalar_tensor_tensor(out=Y[:, f, :], in0=Y[:, f, :], scalar=cc("ln_x_b_2", f), in1=AB[:, f, :],
                                           op0=ALU.add, op1=ALU.add)
        k.dve.link(ins)
        dve.wait_ge(a, 6)
        dve.tensor_tensor(Y, Y, lo, ALU.mult)

    def sync(k, sp):
        for s in k.phase_end.values():
            sp.wait_ge(s, k.phase_index["rwkv_output"] + 1)

    return Phase("rwkv_output", tensor=tensor, vector=vector, scalar=scalar, sync=sync)


def second_block_phases(k, stop):
    M = k.M
    k.rope_in, k.rwkv_in = k.sem("rope_in"), k.sem("rwkv_in")
    A, C, Y = view(M, A_A, KD, S), view(M, A_C, KD, NC_CTX), view(M, A_Y, KD, S)
    ph = [adaptive_phase(k)]
    pre = make_norm(k, "second_norm", k.H, S, [(lambda c: derived_col(k, "gx", c), A, lambda c: mod_col(k, c))], A_SCR)
    cn = make_norm(k, "ctx_norm", k.ctxT, NC_CTX, [(lambda c: derived_col(k, "gc", c), C, lambda c: mod_col(k, c, 1))], A_TMP)
    ph.append(norm_phase(k, "second_norms", [pre, cn]))
    ph += [diff_projection(k), rope_phase(k), diff_attention(k), diff_post(k)]
    ph += [rwkv_projection(k), rwkv_prepare(k), rwkv_loop(k), rwkv_output(k)]
    if stop == "mix2":
        return ph
    ph.append(output_projection(k, "output_projection2", k.a["w_out_2"][0]))
    gate = lambda name, c0: (lambda c: derived_col(k, name, c))
    post = make_norm(k, "mix_post2", Y, S, [], A_SCR)
    pre = make_norm(k, "ffn_pre2", k.H, S, [(lambda c: derived_col(k, "gf", c), A, lambda c: mod_col(k, 24 + c))], A_HID, after=post)
    ph.append(norm_phase(k, "ffn_norm2", [pre], post=(post, lambda c: derived_col(k, "pm", c))))
    if stop == "hmix2":
        return ph
    conv = [{"tap0": VCOL["ffn_tap0"] + off, "tap1": VCOL["ffn_tap1"] + off, "tap2": VCOL["ffn_tap2"] + off,
             "bias": VCOL["ffn_conv_b_2"] + off} for off in (0, KF)]
    w = k.a["w_up_2"][0]
    ph.append(ffn_up(k, "ffn_up2", w, w, 0, D_FF, A_TMP, conv))
    ph.append(ffn_down(k, "ffn_down2", k.a["w_down_2"][0]))
    post = make_norm(k, "ffn_post2", Y, S, [], A_SCR)
    ph.append(norm_phase(k, "layer_norm2", [], post=(post, lambda c: derived_col(k, "pf", c))))
    return ph


def final_phase(k, out):
    X = view(k.M, A_A, 4, D)
    turned, copied = k.sem("out_turned"), k.sem("out_copied")
    o = out[0].rearrange("(t p) d -> t p d", p=P)

    def tensor(k, pe):
        for n in range(8):
            if n >= 4:
                pe.wait_ge(copied, n - 3)
            for j in range(4):
                f = (n % 2) * 4 + j
                mm = pe.transpose(k.bank[n % 4][:, j * P:(j + 1) * P], k.H[:, f, (n // 2) * P:(n // 2 + 1) * P], k.ident)
            mm.then_inc(turned, 1)

    def vector(k, dve):
        for n in range(8):
            dve.wait_ge(turned, n + 1)
            dve.tensor_copy(X[:, n // 2, (n % 2) * 512:(n % 2 + 1) * 512], k.bank[n % 4][:, :]).then_inc(copied, 1)

    def sync(k, sp):
        for t in range(4):
            sp.wait_ge(copied, 2 * t + 2)
            sp.dma_start(o[t], X[:, t, :]).then_inc(k.out_sent, 16)
        sp.wait_ge(k.out_sent, 64)

    return Phase("final", sync=sync, tensor=tensor, vector=vector)


_INS = ['x', 'mem', 'ln_mix_pre', 'ln_mix_post', 'ln_ffn_pre', 'ln_ffn_post', 'ln_mem', 'w_mem_kv', 'w_out',
        'w_ffn_gate', 'w_ffn_up', 'w_ffn_down', 'w_in_a', 'w_spatial', 'b_spatial', 'ln_v_g', 'ln_v_b', 'ln_shared',
        'w_shared_kv', 'b_forget', 'w_in_b', 'c_2', 'ctx_2', 'c_ctx_2', 'w_mod_2', 'b_mod_2', 'g_pre_mix_2',
        'g_post_mix_2', 'g_pre_ffn_2', 'g_post_ffn_2', 'w_in_2', 'rwkv_conv_2', 'w0_fwd_2', 'w2_fwd_2', 'a0_fwd_2',
        'a2_fwd_2', 'w0_bwd_2', 'w2_bwd_2', 'a0_bwd_2', 'a2_bwd_2', 'g2_2', 'k_k_2', 'k_a_2', 'r_k_2', 'ln_x_w_2',
        'ln_x_b_2', 'lam_q1_2', 'lam_k1_2', 'lam_q2_2', 'lam_k2_2', 'subln_w_2', 'w_out_2', 'w_up_2', 'ffn_conv_2',
        'ffn_conv_b_2', 'w_down_2']


def shape_constants():
    p = np.arange(P)
    ident = np.eye(P, dtype=np.float32)
    ones = np.ones((P, P), np.float32)
    causal = np.where(p[None, :] <= p[:, None], 0.0, NEG).astype(np.float32)
    lower = (p[None, :] >= p[:, None]).astype(np.float32)
    inv = (np.float32(10000.0) ** (-np.arange(16, dtype=np.float32) / np.float32(16))).astype(np.float32)
    t = np.arange(S)
    ang = np.concatenate([(t // 64).astype(np.float32)[:, None] * inv, (t % 64).astype(np.float32)[:, None] * inv], 1)
    table = ang.T[p % 32].astype(np.float32)
    rot = np.zeros((P, P), np.float32)
    for m in range(P):
        if m % 64 < 32:
            rot[m + 32, m] = -1.0
        else:
            rot[m - 32, m] = 1.0
    a, hd = p % CH, p // CH
    b = np.arange(CH)
    same2 = a[:, None] // 2 == b[None, :] // 2
    later = [b[None, :] > a[:, None], b[None, :] < a[:, None]]
    earlier = [b[None, :] < a[:, None], b[None, :] > a[:, None]]
    eye = a[:, None] == b[None, :]
    head = hd[:, None] == np.arange(2)[None, :]
    spread = lambda m: (head[:, :, None] & m[:, None, :]).reshape(P, P)
    levels = []
    for lv in range(LEVELS):
        size = 4 << lv
        for d in range(2):
            same = (a[:, None] // size == b[None, :] // size) & (a[:, None] // (size // 2) != b[None, :] // (size // 2))
            levels.append(spread(same & later[d]))
    parts = {"head": head, "eye": eye, "x1": np.concatenate([-1.0 * (same2 & earlier[d]) for d in range(2)], 1),
             "y1": np.concatenate([-1.0 * (same2 & later[d]) for d in range(2)], 1),
             "incl": np.concatenate([later[d] | eye for d in range(2)], 1),
             "neg": np.concatenate([-1.0 * (later[d] | eye) for d in range(2)], 1),
             "strict": np.concatenate([spread(later[d]) for d in range(2)], 1), "level": np.concatenate(levels, 1),
             "reset": np.tile((np.arange(512) % CH != 0)[None, :], (P, 1)), "headsum": hd[:, None] == hd[None, :]}
    rwkv = np.concatenate([parts[n].astype(np.float32) for n in MASKS], 1)
    return {"const_base": np.concatenate([ident, ones, causal, lower], 1),
            "const_rope": np.concatenate([rot, np.cos(table), np.sin(table)], 1), "const_rwkv": rwkv}


def kernel(**inputs):
    import concourse.bacc as _bacc
    from concourse.bass_utils import run_bass_kernel_spmd as _run

    nc = _bacc.Bacc("TRN2", target_bir_lowering=False, num_devices=1)
    arrays, aps = {}, {}
    for name, a in list((n, inputs[n]) for n in _INS) + list(shape_constants().items()):
        a = np.ascontiguousarray(a)
        arrays[f"in_{name}_dram"] = a
        aps[name] = nc.dram_tensor(f"in_{name}_dram", a.shape, mybir.dt.from_np(a.dtype), kind="ExternalInput").ap()
    out = nc.dram_tensor("out_0_dram", (1, S, D), F32, kind="ExternalOutput").ap()
    build(nc, aps, out)
    r = _run(nc, [arrays], core_ids=[0])
    return r.results[0]["out_0_dram"]
```

```python
from contextlib import ExitStack

import numpy as np

import concourse.bass as bass
from concourse import mybir

F32 = mybir.dt.float32
ALU = mybir.AluOpType
ACT = mybir.ActivationFunctionType
AX_X = mybir.AxisListType.X

P = 128
D = 1024
KD = D // P
S = 512
NM = 256
NC_CTX = 256
D_FF = 2816
KF = D_FF // P
MAIN = 768
HEAD = 64
RMS_EPS = 1e-6
LN_EPS = 1e-5
SUBLN_EPS = 1e-5
NEG = -1e30
SLOTS = 4
SLOT_WORDS = 2048

O_H = 0
O_RING = O_H + KD * S
O_MEM = O_RING + SLOTS * SLOT_WORDS
O_CTX = O_MEM + KD * NM
O_VEC = O_CTX + KD * NC_CTX
O_CST = O_VEC + 512
O_MOD = O_CST + 512
O_SML = O_MOD + 256
O_ARENA = O_SML + 256
WORDS = 53100

ROWS = [
    [("ln_mix_pre", 16), ("ln_mix_post", 16), ("ln_ffn_pre", 16), ("ln_ffn_post", 16), ("ln_mem", 16),
     ("ln_shared", 8), ("c_2", 8), ("c_ctx_2", 8), ("g_pre_mix_2", 8), ("g_post_mix_2", 8), ("g_pre_ffn_2", 8)],
    [("g_post_ffn_2", 8), ("b_mod_2", 48), ("w0_fwd_2", 4), ("a0_fwd_2", 4), ("w0_bwd_2", 4), ("a0_bwd_2", 4),
     ("k_k_2", 4), ("k_a_2", 4), ("r_k_2", 4), ("ln_x_w_2", 4), ("ln_x_b_2", 4),
     ("rwkv_tap0", 12), ("rwkv_tap1", 12), ("rwkv_tap2", 12)],
    [("ffn_tap0", 44), ("ffn_tap1", 44)],
    [("ffn_tap2", 44), ("ffn_conv_b_2", 44), ("subln_w_2", 1), ("rwkv_wa_taps", 3), ("rwkv_g_taps", 3)],
]
VCOL = {}
for _t, _rows in enumerate(ROWS):
    _r = 0
    for _name, _n in _rows:
        VCOL[_name] = _t * P + _r
        _r += _n


class Chain:

    def __init__(self, eng, sem):
        self.eng, self.sem, self.count, self.per, self.i, self.k = eng, sem, 0, 0, None, 0

    def link(self, ins):
        ins.then_inc(self.sem, 1)
        if self.i is None:
            self.count += 1
            self.eng.wait_ge(self.sem, self.count)
        else:
            self.k += 1
            self.eng.wait_ge(self.sem, self.i * self.per + (self.count + self.k))

    def enter(self, i, per):
        self.i, self.per, self.k = i, per, 0

    def leave(self, trips):
        assert self.k == self.per, (self.k, self.per)
        self.count += trips * self.per
        self.i = None


class Stream:

    def __init__(self, k, eng):
        self.k, self.eng, self.n, self.i, self.per = k, eng, 0, None, 0

    def enter(self, i, per):
        assert per % SLOTS == 0
        self.i, self.per, self.start = i, per, self.n

    def leave(self, trips):
        assert self.n - self.start == self.per
        self.n = self.start + trips * self.per
        self.i = None

    def load(self, src, kc, cols):
        n, e = self.n, self.eng
        if n >= SLOTS:
            need = 2 * (n - SLOTS + 1)
            e.wait_ge(self.k.half_done, need if self.i is None else self.i * (2 * self.per) + need)
        e.dma_start(self.k.slot(n % SLOTS, kc, cols), src).then_inc(self.k.tile_landed[n % SLOTS], 16)
        self.n += 1

    def take(self, kc, cols):
        n = self.n
        need = 16 * (n // SLOTS + 1)
        if self.i is not None:
            need = self.i * (16 * (self.per // SLOTS)) + need
        self.eng.wait_ge(self.k.tile_landed[n % SLOTS], need)
        self.n += 1
        return self.k.slot(n % SLOTS, kc, cols)


class Kit:
    pass


def view(M, off, *dims):
    n = int(np.prod(dims))
    v = M[:, off:off + n]
    if len(dims) == 1:
        return v
    names = "abcde"[:len(dims)]
    return v.rearrange("p (" + " ".join(names) + ") -> p " + " ".join(names),
                       **{c: d for c, d in zip(names[1:], dims[1:])})


def col(k, name, j=0):
    c = O_VEC + VCOL[name] + j
    return k.M[:, c:c + 1]


A_XTOK = O_ARENA
A_MTOK = A_XTOK + 4 * D
A_CTOK = A_MTOK + 2 * D
A_ROWS = A_CTOK + 2 * D


def turns(k):
    M = k.M
    x, m, c, r = view(M, A_XTOK, 4, D), view(M, A_MTOK, 2, D), view(M, A_CTOK, 2, D), view(M, A_ROWS, 4, P)
    out = [([r[:, t, :] for t in range(4)], M[:, O_VEC:O_VEC + 512])]
    for f in range(KD):
        out.append(([x[:, t, f * P:(f + 1) * P] for t in range(4)], M[:, O_H + f * S:O_H + (f + 1) * S]))
    for f in range(0, KD, 2):
        out.append(([m[:, t, g * P:(g + 1) * P] for g in (f, f + 1) for t in range(2)],
                    M[:, O_MEM + f * NM:O_MEM + (f + 2) * NM]))
    for f in range(0, KD, 2):
        out.append(([c[:, t, g * P:(g + 1) * P] for g in (f, f + 1) for t in range(2)],
                    M[:, O_CTX + f * NM:O_CTX + (f + 2) * NM]))
    return out


def setup_sync(k, sp):
    M, a = k.M, k.a
    sp.dma_start(M[:, O_CST:O_CST + 512], a["const_base"]).then_inc(k.const_in, 16)
    sp.dma_start(view(M, A_XTOK, 4, D), a["x"][0].rearrange("(t p) d -> p t d", p=P)).then_inc(k.const_in, 16)
    rows = view(M, A_ROWS, 4, P)
    sp.wait_ge(k.rows_clear, 1)
    n = 0
    for name, (t, r, cnt, width, src) in k.row_sources.items():
        sp.dma_start(rows[r:r + cnt, t, 0:width], src).then_inc(k.rows_in, 16)
        n += 1
    assert n == k.n_rows
    sp.dma_start(view(M, A_MTOK, 2, D), a["mem"][0].rearrange("(t p) d -> p t d", p=P)).then_inc(k.tok_in, 16)
    sp.dma_start(view(M, A_CTOK, 2, D), a["ctx_2"][0].rearrange("(t p) d -> p t d", p=P)).then_inc(k.tok_in, 16)


def setup_tensor(k, pe):
    pe.wait_ge(k.const_in, 32)
    pe.wait_ge(k.rows_in, 16 * k.n_rows)
    for n, (blocks, _) in enumerate(turns(k)):
        if n == 1 + KD:
            pe.wait_ge(k.tok_in, 32)
        if n >= 4:
            pe.wait_ge(k.turn_read, n - 3)
        for j, b in enumerate(blocks):
            mm = pe.transpose(k.bank[n % 4][:, j * P:(j + 1) * P], b, k.ident)
        mm.then_inc(k.turned, 1)


def setup_vector(k, dve):
    dve.memset(view(k.M, A_ROWS, 512), 0.0).then_inc(k.rows_clear, 1)
    for n, (_, dst) in enumerate(turns(k)):
        dve.wait_ge(k.turned, n + 1)
        dve.tensor_copy(dst, k.bank[n % 4][:, :]).then_inc(k.turn_read, 1)


class Norm:
    def __init__(self, k, name, src, n, outs, scratch, post=None, then=None):
        self.src, self.n, self.outs, self.post = src, n, outs, post
        self.sq = view(k.M, scratch, 2, n)
        self.acc = view(k.M, scratch + 2 * n, n)
        self.rstd = view(k.M, scratch + 3 * n, n)
        self.tmp = view(k.M, scratch + 4 * n, 2, n)
        self.nth, k.norms = k.norms, k.norms + 1
        self.pth = k.posts
        s = k.norm_sems
        self.squared, self.added, self.summed, self.inverted = s["squared"], s["added"], s["summed"], s["inverted"]
        self.rooted, self.scaled, self.moved = s["rooted"], s["scaled"], s["moved"]


def norm_scalar(k, act, j, bank):
    for c in range(KD):
        if c >= 2:
            act.wait_ge(j.added, KD * j.nth + c - 1)
        if j.post == "chained":
            act.wait_ge(j.moved, KD * j.src_post + c + 1)
        act.activation(j.sq[:, c % 2, :], j.src[:, c, :], ACT.Square).then_inc(j.squared, 1)
    act.wait_ge(j.inverted, j.nth + 1)
    act.activation(j.rstd, j.rstd, ACT.Sqrt).then_inc(j.rooted, 1)


def norm_tensor(k, pe, j, bank):
    pe.wait_ge(j.added, KD * (j.nth + 1))
    pe.matmul(bank[:, :j.n], k.ones, j.acc, start=True, stop=True).then_inc(j.summed, 1)


def norm_sum_vector(k, dve, j, bank):
    for c in range(KD):
        dve.wait_ge(j.squared, KD * j.nth + c + 1)
        if c == 0:
            dve.tensor_copy(j.acc, j.sq[:, 0, :]).then_inc(j.added, 1)
        else:
            dve.wait_ge(j.added, KD * j.nth + c)
            dve.tensor_tensor(j.acc, j.acc, j.sq[:, c % 2, :], ALU.add).then_inc(j.added, 1)
    dve.wait_ge(j.summed, j.nth + 1)
    k.dve.link(dve.tensor_scalar(j.rstd, bank[:, :j.n], 1.0 / D, RMS_EPS, ALU.mult, ALU.add))
    dve.reciprocal(j.rstd, j.rstd).then_inc(j.inverted, 1)
    dve.wait_ge(j.rooted, j.nth + 1)


def norm_scale_vector(k, dve, j):
    for gain, dst, shift in j.outs:
        for c in range(KD):
            ins = dve.scalar_tensor_tensor(out=dst[:, c, :], in0=j.src[:, c, :], scalar=gain(c), in1=j.rstd,
                                           op0=ALU.mult, op1=ALU.mult)
            if shift is not None:
                k.dve.link(ins)
                dve.tensor_scalar(dst[:, c, :], dst[:, c, :], shift(c), None, ALU.add)


def post_scale_vector(k, dve, j, gain):
    for c in range(KD):
        if c >= 2:
            dve.wait_ge(j.moved, KD * j.pth + c - 1)
        dve.scalar_tensor_tensor(out=j.tmp[:, c % 2, :], in0=j.src[:, c, :], scalar=gain(c), in1=j.rstd,
                                 op0=ALU.mult, op1=ALU.mult).then_inc(j.scaled, 1)


def post_add_pool(k, pool, j):
    H = k.H
    for c in range(KD):
        pool.wait_ge(j.scaled, KD * j.pth + c + 1)
        pool.tensor_tensor(H[:, c, :], H[:, c, :], j.tmp[:, c % 2, :], ALU.add).then_inc(j.moved, 1)


class Phase:

    def __init__(self, name, sync=None, tensor=None, vector=None, scalar=None, pool=None):
        self.name, self.sync, self.tensor, self.vector, self.scalar, self.pool = name, sync, tensor, vector, scalar, pool


def block_feature(pe, bank, w, c0, m, rhs, kc, k0=0, start=True, stop=True):
    for q in range(kc):
        mm = pe.matmul(bank, w[:, q, c0:c0 + m], rhs(k0 + q), start=start and q == 0, stop=stop and q == kc - 1)
    return mm


def block_token(pe, bank, act_chunk, w, kc):
    for q in range(kc):
        mm = pe.matmul(bank, act_chunk(q), w[:, q, :], start=q == 0, stop=q == kc - 1)
    return mm


def build(nc, a, out, stop=None, consts=None):
    k = Kit()
    k.a = a
    with ExitStack() as ctx:
        k.M = ctx.enter_context(nc.sbuf_tensor("sbuf", [P, WORDS], F32))
        k.psum = ctx.enter_context(nc.psum_tensor("psum", [P, 8 * 512], F32))
        k.bank = [k.psum[:, 512 * i:512 * (i + 1)] for i in range(8)]
        names = []

        def sem(name):
            names.append(name)
            return ctx.enter_context(nc.semaphore(name))

        k.sem = sem
        M = k.M
        k.ident = M[:, O_CST:O_CST + P]
        k.ones = M[:, O_CST + P:O_CST + 2 * P]
        k.causal = M[:, O_CST + 2 * P:O_CST + 3 * P]
        k.lower = M[:, O_CST + 3 * P:O_CST + 4 * P]
        k.H = view(M, O_H, KD, S)
        k.memT = view(M, O_MEM, KD, NM)
        k.ctxT = view(M, O_CTX, KD, NC_CTX)
        k.slot = lambda n, kc, cols: view(M, O_RING + n * SLOT_WORDS, kc, cols)
        k.const_in, k.tok_in, k.rows_in, k.rows_clear = sem("const_in"), sem("tok_in"), sem("rows_in"), sem("rows_clear")
        k.turned, k.turn_read, k.out_sent, k.half_done = sem("turned"), sem("turn_read"), sem("out_sent"), sem("half_done")
        k.dve_steps, k.act_steps, k.pool_steps = sem("dve_steps"), sem("act_steps"), sem("pool_steps")
        k.norms, k.posts = 0, 0
        k.norm_sems = {s: sem(f"norm_{s}") for s in ("squared", "added", "summed", "inverted", "rooted", "scaled", "moved")}
        k.tile_landed = [sem(f"tile_landed{i}") for i in range(SLOTS)]
        k.phase_end = {e: sem(f"phase_end_{e}") for e in ("tensor", "vector", "scalar", "pool")}

        k.row_sources = {}
        for t, rows in enumerate(ROWS):
            r = 0
            for name, n in rows:
                w = P
                if name in a:
                    h = a[name]
                    src = h.rearrange(" ".join("abcd"[:len(h.shape)]) + " -> (" + " ".join("abcd"[:len(h.shape)]) + ")") if len(h.shape) > 1 else h
                    src = src.rearrange("(c p) -> c p", p=P)
                elif name.startswith("rwkv_tap"):
                    src = a["rwkv_conv_2"][0, int(name[-1]), 0:12 * P].rearrange("(c p) -> c p", p=P)
                elif name.startswith("ffn_tap"):
                    src = a["ffn_conv_2"][0, int(name[-1])].rearrange("(c p) -> c p", p=P)
                elif name == "rwkv_wa_taps":
                    src, w = a["rwkv_conv_2"][0, :, 1536:1600], 64
                else:
                    src, w = a["rwkv_conv_2"][0, :, 1600:1696], 96
                k.row_sources[name] = (t, r, n, w, src)
                r += n
        k.n_rows = len(k.row_sources)

        phases = [Phase("setup", sync=setup_sync, tensor=setup_tensor, vector=setup_vector)]
        phases += first_block_phases(k, stop)
        if stop is None or stop.endswith("2"):
            phases += second_block_phases(k, stop)
        k.phase_index = {p.name: n for n, p in enumerate(phases)}
        phases.append(final_phase(k, out))
        block = ctx.enter_context(nc.Block())

        def boundary(eng, me, n):
            eng.drain().then_inc(k.phase_end[me], 1)
            for other, s in k.phase_end.items():
                if other != me:
                    eng.wait_ge(s, n + 1)

        @block.sync
        def _(sp):
            k.sp_stream = Stream(k, sp)
            for ph in phases:
                if ph.sync:
                    ph.sync(k, sp)

        @block.tensor
        def _(pe):
            k.pe_stream = Stream(k, pe)
            for n, ph in enumerate(phases):
                if ph.tensor:
                    ph.tensor(k, pe)
                boundary(pe, "tensor", n)

        @block.vector
        def _(dve):
            k.dve = Chain(dve, k.dve_steps)
            for n, ph in enumerate(phases):
                if ph.vector:
                    ph.vector(k, dve)
                boundary(dve, "vector", n)

        @block.scalar
        def _(act):
            k.act = Chain(act, k.act_steps)
            for n, ph in enumerate(phases):
                if ph.scalar:
                    ph.scalar(k, act)
                boundary(act, "scalar", n)

        @block.gpsimd
        def _(pool):
            k.pool = Chain(pool, k.pool_steps)
            for n, ph in enumerate(phases):
                if ph.pool:
                    ph.pool(k, pool)
                boundary(pool, "pool", n)


A_A = O_ARENA
A_B = A_A + KD * S
A_MIX = A_B + KD * S
A_Y = A_MIX + KD * S
A_HID = A_Y + KD * S
A_SCR = A_HID + KF * S
A_TMP = A_SCR + 6 * S
assert A_TMP + 4 * S <= WORDS
A_MN = A_HID
A_KM = A_MN + KD * NM
A_VM = A_KM + 2 * NM
A_QM = A_VM + 2 * NM
A_V = A_QM + 2 * S
A_K = A_V + 4 * MAIN
assert A_K + 6 * S <= A_SCR
A_Q = A_Y
A_NEGC = A_Y + 6 * S
A_WS = A_Y
A_BC = A_Y + 2 * 6 * P
A_PT = A_A
A_PR = A_TMP


def norm_phase(k, name, jobs, post=None):

    def tensor(k, pe):
        if post:
            norm_tensor(k, pe, post[0], k.bank[7])
        for n, j in enumerate(jobs):
            norm_tensor(k, pe, j, k.bank[n])

    def scalar(k, act):
        if post:
            norm_scalar(k, act, post[0], k.bank[7])
        for n, j in enumerate(jobs):
            norm_scalar(k, act, j, k.bank[n])

    def vector(k, dve):
        if post:
            norm_sum_vector(k, dve, post[0], k.bank[7])
            post_scale_vector(k, dve, post[0], post[1])
        for n, j in enumerate(jobs):
            norm_sum_vector(k, dve, j, k.bank[n])
            norm_scale_vector(k, dve, j)

    def pool(k, pool):
        if post:
            post_add_pool(k, pool, post[0])

    return Phase(name, tensor=tensor, scalar=scalar, vector=vector, pool=pool)


def make_norm(k, name, src, n, outs, scratch, after=None):
    j = Norm(k, name, src, n, outs, scratch)
    if not outs:
        k.posts += 1
    if after is not None:
        j.post, j.src_post = "chained", after.pth
    return j


def mem_projection(k, L):
    t0 = k.plan
    k.plan += 2
    MN, KM, VM = view(k.M, A_MN, KD, NM), view(k.M, A_KM, 2, NM), view(k.M, A_VM, 2, NM)
    w = k.a["w_mem_kv"][L].rearrange("(c p) n -> p c n", p=P)

    def sync(k, sp):
        for t in range(2):
            k.sp_stream.load(w[:, :, t * 256:(t + 1) * 256], KD, 256)

    def tensor(k, pe):
        wk = k.pe_stream.take(KD, 256)
        for b in range(2):
            block_feature(pe, k.bank[b][:, :NM], wk, b * P, P, lambda q: MN[:, q, :], KD).then_inc(k.half_done, 1)
        wv = k.pe_stream.take(KD, 256)
        for t in range(2):
            block_token(pe, k.bank[2 + t][:, :NM], lambda q: MN[:, q, t * P:(t + 1) * P], wv, KD).then_inc(k.half_done, 1)

    def vector(k, dve):
        for b in range(4):
            dve.wait_ge(k.half_done, 2 * t0 + b + 1)
            dst = KM[:, b, :] if b < 2 else VM[:, b - 2, :]
            dve.tensor_copy(dst, k.bank[b][:, :NM])

    return Phase(f"mem_projection{L}", sync=sync, tensor=tensor, vector=vector)


def load_columns(k, w, c0, c1):
    for c in range(c0, c1, 256):
        k.sp_stream.load(w[:, :, c:min(c + 256, c1)], KD, min(256, c1 - c))


def input_projection_a(k):
    t0 = k.plan
    k.plan += 7
    M = k.M
    A, U, V, QM = view(M, A_A, KD, S), view(M, A_B, 6, S), view(M, A_V, 4, MAIN), view(M, A_QM, 2, S)
    w = k.a["w_in_a"][0].rearrange("(c p) n -> p c n", p=P)
    read = k.sem("in_a_read")
    halves = [("u", b) for b in range(6)] + [("v", c, t) for c in range(3) for t in range(2)] + [("q", b) for b in range(2)]

    def sync(k, sp):
        load_columns(k, w, 0, 1792)
        sp.dma_start(view(M, A_WS, 6, P), k.a["w_spatial"][0].rearrange("g t s -> t g s")).then_inc(k.ws_in, 16)
        for n, name in enumerate(("ln_v_g", "ln_v_b")):
            sp.dma_start(view(M, A_BC, 3, MAIN)[:, n, :], k.a[name].broadcast_to([P, MAIN])).then_inc(k.ws_in, 16)
        sp.dma_start(view(M, A_BC, 3, MAIN)[:, 2, :],
                     k.a["b_spatial"].rearrange("a g t -> a (g t)").broadcast_to([P, MAIN])).then_inc(k.ws_in, 16)

    def tensor(k, pe):
        for h, half in enumerate(halves):
            if h % 2 == 0:
                wt = k.pe_stream.take(KD, 256)
            if h >= 4:
                pe.wait_ge(read, h - 3)
            bank = k.bank[h % 4]
            if half[0] == "v":
                for t in range(2):
                    tok = 2 * half[2] + t
                    mm = block_token(pe, bank[:, t * 256:(t + 1) * 256], lambda q: A[:, q, tok * P:(tok + 1) * P], wt, KD)
            else:
                mm = block_feature(pe, bank[:, :], wt, (half[1] % 2) * P, P, lambda q: A[:, q, :], KD)
            mm.then_inc(k.half_done, 1)

    def scalar(k, act):
        for h, half in enumerate(halves):
            act.wait_ge(k.half_done, 2 * t0 + h + 1)
            bank = k.bank[h % 4][:, :]
            if half[0] == "u":
                act.activation(U[:, half[1], :], bank, ACT.Gelu_apprx_tanh).then_inc(read, 1)
            elif half[0] == "v":
                _, c, t = half
                act.activation(V[:, 2 * t:2 * t + 2, c * 256:(c + 1) * 256], bank.rearrange("p (a b) -> p a b", a=2),
                               ACT.Gelu_apprx_tanh).then_inc(read, 1)
            else:
                act.activation(QM[:, half[1], :], bank, ACT.Copy, scale=HEAD ** -0.5).then_inc(read, 1)

    return Phase("input_projection_a", sync=sync, tensor=tensor, scalar=scalar)


def spatial_prepare(k):
    M = k.M
    V, WS, BC = view(M, A_V, 4, MAIN), view(M, A_WS, 12, P), view(M, A_BC, 3, MAIN)
    turned, st = k.sem("ws_turned"), k.sem("v_stats")
    stats, mv = view(M, O_SML, 4, 12), view(M, O_SML + 48, 4, 2)
    rooted = k.sem("v_rooted")

    def tensor(k, pe):
        pe.wait_ge(k.ws_in, 64)
        for g in range(6):
            mm = pe.transpose(k.bank[g // 4][:, (g % 4) * P:(g % 4 + 1) * P], WS[:, g, :], k.ident)
        mm.then_inc(turned, 1)

    def vector(k, dve):
        for t in range(4):
            for n in range(2):
                ins = dve.bn_stats(stats[:, t, 6 * n:6 * n + 6], V[:, t, n * 384:(n + 1) * 384])
        k.dve.link(ins)
        for t in range(4):
            ins = dve.bn_aggr(mv[:, t, :], stats[:, t, :])
        k.dve.link(ins)
        k.dve.link(dve.tensor_scalar(mv[:, :, 1:2], mv[:, :, 1:2], LN_EPS, None, ALU.add))
        dve.reciprocal(mv[:, :, 1:2], mv[:, :, 1:2]).then_inc(st, 1)
        dve.wait_ge(turned, 1)
        dve.wait_ge(k.ws_in, 64)
        for g in range(6):
            dve.tensor_tensor(WS[:, 6 + g, :], k.bank[g // 4][:, (g % 4) * P:(g % 4 + 1) * P], k.lower, ALU.mult)
        dve.wait_ge(rooted, 1)
        for t in range(4):
            k.dve.link(dve.tensor_scalar(V[:, t, :], V[:, t, :], mv[:, t, 0:1], mv[:, t, 1:2], ALU.subtract, ALU.mult))
            k.dve.link(dve.tensor_tensor(V[:, t, :], V[:, t, :], BC[:, 0, :], ALU.mult))
            dve.tensor_tensor(V[:, t, :], V[:, t, :], BC[:, 1, :], ALU.add)

    def scalar(k, act):
        act.wait_ge(st, 1)
        act.activation(mv[:, :, 1:2], mv[:, :, 1:2], ACT.Sqrt).then_inc(rooted, 1)

    return Phase("spatial_prepare", tensor=tensor, vector=vector, scalar=scalar)


def spatial_gate(k):
    M = k.M
    V, WS, BC, U, MIX = (view(M, A_V, 4, MAIN), view(M, A_WS, 12, P), view(M, A_BC, 3, MAIN), view(M, A_B, 6, S),
                         view(M, A_MIX, KD, S))
    mixed, read = k.sem("spatial_mixed"), k.sem("spatial_read")

    def tensor(k, pe):
        for g in range(6):
            if g >= 4:
                pe.wait_ge(read, g - 3)
            for c in range(4):
                mm = pe.matmul(k.bank[g % 4][:, c * P:(c + 1) * P], V[:, c, g * P:(g + 1) * P], WS[:, 6 + g, :],
                               start=True, stop=True)
            mm.then_inc(mixed, 1)

    def vector(k, dve):
        for g in range(6):
            dve.wait_ge(mixed, g + 1)
            bias = BC[:, 2:3, g * P:(g + 1) * P].broadcast_to([P, 4, P])
            ins = dve.tensor_tensor(MIX[:, g, :].rearrange("p (c t) -> p c t", c=4),
                                    k.bank[g % 4][:, :].rearrange("p (c t) -> p c t", c=4), bias, ALU.add)
            ins.then_inc(read, 1)
            dve.wait_ge(read, g + 1)
            dve.tensor_tensor(MIX[:, g, :], MIX[:, g, :], U[:, g, :], ALU.mult)

    return Phase("spatial_gate", tensor=tensor, vector=vector)


class Attention:

    def __init__(self, name, heads, keys, q, key, value, out, negc=None):
        self.name, self.heads, self.keys, self.q, self.key, self.value, self.out, self.negc = \
            name, heads, keys, q, key, value, out, negc


def attention_phase(k, s):
    M = k.M
    NJ = 4
    pt = view(M, A_PT, 2, NJ, S)
    pr = view(M, A_PR, 3, S)
    small = view(M, O_SML, 4, 2)
    scored, maxed, raised, summed_inv, ready, turned, copied, valued, taken = (
        k.sem(f"{s.name}_{x}") for x in ("scored", "maxed", "raised", "inv", "ready", "turned", "copied", "valued", "taken"))
    units = [(h, i) for h in range(s.heads) for i in range(4)]
    nk = [s.keys(i) for i in range(4)]
    rows = lambda h: slice(64 * (h % 2), 64 * (h % 2) + 64)
    last_unit = lambda h: 4 * h + 3

    def tensor(k, pe):
        for u in range(len(units) + 2):
            if u < len(units):
                h, i = units[u]
                bank = k.bank[u % 3][:, :nk[i]]
                if u >= 3:
                    pe.wait_ge(raised, u - 2)
                if s.negc is not None:
                    pe.matmul(bank, k.ident[:, h:h + 1].broadcast_to([P, P]), s.negc[:, :nk[i]], start=True, stop=False)
                    pe.matmul(bank[:, i * P:], k.ident, k.causal, start=False, stop=False)
                pe.matmul(bank, s.q(h, i), s.key(h, nk[i]), start=s.negc is None, stop=True).then_inc(scored, 1)
            if u >= 2:
                v = u - 2
                h, i = units[v]
                pe.wait_ge(ready, v + 1)
                if v >= 2:
                    pe.wait_ge(copied, v - 1)
                for j in range(nk[i] // P):
                    mm = pe.transpose(k.bank[3 + v % 2][:, j * P:(j + 1) * P], pr[:, v % 3, j * P:(j + 1) * P], k.ident)
                mm.then_inc(turned, 1)
                if i == 3 and h >= 1:
                    values(pe, h - 1)
        values(pe, s.heads - 1)

    def values(pe, h):
        pe.wait_ge(copied, last_unit(h) + 1)
        if h >= 2:
            pe.wait_ge(taken, h - 1)
        out = k.bank[5 + h % 2][rows(h), :]
        n = nk[3] // P
        for j in range(n):
            q0 = j * P if s.negc is not None else 0
            mm = pe.matmul(out[:, q0:], s.value(h, j), pt[:, h % 2, j, q0:], start=j == 0, stop=j == n - 1)
        mm.then_inc(valued, 1)

    def vector(k, dve):
        for u in range(len(units) + 1):
            if u < len(units):
                h, i = units[u]
                dve.wait_ge(scored, u + 1)
                k.dve.link(dve.tensor_reduce(small[:, u % 4, 0:1], k.bank[u % 3][:, :nk[i]], AX_X, ALU.max))
                dve.tensor_scalar(small[:, u % 4, 0:1], small[:, u % 4, 0:1], -1.0, None, ALU.mult).then_inc(maxed, 1)
            if u >= 1:
                v = u - 1
                h, i = units[v]
                dve.wait_ge(raised, v + 1)
                k.dve.link(dve.reciprocal(small[:, v % 4, 1:2], small[:, v % 4, 1:2]))
                dve.tensor_scalar(pr[:, v % 3, :nk[i]], pr[:, v % 3, :nk[i]], small[:, v % 4, 1:2], None,
                                  ALU.mult).then_inc(ready, 1)
                if i == 0 and h >= 2:
                    take(dve, h - 2)
        take(dve, s.heads - 2)
        take(dve, s.heads - 1)

    def take(dve, h):
        dve.wait_ge(valued, h + 1)
        dve.tensor_copy(s.out(h), k.bank[5 + h % 2][rows(h), :]).then_inc(taken, 1)

    def scalar(k, act):
        for u in range(len(units) + 3):
            if u < len(units):
                h, i = units[u]
                act.wait_ge(maxed, u + 1)
                if u >= 3:
                    act.wait_ge(turned, u - 2)
                act.activation(pr[:, u % 3, :nk[i]], k.bank[u % 3][:, :nk[i]], ACT.Exp, bias=small[:, u % 4, 0:1],
                               accum_out=small[:, u % 4, 1:2]).then_inc(raised, 1)
            if u >= 3:
                v = u - 3
                h, i = units[v]
                act.wait_ge(turned, v + 1)
                if h >= 2:
                    act.wait_ge(valued, h - 1)
                n = nk[i] // P
                act.activation(pt[:, h % 2, 0:n, i * P:(i + 1) * P],
                               k.bank[3 + v % 2][:, :nk[i]].rearrange("p (j q) -> p j q", q=P), ACT.Copy).then_inc(copied, 1)

    return Phase(s.name, tensor=tensor, vector=vector, scalar=scalar)


def mem_attention(k, L):
    M = k.M
    QM, KM, VM, MIX = view(M, A_QM, 2, S), view(M, A_KM, 2, NM), view(M, A_VM, 2, NM), view(M, A_MIX, KD, S)
    r = lambda h: slice(64 * (h % 2), 64 * (h % 2) + 64)
    return attention_phase(k, Attention(
        f"mem_attention{L}", 4, lambda i: NM,
        q=lambda h, i: QM[r(h), h // 2, i * P:(i + 1) * P],
        key=lambda h, n: KM[r(h), h // 2, :n],
        value=lambda h, j: VM[:, j, h * HEAD:(h + 1) * HEAD],
        out=lambda h: MIX[r(h), 6 + h // 2, :]))


def fox_attention(k):
    M = k.M
    Q, K, V, MIX = view(M, A_Q, 6, S), view(M, A_K, 6, S), view(M, A_V, 4, MAIN), view(M, A_MIX, KD, S)
    r = lambda h: slice(64 * (h % 2), 64 * (h % 2) + 64)
    return attention_phase(k, Attention(
        "fox_attention", 12, lambda i: P * (i + 1),
        q=lambda h, i: Q[r(h), h // 2, i * P:(i + 1) * P],
        key=lambda h, n: K[r(h), h // 2, :n],
        value=lambda h, j: V[:, j, h * HEAD:(h + 1) * HEAD],
        out=lambda h: MIX[r(h), h // 2, :],
        negc=view(M, A_NEGC, S)))


def input_projection_b(k):
    t0 = k.plan
    k.plan += 11
    M = k.M
    A, B = view(M, A_A, KD, S), view(M, A_B, KD, S)
    Q, K, V, QM, NEGC = view(M, A_Q, 6, S), view(M, A_K, 6, S), view(M, A_V, 4, MAIN), view(M, A_QM, 2, S), view(M, A_NEGC, S)
    wkv = k.a["w_shared_kv"].rearrange("(c p) n -> p c n", p=P)
    wb = k.a["w_in_b"][0].rearrange("(c p) n -> p c n", p=P)
    read, cleared = k.sem("in_b_read"), k.sem("in_b_cleared")
    halves = ([("k", b) for b in range(6)] + [("v", c, t) for c in range(3) for t in range(2)] + [("f", 0), ("f", 1)]
              + [("q", b) for b in range(6)] + [("m", b) for b in range(2)])

    def sync(k, sp):
        load_columns(k, wkv, 0, 1536)
        sp.dma_start(k.bf, k.a["b_forget"].rearrange("(h o) -> h o", o=1)).then_inc(k.bf_in, 16)
        load_columns(k, wkv, 1536, 1548)
        load_columns(k, wb, 0, 1024)

    def tensor(k, pe):
        for h, half in enumerate(halves):
            if h % 2 == 0:
                wt = k.pe_stream.take(KD, 12 if half[0] == "f" else 256)
            if h >= 4:
                pe.wait_ge(read, h - 3)
            bank = k.bank[h % 4]
            X = B if half[0] in "kvf" else A
            if half[0] == "v":
                for t in range(2):
                    tok = 2 * half[2] + t
                    mm = block_token(pe, bank[:, t * 256:(t + 1) * 256], lambda q: X[:, q, tok * P:(tok + 1) * P], wt, KD)
            elif half[0] == "f":
                bank = k.bank[4]
                mm = block_feature(pe, bank[0:12, :], Shift(wt, 4 * half[1]), 0, 12, lambda q: X[:, q, :], 4, 4 * half[1],
                                   start=half[1] == 0, stop=half[1] == 1)
            else:
                mm = block_feature(pe, bank[:, :], wt, (half[1] % 2) * P, P, lambda q: X[:, q, :], KD)
            mm.then_inc(k.half_done, 1)

    def scalar(k, act):
        for h, half in enumerate(halves):
            act.wait_ge(k.half_done, 2 * t0 + h + 1)
            bank = k.bank[h % 4][:, :]
            if half[0] == "v":
                _, c, t = half
                act.activation(V[:, 2 * t:2 * t + 2, c * 256:(c + 1) * 256], bank.rearrange("p (a b) -> p a b", a=2),
                               ACT.Copy).then_inc(read, 1)
            elif half[0] == "f":
                if half[1] == 0:
                    act.wait_ge(cleared, 1)
                    act.activation(k.scrap, k.scrap, ACT.Copy).then_inc(read, 1)
                else:
                    act.activation(NEGC[0:12, :], k.bank[4][0:12, :], ACT.Copy).then_inc(read, 1)
            else:
                dst = {"k": K, "q": Q, "m": QM}[half[0]][:, half[1], :]
                act.activation(dst, bank, ACT.Copy, scale=1.0 if half[0] == "k" else HEAD ** -0.5).then_inc(read, 1)

    def vector(k, dve):
        k.dve.link(dve.memset(k.scrap, 0.0))
        dve.memset(NEGC, 0.0).then_inc(cleared, 1)

    return Phase("input_projection_b", sync=sync, tensor=tensor, scalar=scalar, vector=vector)


class Shift:

    def __init__(self, w, first):
        self.w, self.first = w, first

    def __getitem__(self, key):
        a, q, c = key
        return self.w[a, q + self.first, c]


def forget_phase(k):
    M = k.M
    Z = view(M, A_NEGC, S)
    E, R = view(M, A_SCR, S), view(M, A_SCR + S, S)
    a, b = k.sem("forget_abs"), k.sem("forget_log")

    def vector(k, dve):
        dve.wait_ge(k.bf_in, 16)
        k.dve.link(dve.tensor_scalar(R[0:12, :], Z[0:12, :], k.bf, -1.0, ALU.add, ALU.mult))
        k.dve.link(dve.tensor_scalar(E[0:12, :], R[0:12, :], -1.0, None, ALU.mult))
        k.dve.link(dve.tensor_tensor(E[0:12, :], E[0:12, :], R[0:12, :], ALU.max))
        dve.tensor_scalar(R[0:12, :], R[0:12, :], 0.0, None, ALU.max).then_inc(a, 1)
        dve.wait_ge(b, 1)
        k.dve.link(dve.tensor_tensor(R[0:12, :], R[0:12, :], E[0:12, :], ALU.add))
        k.dve.link(dve.memset(E[0:12, :], 1.0))
        k.dve.link(dve.tensor_tensor_scan(Z[0:12, :], E[0:12, :], R[0:12, :], 0.0, ALU.mult, ALU.add))

    def scalar(k, act):
        act.wait_ge(a, 1)
        k.act.link(act.activation(E[0:12, :], E[0:12, :], ACT.Exp, scale=-1.0))
        act.activation(E[0:12, :], E[0:12, :], ACT.Ln, bias=1.0).then_inc(b, 1)

    return Phase("forget", vector=vector, scalar=scalar)


def output_projection(k, name, w):
    t0 = k.plan
    k.plan += 4
    MIX, Y = view(k.M, A_MIX, KD, S), view(k.M, A_Y, KD, S)
    read = k.sem(f"{name}_read")
    w = w.rearrange("(c p) n -> p c n", p=P)

    def sync(k, sp):
        load_columns(k, w, 0, D)

    def tensor(k, pe):
        for b in range(KD):
            if b % 2 == 0:
                wt = k.pe_stream.take(KD, 256)
            if b >= 4:
                pe.wait_ge(read, b - 3)
            block_feature(pe, k.bank[b % 4][:, :], wt, (b % 2) * P, P, lambda q: MIX[:, q, :], KD).then_inc(k.half_done, 1)

    def vector(k, dve):
        for b in range(KD):
            dve.wait_ge(k.half_done, 2 * t0 + b + 1)
            dve.tensor_copy(Y[:, b, :], k.bank[b % 4][:, :]).then_inc(read, 1)

    return Phase(name, sync=sync, tensor=tensor, vector=vector)


def paired_units(k, eng, chains, unit):
    trips = KF // 4
    with eng.Fori(0, trips) as i:
        for c, n in chains:
            c.enter(i, n)
        for u in range(2):
            unit(i, u)
    for c, n in chains:
        c.leave(trips)
    unit(None, 2 * trips)


def at(i, per, off):
    return off if i is None else i * per + off


def ffn_up(k, name, w1, w2, c1, c2, tmp, conv=None):
    t0 = k.plan
    k.plan += KF
    M = k.M
    A, HID, T = view(M, A_A, KD, S), view(M, A_HID, KF, S), view(M, tmp, 4, S)
    w1 = w1.rearrange("(c p) n -> p c n", p=P)
    w2 = w2.rearrange("(c p) n -> p c n", p=P)
    free, gated, centred, tapped = (k.sem(f"{name}_{x}") for x in ("banks_free", "gated", "centred", "tapped"))

    def sync(k, sp):
        def unit(i, u):
            for w, c in ((w1, c1), (w2, c2)):
                k.sp_stream.load(w[:, :, c + 256 * u:][:, :, bass.ds(at(i, 512, 0), 256)], KD, 256)
        paired_units(k, sp, [(k.sp_stream, 4)], unit)

    def tensor(k, pe):
        pe.sem_inc(free, 2)

        def unit(i, u):
            pe.wait_ge(free, at(i, 2, u + 1))
            for g in range(2):
                wt = k.pe_stream.take(KD, 256)
                for b in range(2):
                    block_feature(pe, k.bank[4 * (u % 2) + 2 * g + b][:, :], wt, b * P, P, lambda q: A[:, q, :],
                                  KD).then_inc(k.half_done, 1)
        paired_units(k, pe, [(k.pe_stream, 4)], unit)

    def scalar(k, act):
        def unit(i, u):
            for b in range(2):
                act.wait_ge(k.half_done, at(i, 8, 2 * t0 + 4 * u + b + 1))
                if b == 0:
                    act.wait_ge(free, at(i, 2, u + 1))
                act.activation(T[:, 2 * (u % 2) + b, :], k.bank[4 * (u % 2) + b][:, :], ACT.Silu).then_inc(gated, 1)
        paired_units(k, act, [], unit)

    def vector(k, dve):
        def unit(i, u):
            for b in range(2):
                dve.wait_ge(k.half_done, at(i, 8, 2 * t0 + 4 * u + 2 + b + 1))
                dve.wait_ge(gated, at(i, 4, 2 * u + b + 1))
                bank = k.bank[4 * (u % 2) + 2 + b][:, :]
                dst = HID[:, bass.ds(at(i, 4, 2 * u + b), 1), :].rearrange("p a b -> p (a b)")
                ins = dve.tensor_tensor(dst, bank, T[:, 2 * (u % 2) + b, :], ALU.mult)
            ins.then_inc(free, 1)
        paired_units(k, dve, [], unit)

    def vec(i, u, b, half, what):
        return M[:, bass.ds(at(i, 4, O_VEC + conv[half][what] + 2 * u + b), 1)]

    def conv_scalar(k, act):
        def unit(i, u):
            for half in range(2):
                for b in range(2):
                    act.wait_ge(k.half_done, at(i, 8, 2 * t0 + 4 * u + 2 * half + b + 1))
                    if half == 0 and b == 0:
                        act.wait_ge(free, at(i, 2, u + 2))
                    act.activation(T[:, 2 * half + b, :], k.bank[4 * (u % 2) + 2 * half + b][:, :], ACT.Identity,
                                   scale=vec(i, u, b, half, "tap1"), bias=vec(i, u, b, half, "bias")).then_inc(centred, 1)
            for b in range(2):
                act.wait_ge(tapped, at(i, 4, 2 * u + b + 1))
                act.activation(T[:, 2 + b, :], T[:, 2 + b, :], ACT.Silu).then_inc(gated, 1)
        paired_units(k, act, [], unit)

    def conv_vector(k, dve):
        def unit(i, u):
            for half in range(2):
                for b in range(2):
                    dve.wait_ge(centred, at(i, 8, 4 * u + 2 * half + b + 1))
                    bank, t = k.bank[4 * (u % 2) + 2 * half + b], T[:, 2 * half + b, :]
                    k.dve.link(dve.scalar_tensor_tensor(out=t[:, 1:S], in0=bank[:, 0:S - 1], scalar=vec(i, u, b, half, "tap0"),
                                                        in1=t[:, 1:S], op0=ALU.mult, op1=ALU.add))
                    ins = dve.scalar_tensor_tensor(out=t[:, 0:S - 1], in0=bank[:, 1:S], scalar=vec(i, u, b, half, "tap2"),
                                                   in1=t[:, 0:S - 1], op0=ALU.mult, op1=ALU.add)
                    if half == 1:
                        ins.then_inc(tapped, 1)
                    else:
                        k.dve.link(ins)
            for b in range(2):
                dve.wait_ge(gated, at(i, 4, 2 * u + b + 1))
                dst = HID[:, bass.ds(at(i, 4, 2 * u + b), 1), :].rearrange("p a b -> p (a b)")
                ins = dve.tensor_tensor(dst, T[:, b, :], T[:, 2 + b, :], ALU.mult)
            ins.then_inc(free, 1)
        paired_units(k, dve, [(k.dve, 12)], unit)

    return Phase(name, sync=sync, tensor=tensor, vector=conv_vector if conv else vector,
                 scalar=conv_scalar if conv else scalar)


def ffn_down(k, name, w):
    t0 = k.plan
    k.plan += 16
    HID, Y = view(k.M, A_HID, KF, S), view(k.M, A_Y, KD, S)
    w = w.rearrange("(h c p) n -> p h c n", h=2, p=P)
    free = k.sem(f"{name}_free")
    KH = KF // 2

    def sync(k, sp):
        with sp.Fori(0, KD // 2) as i:
            k.sp_stream.enter(i, 4)
            for b in range(2):
                for h in range(2):
                    k.sp_stream.load(w[:, h, :, b * P:][:, :, bass.ds(i * 256, P)], KH, P)
        k.sp_stream.leave(KD // 2)

    def tensor(k, pe):
        pe.sem_inc(free, 2)
        with pe.Fori(0, KD // 2) as i:
            k.pe_stream.enter(i, 4)
            for b in range(2):
                pe.wait_ge(free, i * 2 + (b + 1))
                for h in range(2):
                    wt = k.pe_stream.take(KH, P)
                    for q in range(KH):
                        mm = pe.matmul(k.bank[b][:, :], wt[:, q, :], HID[:, KH * h + q, :],
                                       start=h == 0 and q == 0, stop=h == 1 and q == KH - 1)
                        if q in (5, KH - 1):
                            mm.then_inc(k.half_done, 1)
        k.pe_stream.leave(KD // 2)

    def vector(k, dve):
        with dve.Fori(0, KD // 2) as i:
            for b in range(2):
                dve.wait_ge(k.half_done, i * 8 + (2 * t0 + 4 * b + 4))
                dve.tensor_copy(Y[:, bass.ds(i * 2 + b, 1), :].rearrange("p a b -> p (a b)"),
                                k.bank[b][:, :]).then_inc(free, 1)

    return Phase(name, sync=sync, tensor=tensor, vector=vector)


def first_block_phases(k, stop):
    M = k.M
    k.plan = 0
    k.ws_in, k.bf_in = k.sem("spatial_in"), k.sem("b_forget_in")
    k.bf = M[0:12, O_SML + 200:O_SML + 201]
    k.scrap = M[0:1, O_SML + 202:O_SML + 203]
    A, B, Y, MN = view(M, A_A, KD, S), view(M, A_B, KD, S), view(M, A_Y, KD, S), view(M, A_MN, KD, NM)
    g = lambda name, base: (lambda c: col(k, name, base + c))

    ph = []
    for L in range(2):
        norms = []
        if L == 0:
            norms.append(make_norm(k, "mix_norm0", k.H, S, [(g("ln_mix_pre", 0), A, None)], A_SCR))
        norms.append(make_norm(k, f"mem_norm{L}", k.memT, NM, [(g("ln_mem", 8 * L), MN, None)], A_TMP))
        ph.append(norm_phase(k, f"input_norms{L}", norms))
        ph.append(mem_projection(k, L))
        if L == 0:
            ph += [input_projection_a(k), spatial_prepare(k), spatial_gate(k)]
        else:
            ph += [input_projection_b(k), forget_phase(k), fox_attention(k)]
        ph.append(mem_attention(k, L))
        if stop == f"mix{L}":
            return ph
        ph.append(output_projection(k, f"output_projection{L}", k.a["w_out"][L]))
        post = make_norm(k, f"mix_post{L}", Y, S, [], A_SCR)
        pre = make_norm(k, f"ffn_pre{L}", k.H, S, [(g("ln_ffn_pre", 8 * L), A, None)], A_HID, after=post)
        ph.append(norm_phase(k, f"ffn_norm{L}", [pre], post=(post, g("ln_mix_post", 8 * L))))
        if stop == f"hmix{L}":
            return ph
        ph.append(ffn_up(k, f"ffn_up{L}", k.a["w_ffn_gate"][L], k.a["w_ffn_up"][L], 0, 0, A_TMP))
        ph.append(ffn_down(k, f"ffn_down{L}", k.a["w_ffn_down"][L]))
        post = make_norm(k, f"ffn_post{L}", Y, S, [], A_SCR)
        nxt = []
        if L == 0:
            nxt = [make_norm(k, "mix_norm1", k.H, S, [(g("ln_mix_pre", 8), A, None), (g("ln_shared", 0), B, None)],
                             A_HID, after=post)]
        ph.append(norm_phase(k, f"layer_norm{L}", nxt, post=(post, g("ln_ffn_post", 8 * L))))
        if stop == f"h{L}":
            return ph
    return ph


T_ALL = NC_CTX + S
TT = T_ALL // P
LAM_INIT = 0.8 - 0.6 * 1.0
LN_X_EPS = 64e-5
CH = 64
NPAIR = 8
DECAY = -float(np.exp(-0.5))

A_C = A_B
D_Q = A_Y
D_K = D_Q + 4 * S
D_V = D_K + 4 * T_ALL
D_ROPE = D_V + TT * 512
D_PT = D_ROPE + P + 2 * S
D_P = D_PT + 2 * TT * S
D_LAM = D_P + 4 * T_ALL
assert D_LAM + 256 <= WORDS
R_R = A_Y
R_K = R_R + 4 * T_ALL
R_V = R_K + 4 * T_ALL
R_KK = R_V + 4 * T_ALL
R_WA = R_KK + 4 * T_ALL
R_GL = R_WA + T_ALL
R_YB = R_GL + S
R_TMP = R_YB + 4 * S
R_ABD = A_A
R_BBD, R_KBD, R_VBD = R_ABD + 1024, R_ABD + 2048, R_ABD + 3072
R_ATK = R_ABD + 4096
R_BTK, R_KTK, R_VTK = R_ATK + 1024, R_ATK + 2048, R_ATK + 3072
assert R_VTK + 1024 <= A_MIX
R_AR = O_MEM
R_B, R_G2, R_QK, R_QB, R_LT, R_RHO = (O_MEM + 1024 + 512 * n for n in range(6))
R_X, R_Y, R_T = R_TMP, R_TMP + 1024, R_TMP + 2048
R_ABAR = R_T
R_PRE = R_TMP + 3072
R_KTBD = R_TMP + 3584
R_KV = R_KTBD
R_LOFF = R_KTBD + 1024
R_S = R_LOFF + 1024
assert R_S + 1024 <= WORDS
R_MASK = O_RING
MASKS = {}
_off = 0
for _n, _w in (("head", 2), ("x1", 2 * P), ("y1", 2 * P), ("incl", 2 * CH), ("neg", 2 * CH),
               ("strict", 2 * P), ("level", 5 * 2 * P), ("reset", 512), ("headsum", P)):
    MASKS[_n] = _off
    _off += _w
N_MASK = _off
R_W2 = R_MASK + N_MASK
R_KD = R_W2 + 1024
R_A2 = R_KD + 1024
R_AL = R_A2 + 1024
R_SIG = R_AL + T_ALL
assert R_SIG + 1024 <= O_MEM
R_S0, R_SA = R_SIG, R_KD

MOD_DERIVED = ("gx", "gc", "gf", "pm", "pf")


def adaptive_phase(k):
    t0 = k.plan
    k.plan += 24
    M = k.M
    COND = view(M, A_SCR, KD, 2)
    SIL = view(M, A_SCR + 16, KD, 2)
    MOD = view(M, O_MOD, 48, 2)
    w = k.a["w_mod_2"][0].rearrange("(c p) n -> p c n", p=P)
    ready, silu = k.sem("cond_ready"), k.sem("cond_silu")

    def sync(k, sp):
        with sp.Fori(0, 6) as i:
            k.sp_stream.enter(i, 4)
            for t in range(4):
                k.sp_stream.load(w[:, :, 256 * t:][:, :, bass.ds(i * 1024, 256)], KD, 256)
        k.sp_stream.leave(6)

    def tensor(k, pe):
        pe.wait_ge(silu, 1)
        out = k.bank[0][:, 0:96].rearrange("p (n two) -> p n two", two=2)
        with pe.Fori(0, 6) as i:
            k.pe_stream.enter(i, 4)
            for t in range(4):
                wt = k.pe_stream.take(KD, 256)
                for b in range(2):
                    dst = out[:, bass.ds(i * 8 + (2 * t + b), 1), :].rearrange("p a b -> p (a b)")
                    block_feature(pe, dst, wt, b * P, P, lambda q: SIL[:, q, :], KD).then_inc(k.half_done, 1)
        k.pe_stream.leave(6)

    def scalar(k, act):
        for n, name in enumerate(("c_2", "c_ctx_2")):
            ins = act.activation(SIL[:, :, n:n + 1], M[:, O_VEC + VCOL[name]:O_VEC + VCOL[name] + KD].rearrange(
                "p (c o) -> p c o", o=1), ACT.Silu)
        ins.then_inc(silu, 1)

    def vector(k, dve):
        dve.wait_ge(k.half_done, 2 * (t0 + 24))
        vec = lambda name, n=KD: M[:, O_VEC + VCOL[name]:O_VEC + VCOL[name] + n].rearrange("p (c o) -> p c o", o=1)
        k.dve.link(dve.tensor_tensor(MOD, k.bank[0][:, 0:96].rearrange("p (n two) -> p n two", two=2),
                                     vec("b_mod_2", 48).broadcast_to([P, 48, 2]), ALU.add))
        for name, (v, c, which, plus) in (("gx", ("g_pre_mix_2", 8, 0, 1.0)), ("gc", ("g_pre_mix_2", 8, 1, 1.0)),
                                          ("gf", ("g_pre_ffn_2", 32, 0, 1.0)), ("pm", ("g_post_mix_2", 16, 0, 0.0)),
                                          ("pf", ("g_post_ffn_2", 40, 0, 0.0))):
            o = O_MOD + 96 + 8 * MOD_DERIVED.index(name)
            dve.scalar_tensor_tensor(out=M[:, o:o + KD].rearrange("p (c o) -> p c o", o=1), in0=MOD[:, c:c + KD, which:which + 1],
                                     scalar=plus, in1=vec(v), op0=ALU.add, op1=ALU.mult)

    return Phase("adaptive", sync=sync, tensor=tensor, scalar=scalar, vector=vector)


def mod_col(k, c, which=0):
    o = O_MOD + 2 * c + which
    return k.M[:, o:o + 1]


def derived_col(k, name, c):
    o = O_MOD + 96 + 8 * MOD_DERIVED.index(name) + c
    return k.M[:, o:o + 1]


def diff_projection(k):
    t0 = k.plan
    k.plan += 6
    M = k.M
    A, C = view(M, A_A, KD, S), view(M, A_C, KD, NC_CTX)
    Q, K, V = view(M, D_Q, 4, S), view(M, D_K, 4, T_ALL), view(M, D_V, TT, 512)
    w = k.a["w_in_2"][0].rearrange("(c p) n -> p c n", p=P)
    read = k.sem("diff_read")
    halves = [("q", b) for b in range(4)] + [("k", b) for b in range(4)] + [("v", c, t) for c in range(2) for t in range(2)]
    tok = lambda t: (lambda q: C[:, q, t * P:(t + 1) * P]) if t < 2 else (lambda q: A[:, q, (t - 2) * P:(t - 1) * P])

    def sync(k, sp):
        load_columns(k, w, 1696, 3232)
        for s in k.phase_end.values():
            sp.wait_ge(s, k.phase_index["second_norms"] + 1)
        sp.dma_start(M[:, D_ROPE:D_ROPE + P + 2 * S], k.a["const_rope"]).then_inc(k.rope_in, 16)
        for n, name in enumerate(("lam_q1_2", "lam_k1_2", "lam_q2_2", "lam_k2_2")):
            sp.dma_start(view(M, D_LAM, 4, HEAD)[:, n, :], k.a[name].broadcast_to([P, HEAD])).then_inc(k.rope_in, 16)

    def tensor(k, pe):
        for h, half in enumerate(halves):
            if h % 2 == 0:
                wt = k.pe_stream.take(KD, 256)
            if h >= 4:
                pe.wait_ge(read, h - 3)
            two = [k.bank[2 * (h % 4)], k.bank[2 * (h % 4) + 1]]
            if half[0] == "v":
                for n in range(3):
                    dst = two[n // 2][:, (n % 2) * 256:(n % 2 + 1) * 256]
                    mm = block_token(pe, dst, tok(3 * half[2] + n), wt, KD)
            else:
                c0 = (half[1] % 2) * P
                if half[0] == "k":
                    block_feature(pe, two[1][:, :NC_CTX], wt, c0, P, lambda q: C[:, q, :], KD)
                mm = block_feature(pe, two[0], wt, c0, P, lambda q: A[:, q, :], KD)
            mm.then_inc(k.half_done, 1)

    def vector(k, dve):
        for h, half in enumerate(halves):
            dve.wait_ge(k.half_done, 2 * t0 + h + 1)
            o = 1024 * (h % 4)
            if half[0] == "q":
                ins = dve.tensor_scalar(Q[:, half[1], :], k.psum[:, o:o + S], HEAD ** -0.5, None, ALU.mult)
            elif half[0] == "k":
                dve.tensor_copy(K[:, half[1], NC_CTX:], k.psum[:, o:o + S])
                ins = dve.tensor_copy(K[:, half[1], :NC_CTX], k.psum[:, o + S:o + S + NC_CTX])
            else:
                _, c, t = half
                ins = dve.tensor_copy(V[:, 3 * t:3 * t + 3, c * 256:(c + 1) * 256],
                                      k.psum[:, o:o + 768].rearrange("p (a b) -> p a b", a=3))
            ins.then_inc(read, 1)

    return Phase("diff_projection", sync=sync, tensor=tensor, vector=vector)


def rope_phase(k):
    M = k.M
    Q, K = view(M, D_Q, 4, S), view(M, D_K, 4, T_ALL)
    rot, cos, sin = M[:, D_ROPE:D_ROPE + P], M[:, D_ROPE + P:D_ROPE + P + S], M[:, D_ROPE + P + S:D_ROPE + P + 2 * S]
    T = view(M, D_PT, 8, S)
    L = view(M, D_LAM, 4, HEAD)
    prod = view(M, D_P, 2, HEAD)
    lam = view(M, O_SML + 100, 4)
    turned, dots, exps = k.sem("rotated"), k.sem("lam_dots"), k.sem("lam_exps")
    blocks = [Q[:, n, :] for n in range(4)] + [K[:, n, NC_CTX:] for n in range(4)]
    k.lam = lam[:, 3:4]

    def tensor(k, pe):
        pe.wait_ge(k.rope_in, 16 * 5)
        for n, x in enumerate(blocks):
            pe.matmul(k.bank[n], rot, x, start=True, stop=True).then_inc(turned, 1)

    def vector(k, dve):
        dve.wait_ge(k.rope_in, 16 * 5)
        for n in range(2):
            k.dve.link(dve.tensor_tensor(prod[:, n, :], L[:, 2 * n, :], L[:, 2 * n + 1, :], ALU.mult))
        dve.tensor_reduce(lam[:, 0:2], prod, AX_X, ALU.add).then_inc(dots, 1)
        for n, x in enumerate(blocks):
            dve.wait_ge(turned, n + 1)
            k.dve.link(dve.tensor_tensor(T[:, n, :], k.bank[n], sin, ALU.mult))
            k.dve.link(dve.tensor_tensor(x, x, cos, ALU.mult))
            dve.tensor_tensor(x, x, T[:, n, :], ALU.add)
        dve.wait_ge(exps, 1)
        k.dve.link(dve.tensor_tensor(lam[:, 2:3], lam[:, 0:1], lam[:, 1:2], ALU.subtract))
        dve.tensor_scalar(lam[:, 3:4], lam[:, 2:3], LAM_INIT, None, ALU.add)

    def scalar(k, act):
        act.wait_ge(dots, 1)
        act.activation(lam[:, 0:2], lam[:, 0:2], ACT.Exp).then_inc(exps, 1)

    return Phase("rope", tensor=tensor, vector=vector, scalar=scalar)


def diff_attention(k):
    M = k.M
    Q, K, V = view(M, D_Q, 4, S), view(M, D_K, 4, T_ALL), view(M, D_V, TT, 512)
    MIX = view(M, A_MIX, KD, S)
    PT, PR = view(M, D_PT, 2, TT, S), view(M, D_P, 2, 2, T_ALL)
    small = view(M, O_SML, 2, 2, 2)
    units = [(h, i) for h in range(4) for i in range(4)]
    scored, maxed, raised, ready, turned, copied, valued, taken = (
        k.sem(f"diff_{x}") for x in ("scored", "maxed", "raised", "ready", "turned", "copied", "valued", "taken"))
    score = lambda m: k.psum[:, 1024 * m:1024 * m + T_ALL]
    TURN = 4

    def values(pe, h):
        pe.wait_ge(copied, 4 * h + 4)
        if h >= 2:
            pe.wait_ge(taken, h - 1)
        for j in range(TT):
            mm = pe.matmul(k.bank[6 + h % 2], V[:, j, h * P:(h + 1) * P], PT[:, h % 2, j, :], start=j == 0, stop=j == TT - 1)
        mm.then_inc(valued, 1)

    def tensor(k, pe):
        for u in range(len(units) + 1):
            if u < len(units):
                h, i = units[u]
                for m in range(2):
                    if u >= 1:
                        pe.wait_ge(raised, 2 * u - 1 + m)
                    r = slice(64 * m, 64 * m + 64)
                    pe.matmul(k.bank[2 * m], Q[r, h, i * P:(i + 1) * P], K[r, h, 0:512], start=True, stop=True)
                    pe.matmul(k.bank[2 * m + 1][:, :256], Q[r, h, i * P:(i + 1) * P], K[r, h, 512:768], start=True,
                              stop=True).then_inc(scored, 1)
            if u >= 1:
                v = u - 1
                h, i = units[v]
                pe.wait_ge(ready, v + 1)
                if v >= 1:
                    pe.wait_ge(copied, v)
                for j in range(TT):
                    mm = pe.transpose(k.bank[TURN + j // 4][:, (j % 4) * P:(j % 4 + 1) * P],
                                      PR[:, v % 2, 0, j * P:(j + 1) * P], k.ident)
                mm.then_inc(turned, 1)
                if i == 1 and h >= 1:
                    values(pe, h - 1)
        values(pe, 3)

    def vector(k, dve):
        for u in range(len(units) + 1):
            if u < len(units):
                for m in range(2):
                    dve.wait_ge(scored, 2 * u + m + 1)
                    k.dve.link(dve.tensor_reduce(small[:, u % 2, m, 0:1], score(m), AX_X, ALU.max))
                    dve.tensor_scalar(small[:, u % 2, m, 0:1], small[:, u % 2, m, 0:1], -1.0, None, ALU.mult).then_inc(maxed, 1)
            if u >= 1:
                v = u - 1
                h, i = units[v]
                sm, pr = small[:, v % 2], PR[:, v % 2]
                dve.wait_ge(raised, 2 * v + 2)
                k.dve.link(dve.reciprocal(sm[:, :, 1:2], sm[:, :, 1:2]))
                k.dve.link(dve.tensor_tensor(sm[:, 1, 1:2], sm[:, 1, 1:2], k.lam, ALU.mult))
                k.dve.link(dve.tensor_scalar(pr[:, 1, :], pr[:, 1, :], sm[:, 1, 1:2], None, ALU.mult))
                dve.scalar_tensor_tensor(out=pr[:, 0, :], in0=pr[:, 0, :], scalar=sm[:, 0, 1:2], in1=pr[:, 1, :],
                                         op0=ALU.mult, op1=ALU.subtract).then_inc(ready, 1)
                if i == 3 and h >= 1:
                    take(dve, h - 1)
        take(dve, 3)

    def take(dve, h):
        dve.wait_ge(valued, h + 1)
        dve.tensor_copy(MIX[:, 4 + h, :], k.bank[6 + h % 2]).then_inc(taken, 1)

    def scalar(k, act):
        for u in range(len(units) + 2):
            if u < len(units):
                if u >= 2:
                    act.wait_ge(turned, u - 1)
                for m in range(2):
                    act.wait_ge(maxed, 2 * u + m + 1)
                    act.activation(PR[:, u % 2, m, :], score(m), ACT.Exp, bias=small[:, u % 2, m, 0:1],
                                   accum_out=small[:, u % 2, m, 1:2]).then_inc(raised, 1)
            if u >= 1 and u - 1 < len(units):
                v = u - 1
                h, i = units[v]
                act.wait_ge(turned, v + 1)
                if h >= 2:
                    act.wait_ge(valued, h - 1)
                act.activation(PT[:, h % 2, :, i * P:(i + 1) * P],
                               k.psum[:, 512 * TURN:512 * TURN + T_ALL].rearrange("p (j q) -> p j q", q=P),
                               ACT.Copy).then_inc(copied, 1)

    return Phase("diff_attention", tensor=tensor, vector=vector, scalar=scalar)


def diff_post(k):
    M = k.M
    O = view(M, A_MIX, KD, S)[:, 4:8, :]
    SQ = view(M, D_PT, 4, S)
    squared, summed, inv, rooted = (k.sem(f"diffpost_{x}") for x in ("squared", "summed", "inverted", "rooted"))
    g = M[:, O_SML + 110:O_SML + 111]

    def scalar(k, act):
        act.activation(SQ, O, ACT.Square).then_inc(squared, 1)
        act.wait_ge(inv, 1)
        act.activation(SQ, SQ, ACT.Sqrt).then_inc(rooted, 1)

    def tensor(k, pe):
        pe.wait_ge(squared, 1)
        for n in range(4):
            mm = pe.matmul(k.bank[n], k.ones, SQ[:, n, :], start=True, stop=True)
        mm.then_inc(summed, 1)

    def vector(k, dve):
        dve.tensor_scalar(g, col(k, "subln_w_2"), 1.0 - LAM_INIT, None, ALU.mult)
        dve.wait_ge(summed, 1)
        k.dve.link(dve.tensor_scalar(SQ, k.psum[:, 0:4 * S].rearrange("p (a b) -> p a b", a=4), 1.0 / P, SUBLN_EPS,
                                     ALU.mult, ALU.add))
        dve.reciprocal(SQ, SQ).then_inc(inv, 1)
        dve.wait_ge(rooted, 1)
        dve.scalar_tensor_tensor(out=O, in0=O, scalar=g, in1=SQ, op0=ALU.mult, op1=ALU.mult)

    return Phase("diff_post", tensor=tensor, vector=vector, scalar=scalar)


def rwkv_projection(k):
    t0 = k.plan
    k.plan += 7
    M = k.M
    A, C = view(M, A_A, KD, S), view(M, A_C, KD, NC_CTX)
    RKV = view(M, R_R, 12, T_ALL)
    WA, GL = view(M, R_WA, T_ALL), view(M, R_GL, S)
    w = k.a["w_in_2"][0].rearrange("(c p) n -> p c n", p=P)
    free, centred = k.sem("rwkv_bank_free"), k.sem("rwkv_centred")

    def part(h):
        if h < 12:
            return RKV[:, h, :], [col(k, f"rwkv_tap{t}", h) for t in range(3)], P, (h % 2) * P
        name, m, c0, dst = (("rwkv_wa_taps", 64, 0, WA), ("rwkv_g_taps", 96, 64, GL))[h - 12]
        return dst[0:m, :], [col(k, name, t)[0:m, :] for t in range(3)], m, c0

    def segments(h):
        o = 1024 * (h % 4)
        return [(o, 0, S)] if h == 13 else [(o, NC_CTX, S), (o + S, 0, NC_CTX)]

    def sync(k, sp):
        load_columns(k, w, 0, 1536)
        load_columns(k, w, 1536, 1696)

    def tensor(k, pe):
        for h in range(14):
            if h % 2 == 0:
                wt = k.pe_stream.take(KD, 256 if h < 12 else 160)
            if h >= 4:
                pe.wait_ge(free, h - 3)
            _, _, m, c0 = part(h)
            two = [k.bank[2 * (h % 4)], k.bank[2 * (h % 4) + 1]]
            if h != 13:
                block_feature(pe, two[1][0:m, :NC_CTX], wt, c0, m, lambda q: C[:, q, :], KD)
            block_feature(pe, two[0][0:m, :], wt, c0, m, lambda q: A[:, q, :], KD).then_inc(k.half_done, 1)

    def scalar(k, act):
        for h in range(14):
            act.wait_ge(k.half_done, 2 * t0 + h + 1)
            dst, taps, m, _ = part(h)
            for o, d0, n in segments(h):
                ins = act.activation(dst[:, d0:d0 + n], k.psum[0:m, o:o + n], ACT.Copy, scale=taps[1])
            ins.then_inc(centred, 1)

    def vector(k, dve):
        for h in range(14):
            dve.wait_ge(centred, h + 1)
            dst, taps, m, _ = part(h)
            for n, (o, d0, cnt) in enumerate(segments(h)):
                x, y = k.psum[0:m, o:o + cnt], dst[:, d0:d0 + cnt]
                k.dve.link(dve.scalar_tensor_tensor(out=y[:, 1:cnt], in0=x[:, 0:cnt - 1], scalar=taps[0], in1=y[:, 1:cnt],
                                                    op0=ALU.mult, op1=ALU.add))
                ins = dve.scalar_tensor_tensor(out=y[:, 0:cnt - 1], in0=x[:, 1:cnt], scalar=taps[2], in1=y[:, 0:cnt - 1],
                                               op0=ALU.mult, op1=ALU.add)
            ins.then_inc(free, 1)

    return Phase("rwkv_projection", sync=sync, tensor=tensor, vector=vector, scalar=scalar)


def mask(k, name, off=0, n=None):
    o = R_MASK + MASKS[name] + off
    return k.M[:, o:o + n]


def rwkv_prepare(k):
    M = k.M
    K, KK = view(M, R_K, 4, T_ALL), view(M, R_KK, 4, T_ALL)
    WA = view(M, R_WA, T_ALL)
    SQ = view(M, R_ABD, 2, T_ALL)
    N = view(M, R_ABD + 2 * T_ALL, 2, T_ALL)
    scaled, squared, summed, rooted, floored = (k.sem(f"kk_{x}") for x in ("scaled", "squared", "summed", "rooted", "done"))

    def sync(k, sp):
        for s in k.phase_end.values():
            sp.wait_ge(s, k.phase_index["rwkv_projection"] + 1)
        sp.dma_start(M[:, R_MASK:R_MASK + N_MASK], k.a["const_rwkv"]).then_inc(k.rwkv_in, 16)
        for d, s in enumerate(("fwd", "bwd")):
            sp.dma_start(view(M, R_W2, 2, 512)[0:32, d, :], k.a[f"w2_{s}_2"][0]).then_inc(k.rwkv_in, 16)
            sp.dma_start(view(M, R_A2, 2, 512)[0:32, d, :], k.a[f"a2_{s}_2"][0]).then_inc(k.rwkv_in, 16)
        sp.dma_start(M[0:96, R_G2:R_G2 + 512], k.a["g2_2"][0]).then_inc(k.rwkv_in, 16)

    def scalar(k, act):
        for f in range(4):
            act.wait_ge(scaled, f + 1)
            if f >= 2:
                act.wait_ge(summed, f - 1)
            act.activation(SQ[:, f % 2, :], KK[:, f, :], ACT.Square).then_inc(squared, 1)
            if f >= 1:
                root(act, f - 1)
        root(act, 3)
        act.activation(WA[0:32, :], WA[0:32, :], ACT.Tanh)

    def root(act, f):
        act.wait_ge(summed, f + 1)
        if f >= 2:
            act.wait_ge(floored, f - 1)
        act.activation(N[:, f % 2, :], k.psum[:, 1024 * (f % 2):1024 * (f % 2) + T_ALL], ACT.Sqrt).then_inc(rooted, 1)

    def tensor(k, pe):
        pe.wait_ge(k.rwkv_in, 16 * 6)
        for f in range(4):
            pe.wait_ge(squared, f + 1)
            if f >= 2:
                pe.wait_ge(rooted, f - 1)
            b = k.bank[2 * (f % 2):2 * (f % 2) + 2]
            pe.matmul(b[0], mask(k, "headsum", 0, P), SQ[:, f % 2, 0:512], start=True, stop=True)
            pe.matmul(b[1][:, :256], mask(k, "headsum", 0, P), SQ[:, f % 2, 512:768], start=True, stop=True).then_inc(summed, 1)

    def vector(k, dve):
        dve.tensor_copy(M[0:32, R_AL:R_AL + T_ALL], WA[32:64, :])
        for f in range(4):
            dve.tensor_scalar(KK[:, f, :], K[:, f, :], col(k, "k_k_2", f), None, ALU.mult).then_inc(scaled, 1)
        for f in range(4):
            dve.wait_ge(rooted, f + 1)
            n = N[:, f % 2, :]
            k.dve.link(dve.tensor_scalar(n, n, 1e-12, None, ALU.max))
            k.dve.link(dve.reciprocal(n, n))
            dve.tensor_tensor(KK[:, f, :], KK[:, f, :], n, ALU.mult).then_inc(floored, 1)

    return Phase("rwkv_prepare", sync=sync, tensor=tensor, vector=vector, scalar=scalar)


LEVELS = 5
NCH_CTX = NC_CTX // CH
LINKS = 9
MAIN_ONLY = ("ydone", "yout", "rho")


def rwkv_loop(k):
    M = k.M
    v4 = lambda o, *d: view(M, o, *d)
    half = lambda ap, d: ap[:, 4 * d:4 * d + 4]
    src = {n: v4(o, 4, T_ALL) for n, o in (("R", R_R), ("K", R_K), ("V", R_V), ("KK", R_KK))}
    latent, factor = (v4(R_WA, T_ALL), v4(R_AL, T_ALL)), (v4(R_W2, 2, 512), v4(R_A2, 2, 512))
    SIG = v4(R_SIG, 2, NPAIR, CH)
    PRE, POST = v4(R_PRE, NPAIR, CH), SIG[:, 0]
    KD_, KKA = v4(R_KD, NPAIR, CH), v4(R_KD + 512, NPAIR, CH)
    TH = v4(O_SML + 120, NPAIR)
    PHN = v4(O_SML + 128, NPAIR)
    PH = v4(O_SML + 136, NPAIR)
    AR, B_ = v4(R_AR, NPAIR, 2, CH), v4(R_B, NPAIR, CH)
    ABD, BBD, KBD, VBD = (v4(o, NPAIR, 2, CH) for o in (R_ABD, R_BBD, R_KBD, R_VBD))
    ATK, BTK, KTK, VTK = (v4(o, NPAIR, P) for o in (R_ATK, R_BTK, R_KTK, R_VTK))
    QK, QB, LT, RHO = (v4(o, NPAIR, CH) for o in (R_QK, R_QB, R_LT, R_RHO))
    XY, T_ = v4(R_X, 2, NPAIR, P), v4(R_T, NPAIR, P)
    KTBD, LOFF = v4(R_KTBD, NPAIR, 2, CH), v4(R_LOFF, NPAIR, 2, CH)
    KV, ABAR, SA, ST, S0 = (v4(o, NPAIR, P) for o in (R_KV, R_ABAR, R_SA, R_S, R_S0))
    YF, YB = v4(A_MIX, KD, S), v4(R_YB, 4, S)
    flat = lambda ap: ap.rearrange("p a b -> p (a b)")
    bd = lambda ap, p: ap[:, p].rearrange("p a b -> p (a b)")
    wide = lambda ap: ap.unsqueeze(2)
    m3 = lambda name, d, w: k.M[:, R_MASK + MASKS[name] + d * w:R_MASK + MASKS[name] + (d + 1) * w]
    sems = {n: k.sem(f"rwkv_{n}") for n in (
        "latents", "shifted", "sigmoid", "summed", "exps", "bd_ab", "bd_k", "bd_v", "grams", "gram_l", "gram2", "lt", "xy0",
        "kq", "turned", "tcopied", "loff", "tdone", "tst", "xydone", "xy", "kvdone", "kvst", "abar", "abarst",
        "rho", "s0", "sadone", "sast", "sdone", "s", "ydone", "yout")}

    def parts(run):
        run(-1, None, 0, False, False, True)
        run(0, 3, 0, False, False, True)
        run(3, None, 0, False, True, True)
        run(4, 7, 0, True, True, True)
        run(11, None, 0, True, False, False)

    def step(n, i):
        def value(name, per, nth, ahead):
            return at(i, per, (n + ahead - (NCH_CTX if name in MAIN_ONLY else 0)) * per + nth)

        def wait(eng, name, per=1, nth=1, ahead=0):
            eng.wait_ge(sems[name], value(name, per, nth, ahead))

        def tokens(d):
            m = n + 1
            if d == 0:
                start = at(i, CH, m * CH)
            else:
                start = at(i, -CH, (NCH_CTX - 1 - m) * CH if m < NCH_CTX else T_ALL - CH - (m - NCH_CTX) * CH)
            return bass.ds(start, CH)

        def out_tokens(d):
            m = n - NCH_CTX
            return bass.ds(at(i, CH, m * CH) if d == 0 else at(i, -CH, S - CH - m * CH), CH)

        return wait, tokens, out_tokens

    def runner(eng, emit, chain=None):
        def run(n, trips, _, main, nxt_main, more):
            if trips is None:
                emit(n, None, main, nxt_main, more)
                return
            with eng.Fori(0, trips) as i:
                if chain:
                    chain.enter(i, LINKS)
                emit(n, i, main, nxt_main, more)
            if chain:
                chain.leave(trips)
        return run

    def tensor(k, pe):
        def emit(n, i, main, nxt_main, more):
            wait, tokens, out_tokens = step(n, i)
            n_ar = 2 if nxt_main else 1

            def latents():
                for which in range(2):
                    for d in range(2):
                        for f in range(4):
                            mm = pe.matmul(k.bank[which][:, (4 * d + f) * CH:(4 * d + f + 1) * CH],
                                           factor[which][0:32, d, f * P:(f + 1) * P], latent[which][0:32, tokens(d)], start=True, stop=True)
                mm.then_inc(sems["latents"], 1)

            def gram(what, banks):
                for p in range(NPAIR):
                    mm = pe.matmul(k.bank[banks[p // 4]][:, (p % 4) * P:(p % 4) * P + n_ar * CH], bd(what, p),
                                   AR[:, p, 0:n_ar, :].rearrange("p a b -> p (a b)"), start=True, stop=True)
                return mm

            def gram_l():
                for p in range(NPAIR):
                    mm = pe.matmul(k.bank[5][:, p * CH:(p + 1) * CH], bd(ABD, p), B_[:, p, :], start=True, stop=True)
                mm.then_inc(sems["gram_l"], 1)

            def turn(what):
                for p in range(NPAIR):
                    mm = pe.transpose(k.bank[p // 4][:, (p % 4) * P:(p % 4 + 1) * P], bd(what, p), k.ident)
                mm.then_inc(sems["turned"], 1)

            def product(banks, lhs, rhs, more_terms=()):
                terms = ((lhs, rhs),) + more_terms
                for p in range(NPAIR):
                    for t, (u, v) in enumerate(terms):
                        mm = pe.matmul(k.bank[banks[p // 4]][:, (p % 4) * P:(p % 4 + 1) * P], u(p), v(p),
                                       start=t == 0, stop=t == len(terms) - 1)
                return mm

            if n < 0:
                latents()
                wait(pe, "bd_ab", ahead=1)
                gram(BBD, (4, 6)).then_inc(sems["grams"], 1)
                gram_l()
                wait(pe, "bd_k", ahead=1)
                gram(KBD, (2, 3)).then_inc(sems["gram2"], 1)
                return
            wait(pe, "s", nth=1)
            wait(pe, "bd_v")
            turn(VBD)
            for lv in range(LEVELS):
                last = lv == LEVELS - 1
                for d in range(2):
                    if lv == 0 and d == 0:
                        wait(pe, "xy0")
                        wait(pe, "kq")
                    wait(pe, "loff", 2 * LEVELS, 2 * lv + d + 1)
                    if lv > 0:
                        wait(pe, "xy", 2 * LEVELS, 2 * (lv - 1) + d + 1)
                    for p in range(4 * d, 4 * d + 4):
                        mm = pe.matmul(k.bank[2 + d][:, (p % 4) * P:(p % 4 + 1) * P], bd(LOFF, p), XY[:, 0, p, :],
                                       start=True, stop=True)
                    mm.then_inc(sems["tdone"], 1)
                if lv == 0:
                    wait(pe, "tcopied", 4, 1)
                    if more:
                        latents()
                elif lv < 4:
                    if lv > 1:
                        wait(pe, "tcopied", 4, lv)
                    elif more:
                        wait(pe, "shifted", ahead=1)
                    turn((ABD, BBD, KBD)[lv - 1])
                else:
                    wait(pe, "tcopied", 4, 4)
                    product((0, 1), lambda p: bd(KTBD, p), lambda p: VTK[:, p, :]).then_inc(sems["kvdone"], 1)
                for d in range(2):
                    wait(pe, "tst", 2 * LEVELS, 2 * lv + d + 1)
                    if lv == 0 and d == 1 and main:
                        wait(pe, "yout", ahead=-1, nth=2)
                    for p in range(4 * d, 4 * d + 4):
                        o = (p % 4) * P
                        if not last:
                            pe.matmul(k.bank[4 + 2 * d][:, o:o + P], XY[:, 1, p, :], T_[:, p, :], start=True, stop=True)
                        mm = pe.matmul(k.bank[5 + 2 * d][:, o:o + P], T_[:, p, :], XY[:, 1, p, :], start=True, stop=True)
                    mm.then_inc(sems["xydone"], 1)
            if more:
                wait(pe, "bd_ab", ahead=1)
                gram(BBD, (4, 6)).then_inc(sems["grams"], 1)
            wait(pe, "xy", 2 * LEVELS, 2 * LEVELS)
            product((2, 3), lambda p: ATK[:, p, :], lambda p: XY[:, 1, p, :]).then_inc(sems["abar"], 1)
            if more:
                gram_l()
            wait(pe, "s0")
            wait(pe, "kvst")
            wait(pe, "abarst")
            product((0, 1), lambda p: XY[:, 1, p, :], lambda p: KV[:, p, :],
                    ((lambda p: ABAR[:, p, :], lambda p: S0[:, p, :]),)).then_inc(sems["sadone"], 1)
            if more:
                wait(pe, "bd_k", ahead=1)
                gram(KBD, (2, 3)).then_inc(sems["gram2"], 1)
            wait(pe, "sast")
            product((0, 1), lambda p: KTK[:, p, :], lambda p: VTK[:, p, :],
                    ((lambda p: BTK[:, p, :], lambda p: SA[:, p, :]),)).then_inc(sems["sdone"], 1)
            if main:
                wait(pe, "rho")
                for p in range(NPAIR):
                    o = k.bank[7][:, p * CH:(p + 1) * CH]
                    pe.matmul(o, S0[:, p, :], RHO[:, p, :], start=True, stop=False)
                    pe.matmul(o, VTK[:, p, :], QK[:, p, :], start=False, stop=False)
                    mm = pe.matmul(o, SA[:, p, :], QB[:, p, :], start=False, stop=True)
                mm.then_inc(sems["ydone"], 1)

        parts(runner(pe, emit))

    def scalar(k, act):
        act.sem_inc(sems["yout"], 1)

        def emit(n, i, main, nxt_main, more):
            wait, tokens, out_tokens = step(n, i)

            def rates():
                wait(act, "shifted", ahead=1)
                act.activation(SIG, SIG, ACT.Sigmoid).then_inc(sems["sigmoid"], 1)

            def exps():
                wait(act, "summed", ahead=1)
                if main:
                    wait(act, "rho")
                for dst, fwd, bwd in ((AR[:, :, 0, :], (1, 1), (0, -1)), (B_, (0, -1), (1, 1)), (AR[:, :, 1, :], (0, 1), (1, -1))):
                    if dst is not B_ and fwd[0] == 0 and not nxt_main:
                        continue
                    for d, (g, sign) in enumerate((fwd, bwd)):
                        act.activation(half(dst, d), half((PRE, POST)[g], d), ACT.Exp, scale=sign * DECAY)
                act.activation(PHN, TH, ACT.Exp, scale=DECAY).then_inc(sems["exps"], 1)

            def copied(m, dst, scale):
                wait(act, "turned", 4, m + 1)
                ins = act.activation(dst.rearrange("p a b -> p (a b)"), k.psum[:, 0:1024], ACT.Copy, scale=scale)
                ins.then_inc(sems["tcopied"], 1)

            if n < 0:
                rates()
                exps()
            else:
                copied(0, VTK, 1.0)
                for lv in range(LEVELS):
                    for d in range(2):
                        wait(act, "tdone", 2 * LEVELS, 2 * lv + d + 1)
                        act.activation(half(T_, d), k.bank[2 + d].rearrange("p (a b) -> p a b", a=4), ACT.Copy).then_inc(sems["tst"], 1)
                    if 1 <= lv < 4:
                        copied(lv, (ATK, BTK, KTK)[lv - 1], -1.0 if lv == 2 else 1.0)
                    if lv == 0 and main:
                        act.activation(RHO, AR[:, :, 1, :], ACT.Copy).then_inc(sems["rho"], 1)
                    if lv == 1 and more:
                        rates()
                    if lv == 2 and more:
                        exps()
                    if lv == 4:
                        wait(act, "kvdone")
                        act.activation(flat(KV), k.psum[:, 0:1024], ACT.Copy).then_inc(sems["kvst"], 1)
                wait(act, "abar")
                act.activation(flat(ABAR), k.psum[:, 1024:2048], ACT.Copy).then_inc(sems["abarst"], 1)
                if more:
                    wait(act, "bd_k", ahead=1)
                wait(act, "sadone")
                act.activation(flat(SA), k.psum[:, 0:1024], ACT.Copy).then_inc(sems["sast"], 1)
            if main:
                wait(act, "ydone")
                for d, Y in enumerate((YF, YB)):
                    ins = act.activation(Y[:, 0:4, out_tokens(d)],
                                         k.bank[7][:, 256 * d:256 * d + 256].rearrange("p (a b) -> p a b", a=4), ACT.Copy)
                ins.then_inc(sems["yout"], 1)

        parts(runner(act, emit))

    def vector(k, dve):
        dve.memset(ST, 0.0).then_inc(sems["s"], 1)

        def emit(n, i, main, nxt_main, more):
            wait, tokens, out_tokens = step(n, i)
            head = m3("head", 0, 2).unsqueeze(1).unsqueeze(3)
            full, hfull = [P, NPAIR, 2, CH], [P, 4, 2, CH]
            gram = lambda b, w: k.psum[:, 512 * b:512 * b + 512].rearrange("p (a w t) -> p a w t", a=4, w=2)[:, :, w, :]
            row = lambda name, d: m3(name, d, CH).unsqueeze(1).broadcast_to([P, 4, CH])

            def shift():
                offs = M[:, O_VEC + VCOL["w0_fwd_2"]:O_VEC + VCOL["w0_fwd_2"] + 16].rearrange("p (d w f o) -> p w d f o", d=2, w=2, o=1)
                wait(dve, "latents", ahead=1)
                for w in range(2):
                    for d in range(2):
                        ins = dve.tensor_tensor(half(SIG[:, w], d), k.bank[w][:, 256 * d:256 * d + 256].rearrange("p (a b) -> p a b", a=4),
                                                offs[:, w, d].broadcast_to([P, 4, CH]), ALU.add)
                ins.then_inc(sems["shifted"], 1)

            def cumulate():
                wait(dve, "sigmoid", ahead=1)
                k.dve.link(dve.tensor_tensor_scan(flat(PRE), mask(k, "reset", 0, 512), flat(POST), 0.0, ALU.mult, ALU.add))
                k.dve.link(dve.tensor_scalar(TH.unsqueeze(2), PRE[:, :, CH - 1:CH], 0.5, None, ALU.mult))
                k.dve.link(dve.tensor_tensor(PRE, PRE, TH.unsqueeze(2).broadcast_to([P, NPAIR, CH]), ALU.subtract))
                dve.tensor_tensor(POST, PRE, POST, ALU.subtract).then_inc(sems["summed"], 1)

            def rated():
                ka = M[:, O_VEC + VCOL["k_a_2"]:O_VEC + VCOL["k_a_2"] + 4].unsqueeze(2).broadcast_to([P, 4, CH])
                for d in range(2):
                    dve.tensor_tensor(half(KKA, d), src["KK"][:, :, tokens(d)], half(SIG[:, 1], d), ALU.mult)
                    ins = dve.scalar_tensor_tensor(out=half(KD_, d), in0=half(SIG[:, 1], d), scalar=-1.0, in1=ka, op0=ALU.add, op1=ALU.mult)
                k.dve.link(ins)
                for d in range(2):
                    ins = dve.scalar_tensor_tensor(out=half(KD_, d), in0=half(KD_, d), scalar=1.0, in1=src["K"][:, :, tokens(d)],
                                                   op0=ALU.add, op1=ALU.mult)
                k.dve.link(ins)

            def alpha_beta():
                wait(dve, "exps", ahead=1)
                for d in range(2):
                    dve.tensor_tensor(half(AR, d)[:, :, 0, :], half(AR, d)[:, :, 0, :], src["KK"][:, :, tokens(d)], ALU.mult)
                    if nxt_main:
                        dve.tensor_tensor(half(AR, d)[:, :, 1, :], half(AR, d)[:, :, 1, :], src["R"][:, :, tokens(d)], ALU.mult)
                dve.tensor_tensor(KD_, KD_, B_, ALU.mult)
                k.dve.link(dve.tensor_tensor(B_, KKA, B_, ALU.mult))

            def diagonal_ab():
                if n >= 0:
                    wait(dve, "turned", 4, 4)
                dve.tensor_tensor(ABD, AR[:, :, 0:1, :].broadcast_to(full), head.broadcast_to(full), ALU.mult)
                dve.tensor_tensor(BBD, wide(B_).broadcast_to(full), head.broadcast_to(full), ALU.mult).then_inc(sems["bd_ab"], 1)

            def diagonal_k():
                dve.tensor_tensor(KBD, wide(KD_).broadcast_to(full), head.broadcast_to(full), ALU.mult).then_inc(sems["bd_k"], 1)

            def next_xy():
                wait(dve, "grams", ahead=1)
                if n >= 0:
                    wait(dve, "loff", 2 * LEVELS, 2 * LEVELS)
                for d in range(2):
                    ins = dve.tensor_copy(half(LT, d), gram(4 + 2 * d, 0))
                ins.then_inc(sems["lt"], 1)
                blocks = lambda name, d: m3(name, d, P).rearrange("p (h t) -> p h t", h=2).unsqueeze(1).broadcast_to(hfull)
                as_heads = lambda w, d: half(XY[:, w], d).rearrange("p a (h t) -> p a h t", h=2)
                wait(dve, "gram_l", ahead=1)
                for d in range(2):
                    dve.tensor_tensor(as_heads(0, d), wide(k.bank[5][:, 256 * d:256 * d + 256].rearrange("p (a b) -> p a b", a=4)).broadcast_to(hfull),
                                      blocks("x1", d), ALU.mult)
                if n >= 0:
                    wait(dve, "sadone")
                for d in range(2):
                    ins = dve.tensor_tensor(as_heads(1, d), gram(4 + 2 * d, 0).unsqueeze(2).broadcast_to(hfull), blocks("y1", d), ALU.mult)
                k.dve.link(ins)
                both = XY.rearrange("p w a t -> p (w a) t")
                dve.tensor_tensor(both, both, k.ident.unsqueeze(1).broadcast_to([P, 2 * NPAIR, P]), ALU.add).then_inc(sems["xy0"], 1)

            def next_kq():
                wait(dve, "gram2", ahead=1)
                for d in range(2):
                    st = m3("strict", d, P).rearrange("p (h t) -> p h t", h=2).unsqueeze(1).broadcast_to(hfull)
                    ins = dve.tensor_tensor(half(KTBD, d), gram(2 + d, 0).unsqueeze(2).broadcast_to(hfull), st, ALU.mult)
                if main:
                    wait(dve, "ydone")
                if nxt_main:
                    for d in range(2):
                        dve.tensor_tensor(half(QB, d), gram(4 + 2 * d, 1), row("neg", d), ALU.mult)
                        ins = dve.tensor_tensor(half(QK, d), gram(2 + d, 1), row("incl", d), ALU.mult)
                ins.then_inc(sems["kq"], 1)

            def state():
                wait(dve, "sdone")
                k.dve.link(dve.tensor_tensor(flat(ST), flat(S0), k.psum[:, 0:1024], ALU.add))
                dve.tensor_tensor(ST, ST, PH.unsqueeze(2).broadcast_to([P, NPAIR, P]), ALU.mult).then_inc(sems["s"], 1)

            if n < 0:
                for part in (shift, cumulate, rated, alpha_beta, diagonal_ab, diagonal_k, next_xy, next_kq):
                    part()
                return
            wait(dve, "exps")
            wait(dve, "s")
            k.dve.link(dve.tensor_copy(PH, PHN))
            beside = {0: (shift,), 1: (cumulate, rated), 2: (alpha_beta,), 3: (diagonal_ab,), 4: (diagonal_k,)}
            for lv in range(LEVELS):
                for d in range(2):
                    wait(dve, "xydone", 2 * LEVELS, 2 * lv + d + 1)
                    w = 0 if lv < LEVELS - 1 else 1
                    xy = XY[:, w:, 4 * d:4 * d + 4, :]
                    new = k.psum[:, (4 + 2 * d + w) * 512:(6 + 2 * d) * 512].rearrange("p (w a t) -> p w a t", w=2 - w, a=4)
                    dve.tensor_tensor(xy, xy, new, ALU.subtract).then_inc(sems["xy"], 1)
                if lv == LEVELS - 1:
                    dve.tensor_tensor(S0, ST, PH.unsqueeze(2).broadcast_to([P, NPAIR, P]), ALU.mult).then_inc(sems["s0"], 1)
                for part in beside[lv] if more else ():
                    part()
            if more:
                next_xy()
            state()
            if more:
                next_kq()

        parts(runner(dve, emit, k.dve))

    def pool(k, pool):
        def emit(n, i, main, nxt_main, more):
            wait, tokens, out_tokens = step(n, i)
            hfull = [P, 4, 2, CH]
            head = m3("head", 0, 2).unsqueeze(1).unsqueeze(3).broadcast_to(hfull)

            def loff(lv, d):
                m = m3("level", 2 * lv + d, P).rearrange("p (h t) -> p h t", h=2).unsqueeze(1).broadcast_to(hfull)
                pool.tensor_tensor(half(LOFF, d), wide(half(LT, d)).broadcast_to(hfull), m, ALU.mult).then_inc(sems["loff"], 1)

            def diagonal_v():
                if n >= 0:
                    wait(pool, "turned", 4, 1)
                for d in range(2):
                    ins = pool.tensor_tensor(half(VBD, d), wide(src["V"][:, :, tokens(d)]).broadcast_to(hfull), head, ALU.mult)
                ins.then_inc(sems["bd_v"], 1)

            if n >= 0:
                for lv in range(LEVELS):
                    for d in range(2):
                        if lv > 0:
                            wait(pool, "tdone", 2 * LEVELS, 2 * (lv - 1) + d + 1)
                            loff(lv, d)
                if more:
                    diagonal_v()
            else:
                diagonal_v()
            if more:
                wait(pool, "lt", ahead=1)
                for d in range(2):
                    loff(0, d)

        parts(runner(pool, emit))

    return Phase("rwkv_loop", tensor=tensor, vector=vector, scalar=scalar, pool=pool)


def rwkv_output(k):
    M = k.M
    R, K, V = view(M, R_R, 4, T_ALL), view(M, R_K, 4, T_ALL), view(M, R_V, 4, T_ALL)
    AL, GL, A2 = view(M, R_AL, T_ALL), view(M, R_GL, S), view(M, R_A2, 2, 512)
    Y, YB = view(M, A_MIX, 4, S), view(M, R_YB, 4, S)
    SQ, AF, AB, T = view(M, A_A, 4, S), view(M, A_A + 2048, 4, S), view(M, A_A + 4096, 4, S), view(M, A_A + 6144, 4, S)
    G2 = M[0:96, R_G2:R_G2 + 512]
    lo, hi = k.psum[:, 0:2048].rearrange("p (a b) -> p a b", a=4), k.psum[:, 2048:4096].rearrange("p (a b) -> p a b", a=4)
    a, b = k.sem("rwkv_out_product"), k.sem("rwkv_out_vector")
    c = k.sem("rwkv_out_scalar")
    cc = lambda name, f: col(k, name, f)

    def tensor(k, pe):
        headsum = mask(k, "headsum", 0, P)

        def each(base, lhsT, rhs):
            for f in range(4):
                mm = pe.matmul(k.bank[base + f], lhsT(f), rhs(f), start=True, stop=True)
            mm.then_inc(a, 1)

        each(4, lambda f: A2[0:32, 0, f * P:(f + 1) * P], lambda f: AL[0:32, NC_CTX:])
        pe.wait_ge(b, 1)
        each(0, lambda f: headsum, lambda f: Y[:, f, :])
        pe.wait_ge(c, 1)
        each(4, lambda f: A2[0:32, 1, f * P:(f + 1) * P], lambda f: AL[0:32, NC_CTX:])
        pe.wait_ge(b, 2)
        pe.wait_ge(c, 3)
        each(0, lambda f: headsum, lambda f: SQ[:, f, :])
        pe.wait_ge(b, 3)
        each(4, lambda f: headsum, lambda f: T[:, f, :])
        pe.wait_ge(b, 4)
        pe.wait_ge(c, 4)
        each(0, lambda f: G2[:, f * P:(f + 1) * P], lambda f: GL[0:96, :])

    def scalar(k, act):
        def rate(dst, name):
            for f in range(4):
                ins = act.activation(dst[:, f, :], k.bank[4 + f], ACT.Sigmoid, bias=cc(name, f))
            ins.then_inc(c, 1)

        act.wait_ge(a, 1)
        rate(AF, "a0_fwd_2")
        act.wait_ge(a, 3)
        rate(AB, "a0_bwd_2")
        act.wait_ge(b, 2)
        act.activation(SQ, Y, ACT.Square).then_inc(c, 1)
        act.activation(GL[0:96, :], GL[0:96, :], ACT.Sigmoid).then_inc(c, 1)
        act.wait_ge(b, 5)
        act.activation(SQ, SQ, ACT.Sqrt).then_inc(c, 1)

    def vector(k, dve):
        dve.tensor_tensor(Y, Y, YB, ALU.add).then_inc(b, 1)
        dve.wait_ge(b, 1)
        dve.wait_ge(a, 2)
        dve.scalar_tensor_tensor(out=Y, in0=lo, scalar=-1.0 / HEAD, in1=Y, op0=ALU.mult, op1=ALU.add).then_inc(b, 1)
        dve.wait_ge(c, 2)
        k.dve.link(dve.tensor_tensor(AF, AF, AB, ALU.add))
        k.dve.link(dve.tensor_scalar(AF, AF, 0.5, -1.0, ALU.mult, ALU.add))
        for f in range(4):
            ins = dve.tensor_scalar(AF[:, f, :], AF[:, f, :], cc("k_a_2", f), 1.0, ALU.mult, ALU.add)
        k.dve.link(ins)
        k.dve.link(dve.tensor_tensor(AF, AF, K[:, :, NC_CTX:], ALU.mult))
        for f in range(4):
            ins = dve.scalar_tensor_tensor(out=T[:, f, :], in0=R[:, f, NC_CTX:], scalar=cc("r_k_2", f), in1=AF[:, f, :],
                                           op0=ALU.mult, op1=ALU.mult)
        ins.then_inc(b, 1)
        dve.wait_ge(a, 4)
        dve.tensor_scalar(SQ, lo, 1.0 / HEAD, LN_X_EPS, ALU.mult, ALU.add).then_inc(b, 1)
        dve.wait_ge(b, 4)
        dve.reciprocal(SQ, SQ).then_inc(b, 1)
        dve.wait_ge(a, 5)
        k.dve.link(dve.tensor_tensor(AB, hi, V[:, :, NC_CTX:], ALU.mult))
        dve.wait_ge(c, 5)
        for f in range(4):
            ins = dve.scalar_tensor_tensor(out=Y[:, f, :], in0=Y[:, f, :], scalar=cc("ln_x_w_2", f), in1=SQ[:, f, :],
                                           op0=ALU.mult, op1=ALU.mult)
        k.dve.link(ins)
        for f in range(4):
            ins = dve.scalar_tensor_tensor(out=Y[:, f, :], in0=Y[:, f, :], scalar=cc("ln_x_b_2", f), in1=AB[:, f, :],
                                           op0=ALU.add, op1=ALU.add)
        k.dve.link(ins)
        dve.wait_ge(a, 6)
        dve.tensor_tensor(Y, Y, lo, ALU.mult)

    def sync(k, sp):
        for s in k.phase_end.values():
            sp.wait_ge(s, k.phase_index["rwkv_output"] + 1)

    return Phase("rwkv_output", tensor=tensor, vector=vector, scalar=scalar, sync=sync)


def second_block_phases(k, stop):
    M = k.M
    k.rope_in, k.rwkv_in = k.sem("rope_in"), k.sem("rwkv_in")
    A, C, Y = view(M, A_A, KD, S), view(M, A_C, KD, NC_CTX), view(M, A_Y, KD, S)
    ph = [adaptive_phase(k)]
    pre = make_norm(k, "second_norm", k.H, S, [(lambda c: derived_col(k, "gx", c), A, lambda c: mod_col(k, c))], A_SCR)
    cn = make_norm(k, "ctx_norm", k.ctxT, NC_CTX, [(lambda c: derived_col(k, "gc", c), C, lambda c: mod_col(k, c, 1))], A_TMP)
    ph.append(norm_phase(k, "second_norms", [pre, cn]))
    ph += [diff_projection(k), rope_phase(k), diff_attention(k), diff_post(k)]
    ph += [rwkv_projection(k), rwkv_prepare(k), rwkv_loop(k), rwkv_output(k)]
    if stop == "mix2":
        return ph
    ph.append(output_projection(k, "output_projection2", k.a["w_out_2"][0]))
    gate = lambda name, c0: (lambda c: derived_col(k, name, c))
    post = make_norm(k, "mix_post2", Y, S, [], A_SCR)
    pre = make_norm(k, "ffn_pre2", k.H, S, [(lambda c: derived_col(k, "gf", c), A, lambda c: mod_col(k, 24 + c))], A_HID, after=post)
    ph.append(norm_phase(k, "ffn_norm2", [pre], post=(post, lambda c: derived_col(k, "pm", c))))
    if stop == "hmix2":
        return ph
    conv = [{"tap0": VCOL["ffn_tap0"] + off, "tap1": VCOL["ffn_tap1"] + off, "tap2": VCOL["ffn_tap2"] + off,
             "bias": VCOL["ffn_conv_b_2"] + off} for off in (0, KF)]
    w = k.a["w_up_2"][0]
    ph.append(ffn_up(k, "ffn_up2", w, w, 0, D_FF, A_TMP, conv))
    ph.append(ffn_down(k, "ffn_down2", k.a["w_down_2"][0]))
    post = make_norm(k, "ffn_post2", Y, S, [], A_SCR)
    ph.append(norm_phase(k, "layer_norm2", [], post=(post, lambda c: derived_col(k, "pf", c))))
    return ph


def final_phase(k, out):
    X = view(k.M, A_A, 4, D)
    turned, copied = k.sem("out_turned"), k.sem("out_copied")
    o = out[0].rearrange("(t p) d -> t p d", p=P)

    def tensor(k, pe):
        for n in range(8):
            if n >= 4:
                pe.wait_ge(copied, n - 3)
            for j in range(4):
                f = (n % 2) * 4 + j
                mm = pe.transpose(k.bank[n % 4][:, j * P:(j + 1) * P], k.H[:, f, (n // 2) * P:(n // 2 + 1) * P], k.ident)
            mm.then_inc(turned, 1)

    def vector(k, dve):
        for n in range(8):
            dve.wait_ge(turned, n + 1)
            dve.tensor_copy(X[:, n // 2, (n % 2) * 512:(n % 2 + 1) * 512], k.bank[n % 4][:, :]).then_inc(copied, 1)

    def sync(k, sp):
        for t in range(4):
            sp.wait_ge(copied, 2 * t + 2)
            sp.dma_start(o[t], X[:, t, :]).then_inc(k.out_sent, 16)
        sp.wait_ge(k.out_sent, 64)

    return Phase("final", sync=sync, tensor=tensor, vector=vector)


_INS = ['x', 'mem', 'ln_mix_pre', 'ln_mix_post', 'ln_ffn_pre', 'ln_ffn_post', 'ln_mem', 'w_mem_kv', 'w_out',
        'w_ffn_gate', 'w_ffn_up', 'w_ffn_down', 'w_in_a', 'w_spatial', 'b_spatial', 'ln_v_g', 'ln_v_b', 'ln_shared',
        'w_shared_kv', 'b_forget', 'w_in_b', 'c_2', 'ctx_2', 'c_ctx_2', 'w_mod_2', 'b_mod_2', 'g_pre_mix_2',
        'g_post_mix_2', 'g_pre_ffn_2', 'g_post_ffn_2', 'w_in_2', 'rwkv_conv_2', 'w0_fwd_2', 'w2_fwd_2', 'a0_fwd_2',
        'a2_fwd_2', 'w0_bwd_2', 'w2_bwd_2', 'a0_bwd_2', 'a2_bwd_2', 'g2_2', 'k_k_2', 'k_a_2', 'r_k_2', 'ln_x_w_2',
        'ln_x_b_2', 'lam_q1_2', 'lam_k1_2', 'lam_q2_2', 'lam_k2_2', 'subln_w_2', 'w_out_2', 'w_up_2', 'ffn_conv_2',
        'ffn_conv_b_2', 'w_down_2']


def shape_constants():
    p = np.arange(P)
    ident = np.eye(P, dtype=np.float32)
    ones = np.ones((P, P), np.float32)
    causal = np.where(p[None, :] <= p[:, None], 0.0, NEG).astype(np.float32)
    lower = (p[None, :] >= p[:, None]).astype(np.float32)
    inv = (np.float32(10000.0) ** (-np.arange(16, dtype=np.float32) / np.float32(16))).astype(np.float32)
    t = np.arange(S)
    ang = np.concatenate([(t // 64).astype(np.float32)[:, None] * inv, (t % 64).astype(np.float32)[:, None] * inv], 1)
    table = ang.T[p % 32].astype(np.float32)
    rot = np.zeros((P, P), np.float32)
    for m in range(P):
        if m % 64 < 32:
            rot[m + 32, m] = -1.0
        else:
            rot[m - 32, m] = 1.0
    a, hd = p % CH, p // CH
    b = np.arange(CH)
    same2 = a[:, None] // 2 == b[None, :] // 2
    later = [b[None, :] > a[:, None], b[None, :] < a[:, None]]
    earlier = [b[None, :] < a[:, None], b[None, :] > a[:, None]]
    eye = a[:, None] == b[None, :]
    head = hd[:, None] == np.arange(2)[None, :]
    spread = lambda m: (head[:, :, None] & m[:, None, :]).reshape(P, P)
    levels = []
    for lv in range(LEVELS):
        size = 4 << lv
        for d in range(2):
            same = (a[:, None] // size == b[None, :] // size) & (a[:, None] // (size // 2) != b[None, :] // (size // 2))
            levels.append(spread(same & later[d]))
    parts = {"head": head, "x1": np.concatenate([-1.0 * spread(same2 & earlier[d]) for d in range(2)], 1),
             "y1": np.concatenate([-1.0 * spread(same2 & later[d]) for d in range(2)], 1),
             "incl": np.concatenate([later[d] | eye for d in range(2)], 1),
             "neg": np.concatenate([-1.0 * (later[d] | eye) for d in range(2)], 1),
             "strict": np.concatenate([spread(later[d]) for d in range(2)], 1), "level": np.concatenate(levels, 1),
             "reset": np.tile((np.arange(512) % CH != 0)[None, :], (P, 1)), "headsum": hd[:, None] == hd[None, :]}
    rwkv = np.concatenate([parts[n].astype(np.float32) for n in MASKS], 1)
    return {"const_base": np.concatenate([ident, ones, causal, lower], 1),
            "const_rope": np.concatenate([rot, np.cos(table), np.sin(table)], 1), "const_rwkv": rwkv}


def kernel(**inputs):
    import concourse.bacc as _bacc
    from concourse.bass_utils import run_bass_kernel_spmd as _run

    nc = _bacc.Bacc("TRN2", target_bir_lowering=False, num_devices=1)
    arrays, aps = {}, {}
    for name, a in list((n, inputs[n]) for n in _INS) + list(shape_constants().items()):
        a = np.ascontiguousarray(a)
        arrays[f"in_{name}_dram"] = a
        aps[name] = nc.dram_tensor(f"in_{name}_dram", a.shape, mybir.dt.from_np(a.dtype), kind="ExternalInput").ap()
    out = nc.dram_tensor("out_0_dram", (1, S, D), F32, kind="ExternalOutput").ap()
    build(nc, aps, out)
    r = _run(nc, [arrays], core_ids=[0])
    return r.results[0]["out_0_dram"]
```

```python
from contextlib import ExitStack

import numpy as np

import concourse.bass as bass
from concourse import mybir

F32 = mybir.dt.float32
ALU = mybir.AluOpType
ACT = mybir.ActivationFunctionType
AX_X = mybir.AxisListType.X

P = 128
D = 1024
KD = D // P
S = 512
NM = 256
NC_CTX = 256
D_FF = 2816
KF = D_FF // P
MAIN = 768
HEAD = 64
RMS_EPS = 1e-6
LN_EPS = 1e-5
SUBLN_EPS = 1e-5
NEG = -1e30
SLOTS = 4
SLOT_WORDS = 2048

O_H = 0
O_RING = O_H + KD * S
O_MEM = O_RING + SLOTS * SLOT_WORDS
O_CTX = O_MEM + KD * NM
O_VEC = O_CTX + KD * NC_CTX
O_CST = O_VEC + 512
O_MOD = O_CST + 512
O_SML = O_MOD + 256
O_ARENA = O_SML + 256
WORDS = 53100

ROWS = [
    [("ln_mix_pre", 16), ("ln_mix_post", 16), ("ln_ffn_pre", 16), ("ln_ffn_post", 16), ("ln_mem", 16),
     ("ln_shared", 8), ("c_2", 8), ("c_ctx_2", 8), ("g_pre_mix_2", 8), ("g_post_mix_2", 8), ("g_pre_ffn_2", 8)],
    [("g_post_ffn_2", 8), ("b_mod_2", 48), ("w0_fwd_2", 4), ("a0_fwd_2", 4), ("w0_bwd_2", 4), ("a0_bwd_2", 4),
     ("k_k_2", 4), ("k_a_2", 4), ("r_k_2", 4), ("ln_x_w_2", 4), ("ln_x_b_2", 4),
     ("rwkv_tap0", 12), ("rwkv_tap1", 12), ("rwkv_tap2", 12)],
    [("ffn_tap0", 44), ("ffn_tap1", 44)],
    [("ffn_tap2", 44), ("ffn_conv_b_2", 44), ("subln_w_2", 1), ("rwkv_wa_taps", 3), ("rwkv_g_taps", 3)],
]
VCOL = {}
for _t, _rows in enumerate(ROWS):
    _r = 0
    for _name, _n in _rows:
        VCOL[_name] = _t * P + _r
        _r += _n


class Chain:

    def __init__(self, eng, sem):
        self.eng, self.sem, self.count, self.per, self.i, self.k = eng, sem, 0, 0, None, 0

    def link(self, ins):
        ins.then_inc(self.sem, 1)
        if self.i is None:
            self.count += 1
            self.eng.wait_ge(self.sem, self.count)
        else:
            self.k += 1
            self.eng.wait_ge(self.sem, self.i * self.per + (self.count + self.k))

    def enter(self, i, per):
        self.i, self.per, self.k = i, per, 0

    def leave(self, trips):
        assert self.k == self.per, (self.k, self.per)
        self.count += trips * self.per
        self.i = None


class Stream:

    def __init__(self, k, eng):
        self.k, self.eng, self.n, self.i, self.per = k, eng, 0, None, 0

    def enter(self, i, per):
        assert per % SLOTS == 0
        self.i, self.per, self.start = i, per, self.n

    def leave(self, trips):
        assert self.n - self.start == self.per
        self.n = self.start + trips * self.per
        self.i = None

    def load(self, src, kc, cols):
        n, e = self.n, self.eng
        if n >= SLOTS:
            need = 2 * (n - SLOTS + 1)
            e.wait_ge(self.k.half_done, need if self.i is None else self.i * (2 * self.per) + need)
        e.dma_start(self.k.slot(n % SLOTS, kc, cols), src).then_inc(self.k.tile_landed[n % SLOTS], 16)
        self.n += 1

    def take(self, kc, cols):
        n = self.n
        need = 16 * (n // SLOTS + 1)
        if self.i is not None:
            need = self.i * (16 * (self.per // SLOTS)) + need
        self.eng.wait_ge(self.k.tile_landed[n % SLOTS], need)
        self.n += 1
        return self.k.slot(n % SLOTS, kc, cols)


class Kit:
    pass


def view(M, off, *dims):
    n = int(np.prod(dims))
    v = M[:, off:off + n]
    if len(dims) == 1:
        return v
    names = "abcde"[:len(dims)]
    return v.rearrange("p (" + " ".join(names) + ") -> p " + " ".join(names),
                       **{c: d for c, d in zip(names[1:], dims[1:])})


def col(k, name, j=0):
    c = O_VEC + VCOL[name] + j
    return k.M[:, c:c + 1]


A_XTOK = O_ARENA
A_MTOK = A_XTOK + 4 * D
A_CTOK = A_MTOK + 2 * D
A_ROWS = A_CTOK + 2 * D


def turns(k):
    M = k.M
    x, m, c, r = view(M, A_XTOK, 4, D), view(M, A_MTOK, 2, D), view(M, A_CTOK, 2, D), view(M, A_ROWS, 4, P)
    out = []
    for f in range(KD):
        out.append(([x[:, t, f * P:(f + 1) * P] for t in range(4)], M[:, O_H + f * S:O_H + (f + 1) * S]))
    for f in range(0, KD, 2):
        out.append(([m[:, t, g * P:(g + 1) * P] for g in (f, f + 1) for t in range(2)],
                    M[:, O_MEM + f * NM:O_MEM + (f + 2) * NM]))
    for f in range(0, KD, 2):
        out.append(([c[:, t, g * P:(g + 1) * P] for g in (f, f + 1) for t in range(2)],
                    M[:, O_CTX + f * NM:O_CTX + (f + 2) * NM]))
    out.append(([r[:, t, :] for t in range(4)], M[:, O_VEC:O_VEC + 512]))
    return out


def setup_sync(k, sp):
    M, a = k.M, k.a
    sp.dma_start(M[:, O_CST:O_CST + 512], a["const_base"]).then_inc(k.const_in, 16)
    sp.dma_start(view(M, A_XTOK, 4, D), a["x"][0].rearrange("(t p) d -> p t d", p=P)).then_inc(k.const_in, 16)
    sp.dma_start(view(M, A_MTOK, 2, D), a["mem"][0].rearrange("(t p) d -> p t d", p=P)).then_inc(k.tok_in, 16)
    sp.dma_start(view(M, A_CTOK, 2, D), a["ctx_2"][0].rearrange("(t p) d -> p t d", p=P)).then_inc(k.tok_in, 16)
    load_rows(k, sp, 0)


def load_rows(k, eng, which):
    rows = view(k.M, A_ROWS, 4, P)
    eng.wait_ge(k.rows_clear, 1)
    for n, (t, r, cnt, width, src) in enumerate(k.row_sources.values()):
        if n % 2 == which:
            eng.dma_start(rows[r:r + cnt, t, 0:width], src).then_inc(k.rows_in, 16)


def setup_scalar(k, act):
    load_rows(k, act, 1)


def setup_tensor(k, pe):
    pe.wait_ge(k.const_in, 32)
    for n, (blocks, _) in enumerate(turns(k)):
        if n == KD:
            pe.wait_ge(k.tok_in, 32)
        if n == 2 * KD:
            pe.wait_ge(k.rows_in, 16 * k.n_rows)
        if n >= 4:
            pe.wait_ge(k.turn_read, n - 3)
        for j, b in enumerate(blocks):
            mm = pe.transpose(k.bank[n % 4][:, j * P:(j + 1) * P], b, k.ident)
        mm.then_inc(k.turned, 1)


def setup_vector(k, dve):
    dve.memset(view(k.M, A_ROWS, 512), 0.0).then_inc(k.rows_clear, 1)
    for n, (_, dst) in enumerate(turns(k)):
        dve.wait_ge(k.turned, n + 1)
        dve.tensor_copy(dst, k.bank[n % 4][:, :]).then_inc(k.turn_read, 1)


NORM_SIGNALS = ("squared", "added", "summed", "inverted", "rooted", "scaled", "moved", "renewed", "normed")
HALF = KD // 2


class Norm:
    def __init__(self, k, name, src, n, outs, scratch):
        self.src, self.n, self.outs = src, n, outs
        self.sq = view(k.M, scratch, 2, n)
        self.acc = view(k.M, scratch + 2 * n, n)
        self.rstd = view(k.M, scratch + 3 * n, n)
        self.tmp = view(k.M, scratch + 4 * n, 2, n)
        self.before, k.outs = k.outs, k.outs + KD * len(outs)
        self.nth, k.norms = k.norms, k.norms + 1
        self.pth = k.posts
        s = k.norm_sems
        self.squared, self.added, self.summed, self.inverted, self.rooted, self.scaled, self.moved, self.renewed, self.normed = (
            s[x] for x in NORM_SIGNALS)


def norm_scalar(k, act, j):
    for c in range(KD):
        if c >= 2:
            act.wait_ge(j.added, KD * j.nth + c - 1)
        if j.chained:
            act.wait_ge((j.moved, j.renewed)[c % 2], HALF * j.src_post + c // 2 + 1)
        act.activation(j.sq[:, c % 2, :], j.src[:, c, :], ACT.Square).then_inc(j.squared, 1)


def norm_add_vector(k, dve, j):
    for c in range(KD):
        dve.wait_ge(j.squared, KD * j.nth + c + 1)
        if c == 0:
            dve.tensor_copy(j.acc, j.sq[:, 0, :]).then_inc(j.added, 1)
        else:
            dve.wait_ge(j.added, KD * j.nth + c)
            dve.tensor_tensor(j.acc, j.acc, j.sq[:, c % 2, :], ALU.add).then_inc(j.added, 1)


def norm_tensor(k, pe, j, bank):
    if j.chained:
        for c in range(KD):
            pe.wait_ge(j.squared, KD * j.nth + c + 1)
            pe.matmul(bank[:, :j.n], k.means, j.sq[:, c % 2, :], start=c == 0, stop=c == KD - 1).then_inc(j.added, 1)
        return
    pe.wait_ge(j.added, KD * (j.nth + 1))
    pe.matmul(bank[:, :j.n], k.means, j.acc, start=True, stop=True).then_inc(j.summed, 1)


def norm_root_vector(k, dve, j, bank):
    if j.chained:
        dve.wait_ge(j.added, KD * (j.nth + 1))
    else:
        dve.wait_ge(j.summed, j.sth + 1)
    k.dve.link(dve.tensor_scalar(j.rstd, bank[:, :j.n], RMS_EPS, None, ALU.add))
    dve.reciprocal(j.rstd, j.rstd).then_inc(j.inverted, 1)
    dve.wait_ge(j.rooted, j.nth + 1)


def norm_root_scalar(k, act, j):
    act.wait_ge(j.inverted, j.nth + 1)
    act.activation(j.rstd, j.rstd, ACT.Sqrt).then_inc(j.rooted, 1)


def norm_scale_vector(k, dve, j):
    for gain, dst, shift in j.outs:
        for c in range(KD):
            ins = dve.scalar_tensor_tensor(out=dst[:, c, :], in0=j.src[:, c, :], scalar=gain(c), in1=j.rstd,
                                           op0=ALU.mult, op1=ALU.mult)
            if shift is not None:
                k.dve.link(ins)
                ins = dve.tensor_scalar(dst[:, c, :], dst[:, c, :], shift(c), None, ALU.add)
            ins.then_inc(j.normed, 1)


def post_scale_vector(k, dve, j, gain):
    for c in range(KD):
        if c % 2 == 0 and c >= 2:
            dve.wait_ge(j.moved, HALF * j.pth + c // 2)
        if c % 2 == 1 and c >= 3:
            dve.wait_ge(j.renewed, HALF * j.pth + c // 2)
        ins = dve.scalar_tensor_tensor(out=j.tmp[:, c % 2, :], in0=j.src[:, c, :], scalar=gain(c), in1=j.rstd,
                                       op0=ALU.mult, op1=ALU.mult)
        if c % 2 == 0:
            ins.then_inc(j.scaled, 1)
        else:
            k.dve.link(ins)
            dve.tensor_tensor(k.H[:, c, :], k.H[:, c, :], j.tmp[:, 1, :], ALU.add).then_inc(j.renewed, 1)


def post_add_pool(k, pool, j):
    for c in range(0, KD, 2):
        pool.wait_ge(j.scaled, HALF * j.pth + c // 2 + 1)
        pool.tensor_tensor(k.H[:, c, :], k.H[:, c, :], j.tmp[:, 0, :], ALU.add).then_inc(j.moved, 1)


class Phase:

    soft = False

    def __init__(self, name, sync=None, tensor=None, vector=None, scalar=None, pool=None):
        self.name, self.sync, self.tensor, self.vector, self.scalar, self.pool = name, sync, tensor, vector, scalar, pool


def block_feature(pe, bank, w, c0, m, rhs, kc, k0=0, start=True, stop=True):
    for q in range(kc):
        mm = pe.matmul(bank, w[:, q, c0:c0 + m], rhs(k0 + q), start=start and q == 0, stop=stop and q == kc - 1)
    return mm


def settle(k, pe, phase):
    for other, s in k.phase_end.items():
        if other != "tensor":
            pe.wait_ge(s, k.phase_index[phase] + 1)


class Lead:

    def __init__(self, phase, norm):
        self.phase, self.norm = phase.name, norm
        phase.soft = True

    def block(self, k, pe, bank, w, rhs):
        for q in range(KD):
            pe.wait_ge(self.norm.normed, self.norm.before + q + 1)
            mm = pe.matmul(bank, w[:, q, 0:P], rhs(q), start=q == 0, stop=q == KD - 1)
        mm.then_inc(k.half_done, 1)
        settle(k, pe, self.phase)


def block_token(pe, bank, act_chunk, w, kc):
    for q in range(kc):
        mm = pe.matmul(bank, act_chunk(q), w[:, q, :], start=q == 0, stop=q == kc - 1)
    return mm


def build(nc, a, out, stop=None, consts=None):
    k = Kit()
    k.a = a
    with ExitStack() as ctx:
        k.M = ctx.enter_context(nc.sbuf_tensor("sbuf", [P, WORDS], F32))
        k.psum = ctx.enter_context(nc.psum_tensor("psum", [P, 8 * 512], F32))
        k.bank = [k.psum[:, 512 * i:512 * (i + 1)] for i in range(8)]
        names = []

        def sem(name):
            names.append(name)
            return ctx.enter_context(nc.semaphore(name))

        k.sem = sem
        M = k.M
        k.ident = M[:, O_CST:O_CST + P]
        k.means = M[:, O_CST + P:O_CST + 2 * P]
        k.causal = M[:, O_CST + 2 * P:O_CST + 3 * P]
        k.lower = M[:, O_CST + 3 * P:O_CST + 4 * P]
        k.H = view(M, O_H, KD, S)
        k.memT = view(M, O_MEM, KD, NM)
        k.ctxT = view(M, O_CTX, KD, NC_CTX)
        k.slot = lambda n, kc, cols: view(M, O_RING + n * SLOT_WORDS, kc, cols)
        k.const_in, k.tok_in, k.rows_in, k.rows_clear = sem("const_in"), sem("tok_in"), sem("rows_in"), sem("rows_clear")
        k.turned, k.turn_read, k.out_sent, k.half_done = sem("turned"), sem("turn_read"), sem("out_sent"), sem("half_done")
        k.dve_steps, k.act_steps, k.pool_steps = sem("dve_steps"), sem("act_steps"), sem("pool_steps")
        k.norms, k.sums, k.posts, k.outs = 0, 0, 0, 0
        k.norm_sems = {s: sem(f"norm_{s}") for s in NORM_SIGNALS}
        k.tile_landed = [sem(f"tile_landed{i}") for i in range(SLOTS)]
        k.phase_end = {e: sem(f"phase_end_{e}") for e in ("tensor", "vector", "scalar", "pool")}

        k.row_sources = {}
        for t, rows in enumerate(ROWS):
            r = 0
            for name, n in rows:
                w = P
                if name in a:
                    h = a[name]
                    src = h.rearrange(" ".join("abcd"[:len(h.shape)]) + " -> (" + " ".join("abcd"[:len(h.shape)]) + ")") if len(h.shape) > 1 else h
                    src = src.rearrange("(c p) -> c p", p=P)
                elif name.startswith("rwkv_tap"):
                    src = a["rwkv_conv_2"][0, int(name[-1]), 0:12 * P].rearrange("(c p) -> c p", p=P)
                elif name.startswith("ffn_tap"):
                    src = a["ffn_conv_2"][0, int(name[-1])].rearrange("(c p) -> c p", p=P)
                elif name == "rwkv_wa_taps":
                    src, w = a["rwkv_conv_2"][0, :, 1536:1600], 64
                else:
                    src, w = a["rwkv_conv_2"][0, :, 1600:1696], 96
                k.row_sources[name] = (t, r, n, w, src)
                r += n
        k.n_rows = len(k.row_sources)

        phases = [Phase("setup", sync=setup_sync, tensor=setup_tensor, vector=setup_vector, scalar=setup_scalar)]
        phases += first_block_phases(k, stop)
        if stop is None or stop.endswith("2"):
            phases += second_block_phases(k, stop)
        k.phase_index = {p.name: n for n, p in enumerate(phases)}
        phases.append(final_phase(k, out))
        block = ctx.enter_context(nc.Block())

        def boundary(eng, me, n):
            eng.drain().then_inc(k.phase_end[me], 1)
            for other, s in k.phase_end.items():
                if other != me and not (me == "tensor" and phases[n].soft):
                    eng.wait_ge(s, n + 1)

        @block.sync
        def _(sp):
            k.sp_stream = Stream(k, sp)
            for ph in phases:
                if ph.sync:
                    ph.sync(k, sp)

        @block.tensor
        def _(pe):
            k.pe_stream = Stream(k, pe)
            for n, ph in enumerate(phases):
                for step in ph.tensor if isinstance(ph.tensor, list) else [ph.tensor] if ph.tensor else []:
                    step(k, pe)
                boundary(pe, "tensor", n)

        @block.vector
        def _(dve):
            k.dve = Chain(dve, k.dve_steps)
            for n, ph in enumerate(phases):
                if ph.vector:
                    ph.vector(k, dve)
                boundary(dve, "vector", n)

        @block.scalar
        def _(act):
            k.act = Chain(act, k.act_steps)
            for n, ph in enumerate(phases):
                if ph.scalar:
                    ph.scalar(k, act)
                boundary(act, "scalar", n)

        @block.gpsimd
        def _(pool):
            k.pool = Chain(pool, k.pool_steps)
            for n, ph in enumerate(phases):
                if ph.pool:
                    ph.pool(k, pool)
                boundary(pool, "pool", n)


A_A = O_ARENA
A_B = A_A + KD * S
A_MIX = A_B + KD * S
A_Y = A_MIX + KD * S
A_HID = A_Y + KD * S
A_SCR = A_HID + KF * S
A_TMP = A_SCR + 6 * S
assert A_TMP + 4 * S <= WORDS
A_MN = A_HID
A_KM = A_MN + KD * NM
A_VM = A_KM + 2 * NM
A_QM = A_VM + 2 * NM
A_V = A_QM + 2 * S
A_K = A_V + 4 * MAIN
assert A_K + 6 * S <= A_SCR
A_Q = A_Y
A_NEGC = A_Y + 6 * S
A_WS = A_Y
A_BC = A_Y + 2 * 6 * P
A_PT = A_A
A_PR = A_TMP


def norm_phase(k, name, jobs, post=None):

    tensor = [lambda k, pe, j=j, b=b: norm_tensor(k, pe, j, k.bank[b])
              for j, b in ([(post[0], 7)] if post else []) + [(j, n) for n, j in enumerate(jobs)]]

    def scalar(k, act):
        if post:
            norm_root_scalar(k, act, post[0])
        for j in jobs:
            norm_scalar(k, act, j)
            norm_root_scalar(k, act, j)

    def vector(k, dve):
        if post:
            norm_root_vector(k, dve, post[0], k.bank[7])
            post_scale_vector(k, dve, post[0], post[1])
        for n, j in enumerate(jobs):
            if not j.chained:
                norm_add_vector(k, dve, j)
            norm_root_vector(k, dve, j, k.bank[n])
            norm_scale_vector(k, dve, j)

    def pool(k, pool):
        if post:
            post_add_pool(k, pool, post[0])

    return Phase(name, tensor=tensor, scalar=scalar, vector=vector, pool=pool)


def square_scalar(k, act, j, copied, c, i=None):
    act.wait_ge(copied[0], at(i, 2, copied[1] + c + 1))
    act.wait_ge(j.added, at(i, 2, KD * j.nth + c - 1))
    src = j.src[:, bass.ds(at(i, 2, c), 1), :].rearrange("p a b -> p (a b)") if i is not None else j.src[:, c, :]
    act.activation(j.sq[:, c % 2, :], src, ACT.Square).then_inc(j.squared, 1)


def square_vector(k, dve, j, c, i=None):
    dve.wait_ge(j.squared, at(i, 2, KD * j.nth + c + 1))
    dve.wait_ge(j.added, at(i, 2, KD * j.nth + c))
    dve.tensor_tensor(j.acc, j.acc, j.sq[:, c % 2, :], ALU.add).then_inc(j.added, 1)


def make_norm(k, name, src, n, outs, scratch, after=None):
    j = Norm(k, name, src, n, outs, scratch)
    if not outs:
        k.posts += 1
    j.chained = after is not None
    if j.chained:
        j.src_post = after.pth
    else:
        j.sth, k.sums = k.sums, k.sums + 1
    return j


def mem_projection(k, L):
    t0 = k.plan
    k.plan += 2
    MN, KM, VM = view(k.M, A_MN, KD, NM) if L == 0 else k.memT, view(k.M, A_KM, 2, NM), view(k.M, A_VM, 2, NM)
    w = k.a["w_mem_kv"][L].rearrange("(c p) n -> p c n", p=P)

    def sync(k, sp):
        for t in range(2):
            k.sp_stream.load(w[:, :, t * 256:(t + 1) * 256], KD, 256)

    def tensor(k, pe):
        wk = k.pe_stream.take(KD, 256)
        for b in range(2):
            block_feature(pe, k.bank[2 + b][:, :NM], wk, b * P, P, lambda q: MN[:, q, :], KD).then_inc(k.half_done, 1)
        wv = k.pe_stream.take(KD, 256)
        for t in range(2):
            block_token(pe, k.bank[4 + t][:, :NM], lambda q: MN[:, q, t * P:(t + 1) * P], wv, KD).then_inc(k.half_done, 1)

    def vector(k, dve):
        for b in range(4):
            dve.wait_ge(k.half_done, 2 * t0 + b + 1)
            dst = KM[:, b, :] if b < 2 else VM[:, b - 2, :]
            dve.tensor_copy(dst, k.bank[2 + b][:, :NM])

    return Phase(f"mem_projection{L}", sync=sync, tensor=tensor, vector=vector)


def beside(phase, other, at_step):
    steps = list(phase.tensor) if isinstance(phase.tensor, list) else [phase.tensor]
    steps.insert(at_step, other.tensor)

    def sync(k, sp):
        other.sync(k, sp)
        if phase.sync:
            phase.sync(k, sp)

    def vector(k, dve):
        phase.vector(k, dve)
        other.vector(k, dve)

    return Phase(phase.name, sync=sync, tensor=steps, vector=vector, scalar=phase.scalar, pool=phase.pool)


def load_columns(k, w, c0, c1):
    for c in range(c0, c1, 256):
        k.sp_stream.load(w[:, :, c:min(c + 256, c1)], KD, min(256, c1 - c))


def input_projection_a(k, aside, lead):
    t0 = k.plan
    k.plan += 7
    M = k.M
    A, U, V, QM = view(M, A_A, KD, S), view(M, A_B, 6, S), view(M, A_V, 4, MAIN), view(M, A_QM, 2, S)
    w = k.a["w_in_a"][0].rearrange("(c p) n -> p c n", p=P)
    read = k.sem("in_a_read")
    halves = [("u", b) for b in range(6)] + [("v", c, t) for c in range(3) for t in range(2)] + [("q", b) for b in range(2)]

    def sync(k, sp):
        load_columns(k, w, 0, 1792)
        sp.dma_start(view(M, A_WS, 6, P), k.a["w_spatial"][0].rearrange("g t s -> t g s")).then_inc(k.ws_in, 16)
        for n, name in enumerate(("ln_v_g", "ln_v_b")):
            sp.dma_start(view(M, A_BC, 3, MAIN)[:, n, :], k.a[name].broadcast_to([P, MAIN])).then_inc(k.ws_in, 16)
        sp.dma_start(view(M, A_BC, 3, MAIN)[:, 2, :],
                     k.a["b_spatial"].rearrange("a g t -> a (g t)").broadcast_to([P, MAIN])).then_inc(k.ws_in, 16)

    def tensor(k, pe):
        for h, half in enumerate(halves):
            if h == 4:
                norm_tensor(k, pe, aside, k.bank[4])
            if h % 2 == 0:
                wt = k.pe_stream.take(KD, 256)
            if h >= 4:
                pe.wait_ge(read, h - 3)
            bank = k.bank[h % 4]
            if h == 0:
                lead.block(k, pe, bank, wt, lambda q: A[:, q, :])
                continue
            if half[0] == "v":
                for t in range(2):
                    tok = 2 * half[2] + t
                    mm = block_token(pe, bank[:, t * 256:(t + 1) * 256], lambda q: A[:, q, tok * P:(tok + 1) * P], wt, KD)
            else:
                mm = block_feature(pe, bank[:, :], wt, (half[1] % 2) * P, P, lambda q: A[:, q, :], KD)
            mm.then_inc(k.half_done, 1)

    def vector(k, dve):
        norm_add_vector(k, dve, aside)
        norm_root_vector(k, dve, aside, k.bank[4])
        norm_scale_vector(k, dve, aside)

    def scalar(k, act):
        norm_scalar(k, act, aside)
        for h, half in enumerate(halves):
            if h == 4:
                norm_root_scalar(k, act, aside)
            act.wait_ge(k.half_done, 2 * t0 + h + 1)
            bank = k.bank[h % 4][:, :]
            if half[0] == "u":
                act.activation(U[:, half[1], :], bank, ACT.Gelu_apprx_tanh).then_inc(read, 1)
            elif half[0] == "v":
                _, c, t = half
                act.activation(V[:, 2 * t:2 * t + 2, c * 256:(c + 1) * 256], bank.rearrange("p (a b) -> p a b", a=2),
                               ACT.Gelu_apprx_tanh).then_inc(read, 1)
            else:
                act.activation(QM[:, half[1], :], bank, ACT.Copy, scale=HEAD ** -0.5).then_inc(read, 1)

    return Phase("input_projection_a", sync=sync, tensor=tensor, vector=vector, scalar=scalar)


def spatial_prepare(k):
    M = k.M
    V, WS, BC = view(M, A_V, 4, MAIN), view(M, A_WS, 12, P), view(M, A_BC, 3, MAIN)
    turned, st = k.sem("ws_turned"), k.sem("v_stats")
    stats, mv = view(M, O_SML, 4, 12), view(M, O_SML + 48, 4, 2)
    rooted = k.sem("v_rooted")

    def tensor(k, pe):
        pe.wait_ge(k.ws_in, 64)
        for g in range(6):
            mm = pe.transpose(k.bank[g // 4][:, (g % 4) * P:(g % 4 + 1) * P], WS[:, g, :], k.ident)
        mm.then_inc(turned, 1)

    def vector(k, dve):
        for t in range(4):
            for n in range(2):
                ins = dve.bn_stats(stats[:, t, 6 * n:6 * n + 6], V[:, t, n * 384:(n + 1) * 384])
        k.dve.link(ins)
        for t in range(4):
            ins = dve.bn_aggr(mv[:, t, :], stats[:, t, :])
        k.dve.link(ins)
        k.dve.link(dve.tensor_scalar(mv[:, :, 1:2], mv[:, :, 1:2], LN_EPS, None, ALU.add))
        dve.reciprocal(mv[:, :, 1:2], mv[:, :, 1:2]).then_inc(st, 1)
        dve.wait_ge(turned, 1)
        dve.wait_ge(k.ws_in, 64)
        for g in range(6):
            dve.tensor_tensor(WS[:, 6 + g, :], k.bank[g // 4][:, (g % 4) * P:(g % 4 + 1) * P], k.lower, ALU.mult)
        dve.wait_ge(rooted, 1)
        for t in range(4):
            k.dve.link(dve.tensor_scalar(V[:, t, :], V[:, t, :], mv[:, t, 0:1], mv[:, t, 1:2], ALU.subtract, ALU.mult))
            k.dve.link(dve.tensor_tensor(V[:, t, :], V[:, t, :], BC[:, 0, :], ALU.mult))
            dve.tensor_tensor(V[:, t, :], V[:, t, :], BC[:, 1, :], ALU.add)

    def scalar(k, act):
        act.wait_ge(st, 1)
        act.activation(mv[:, :, 1:2], mv[:, :, 1:2], ACT.Sqrt).then_inc(rooted, 1)

    return Phase("spatial_prepare", tensor=tensor, vector=vector, scalar=scalar)


def spatial_gate(k):
    M = k.M
    V, WS, BC, U, MIX = (view(M, A_V, 4, MAIN), view(M, A_WS, 12, P), view(M, A_BC, 3, MAIN), view(M, A_B, 6, S),
                         view(M, A_MIX, KD, S))
    mixed, read = k.sem("spatial_mixed"), k.sem("spatial_read")

    def tensor(k, pe):
        for g in range(6):
            if g >= 4:
                pe.wait_ge(read, g - 3)
            for c in range(4):
                mm = pe.matmul(k.bank[g % 4][:, c * P:(c + 1) * P], V[:, c, g * P:(g + 1) * P], WS[:, 6 + g, :],
                               start=True, stop=True)
            mm.then_inc(mixed, 1)

    def vector(k, dve):
        for g in range(6):
            dve.wait_ge(mixed, g + 1)
            bias = BC[:, 2:3, g * P:(g + 1) * P].broadcast_to([P, 4, P])
            ins = dve.tensor_tensor(MIX[:, g, :].rearrange("p (c t) -> p c t", c=4),
                                    k.bank[g % 4][:, :].rearrange("p (c t) -> p c t", c=4), bias, ALU.add)
            ins.then_inc(read, 1)
            dve.wait_ge(read, g + 1)
            dve.tensor_tensor(MIX[:, g, :], MIX[:, g, :], U[:, g, :], ALU.mult)

    return Phase("spatial_gate", tensor=tensor, vector=vector)


class Attention:

    def __init__(self, name, heads, keys, q, key, value, out, negc=None):
        self.name, self.heads, self.keys, self.q, self.key, self.value, self.out, self.negc = \
            name, heads, keys, q, key, value, out, negc


def attention_phase(k, s):
    M = k.M
    NJ = 4
    pt = view(M, A_PT, 2, NJ, S)
    pr = view(M, A_PR, 3, S)
    small = view(M, O_SML, 4, 2)
    scored, maxed, raised, summed_inv, ready, turned, copied, valued, taken = (
        k.sem(f"{s.name}_{x}") for x in ("scored", "maxed", "raised", "inv", "ready", "turned", "copied", "valued", "taken"))
    units = [(h, i) for h in range(s.heads) for i in range(4)]
    nk = [s.keys(i) for i in range(4)]
    rows = lambda h: slice(64 * (h % 2), 64 * (h % 2) + 64)
    last_unit = lambda h: 4 * h + 3

    def tensor(k, pe):
        for u in range(len(units) + 2):
            if u < len(units):
                h, i = units[u]
                bank = k.bank[u % 3][:, :nk[i]]
                if u >= 3:
                    pe.wait_ge(raised, u - 2)
                if s.negc is not None:
                    pe.matmul(bank, k.ident[:, h:h + 1].broadcast_to([P, P]), s.negc[:, :nk[i]], start=True, stop=False)
                    pe.matmul(bank[:, i * P:], k.ident, k.causal, start=False, stop=False)
                pe.matmul(bank, s.q(h, i), s.key(h, nk[i]), start=s.negc is None, stop=True).then_inc(scored, 1)
            if u >= 2:
                v = u - 2
                h, i = units[v]
                pe.wait_ge(ready, v + 1)
                if v >= 2:
                    pe.wait_ge(copied, v - 1)
                for j in range(nk[i] // P):
                    mm = pe.transpose(k.bank[3 + v % 2][:, j * P:(j + 1) * P], pr[:, v % 3, j * P:(j + 1) * P], k.ident)
                mm.then_inc(turned, 1)
                if i == 3 and h >= 1:
                    values(pe, h - 1)
        values(pe, s.heads - 1)

    def values(pe, h):
        pe.wait_ge(copied, last_unit(h) + 1)
        if h >= 2:
            pe.wait_ge(taken, h - 1)
        out = k.bank[5 + h % 2][rows(h), :]
        n = nk[3] // P
        for j in range(n):
            q0 = j * P if s.negc is not None else 0
            mm = pe.matmul(out[:, q0:], s.value(h, j), pt[:, h % 2, j, q0:], start=j == 0, stop=j == n - 1)
        mm.then_inc(valued, 1)

    def vector(k, dve):
        for u in range(len(units) + 1):
            if u < len(units):
                h, i = units[u]
                dve.wait_ge(scored, u + 1)
                k.dve.link(dve.tensor_reduce(small[:, u % 4, 0:1], k.bank[u % 3][:, :nk[i]], AX_X, ALU.max))
                dve.tensor_scalar(small[:, u % 4, 0:1], small[:, u % 4, 0:1], -1.0, None, ALU.mult).then_inc(maxed, 1)
            if u >= 1:
                v = u - 1
                h, i = units[v]
                dve.wait_ge(raised, v + 1)
                k.dve.link(dve.reciprocal(small[:, v % 4, 1:2], small[:, v % 4, 1:2]))
                dve.tensor_scalar(pr[:, v % 3, :nk[i]], pr[:, v % 3, :nk[i]], small[:, v % 4, 1:2], None,
                                  ALU.mult).then_inc(ready, 1)
                if i == 0 and h >= 2:
                    take(dve, h - 2)
        take(dve, s.heads - 2)
        take(dve, s.heads - 1)

    def take(dve, h):
        dve.wait_ge(valued, h + 1)
        dve.tensor_copy(s.out(h), k.bank[5 + h % 2][rows(h), :]).then_inc(taken, 1)

    def scalar(k, act):
        for u in range(len(units) + 3):
            if u < len(units):
                h, i = units[u]
                act.wait_ge(maxed, u + 1)
                if u >= 3:
                    act.wait_ge(turned, u - 2)
                act.activation(pr[:, u % 3, :nk[i]], k.bank[u % 3][:, :nk[i]], ACT.Exp, bias=small[:, u % 4, 0:1],
                               accum_out=small[:, u % 4, 1:2]).then_inc(raised, 1)
            if u >= 3:
                v = u - 3
                h, i = units[v]
                act.wait_ge(turned, v + 1)
                if h >= 2:
                    act.wait_ge(valued, h - 1)
                n = nk[i] // P
                act.activation(pt[:, h % 2, 0:n, i * P:(i + 1) * P],
                               k.bank[3 + v % 2][:, :nk[i]].rearrange("p (j q) -> p j q", q=P), ACT.Copy).then_inc(copied, 1)

    return Phase(s.name, tensor=tensor, vector=vector, scalar=scalar)


def mem_attention(k, L):
    M = k.M
    QM, KM, VM, MIX = view(M, A_QM, 2, S), view(M, A_KM, 2, NM), view(M, A_VM, 2, NM), view(M, A_MIX, KD, S)
    r = lambda h: slice(64 * (h % 2), 64 * (h % 2) + 64)
    return attention_phase(k, Attention(
        f"mem_attention{L}", 4, lambda i: NM,
        q=lambda h, i: QM[r(h), h // 2, i * P:(i + 1) * P],
        key=lambda h, n: KM[r(h), h // 2, :n],
        value=lambda h, j: VM[:, j, h * HEAD:(h + 1) * HEAD],
        out=lambda h: MIX[r(h), 6 + h // 2, :]))


def fox_attention(k):
    M = k.M
    Q, K, V, MIX = view(M, A_Q, 6, S), view(M, A_K, 6, S), view(M, A_V, 4, MAIN), view(M, A_MIX, KD, S)
    r = lambda h: slice(64 * (h % 2), 64 * (h % 2) + 64)
    return attention_phase(k, Attention(
        "fox_attention", 12, lambda i: P * (i + 1),
        q=lambda h, i: Q[r(h), h // 2, i * P:(i + 1) * P],
        key=lambda h, n: K[r(h), h // 2, :n],
        value=lambda h, j: V[:, j, h * HEAD:(h + 1) * HEAD],
        out=lambda h: MIX[r(h), h // 2, :],
        negc=view(M, A_NEGC, S)))


def input_projection_b(k, lead):
    t0 = k.plan
    k.plan += 11
    M = k.M
    A, B = view(M, A_A, KD, S), view(M, A_B, KD, S)
    Q, K, V, QM, NEGC = view(M, A_Q, 6, S), view(M, A_K, 6, S), view(M, A_V, 4, MAIN), view(M, A_QM, 2, S), view(M, A_NEGC, S)
    wkv = k.a["w_shared_kv"].rearrange("(c p) n -> p c n", p=P)
    wb = k.a["w_in_b"][0].rearrange("(c p) n -> p c n", p=P)
    read, cleared = k.sem("in_b_read"), k.sem("in_b_cleared")
    halves = ([("k", b) for b in range(6)] + [("v", c, t) for c in range(3) for t in range(2)] + [("f", 0), ("f", 1)]
              + [("q", b) for b in range(6)] + [("m", b) for b in range(2)])

    def sync(k, sp):
        load_columns(k, wkv, 0, 1536)
        sp.dma_start(k.bf, k.a["b_forget"].rearrange("(h o) -> h o", o=1)).then_inc(k.bf_in, 16)
        load_columns(k, wkv, 1536, 1548)
        load_columns(k, wb, 0, 1024)

    def tensor(k, pe):
        for h, half in enumerate(halves):
            if h % 2 == 0:
                wt = k.pe_stream.take(KD, 12 if half[0] == "f" else 256)
            if h >= 4:
                pe.wait_ge(read, h - 3)
            bank = k.bank[h % 4]
            X = B if half[0] in "kvf" else A
            if h == 0:
                lead.block(k, pe, bank, wt, lambda q: B[:, q, :])
                continue
            if half[0] == "v":
                for t in range(2):
                    tok = 2 * half[2] + t
                    mm = block_token(pe, bank[:, t * 256:(t + 1) * 256], lambda q: X[:, q, tok * P:(tok + 1) * P], wt, KD)
            elif half[0] == "f":
                bank = k.bank[4]
                mm = block_feature(pe, bank[0:12, :], Shift(wt, 4 * half[1]), 0, 12, lambda q: X[:, q, :], 4, 4 * half[1],
                                   start=half[1] == 0, stop=half[1] == 1)
            else:
                mm = block_feature(pe, bank[:, :], wt, (half[1] % 2) * P, P, lambda q: X[:, q, :], KD)
            mm.then_inc(k.half_done, 1)

    def scalar(k, act):
        for h, half in enumerate(halves):
            act.wait_ge(k.half_done, 2 * t0 + h + 1)
            bank = k.bank[h % 4][:, :]
            if half[0] == "v":
                _, c, t = half
                act.activation(V[:, 2 * t:2 * t + 2, c * 256:(c + 1) * 256], bank.rearrange("p (a b) -> p a b", a=2),
                               ACT.Copy).then_inc(read, 1)
            elif half[0] == "f":
                if half[1] == 0:
                    act.wait_ge(cleared, 1)
                    act.activation(k.scrap, k.scrap, ACT.Copy).then_inc(read, 1)
                else:
                    act.activation(NEGC[0:12, :], k.bank[4][0:12, :], ACT.Copy).then_inc(read, 1)
            else:
                dst = {"k": K, "q": Q, "m": QM}[half[0]][:, half[1], :]
                act.activation(dst, bank, ACT.Copy, scale=1.0 if half[0] == "k" else HEAD ** -0.5).then_inc(read, 1)

    def vector(k, dve):
        k.dve.link(dve.memset(k.scrap, 0.0))
        dve.memset(NEGC, 0.0).then_inc(cleared, 1)

    return Phase("input_projection_b", sync=sync, tensor=tensor, scalar=scalar, vector=vector)


class Shift:

    def __init__(self, w, first):
        self.w, self.first = w, first

    def __getitem__(self, key):
        a, q, c = key
        return self.w[a, q + self.first, c]


def forget_phase(k):
    M = k.M
    Z = view(M, A_NEGC, S)
    E, R = view(M, A_SCR, S), view(M, A_SCR + S, S)
    a, b = k.sem("forget_abs"), k.sem("forget_log")

    def vector(k, dve):
        dve.wait_ge(k.bf_in, 16)
        k.dve.link(dve.tensor_scalar(R[0:12, :], Z[0:12, :], k.bf, -1.0, ALU.add, ALU.mult))
        k.dve.link(dve.tensor_scalar(E[0:12, :], R[0:12, :], -1.0, None, ALU.mult))
        k.dve.link(dve.tensor_tensor(E[0:12, :], E[0:12, :], R[0:12, :], ALU.max))
        dve.tensor_scalar(R[0:12, :], R[0:12, :], 0.0, None, ALU.max).then_inc(a, 1)
        dve.wait_ge(b, 1)
        k.dve.link(dve.tensor_tensor(R[0:12, :], R[0:12, :], E[0:12, :], ALU.add))
        k.dve.link(dve.memset(E[0:12, :], 1.0))
        k.dve.link(dve.tensor_tensor_scan(Z[0:12, :], E[0:12, :], R[0:12, :], 0.0, ALU.mult, ALU.add))

    def scalar(k, act):
        act.wait_ge(a, 1)
        k.act.link(act.activation(E[0:12, :], E[0:12, :], ACT.Exp, scale=-1.0))
        act.activation(E[0:12, :], E[0:12, :], ACT.Ln, bias=1.0).then_inc(b, 1)

    return Phase("forget", vector=vector, scalar=scalar)


def output_projection(k, name, w, post):
    t0 = k.plan
    k.plan += 4
    MIX, Y = view(k.M, A_MIX, KD, S), view(k.M, A_Y, KD, S)
    read = k.sem(f"{name}_read")
    w = w.rearrange("(c p) n -> p c n", p=P)

    def sync(k, sp):
        load_columns(k, w, 0, D)

    def tensor(k, pe):
        for b in range(KD):
            if b % 2 == 0:
                wt = k.pe_stream.take(KD, 256)
            if b >= 4:
                pe.wait_ge(read, b - 3)
            block_feature(pe, k.bank[b % 4][:, :], wt, (b % 2) * P, P, lambda q: MIX[:, q, :], KD).then_inc(k.half_done, 1)

    def vector(k, dve):
        k.dve.link(dve.memset(post.acc, 0.0))
        for b in range(KD):
            dve.wait_ge(k.half_done, 2 * t0 + b + 1)
            dve.tensor_copy(Y[:, b, :], k.bank[b % 4][:, :]).then_inc(read, 1)
            square_vector(k, dve, post, b)

    def scalar(k, act):
        for b in range(KD):
            square_scalar(k, act, post, (read, 0), b)

    return Phase(name, sync=sync, tensor=tensor, vector=vector, scalar=scalar)


def paired_units(k, eng, chains, unit):
    trips = KF // 4
    with eng.Fori(0, trips) as i:
        for c, n in chains:
            c.enter(i, n)
        for u in range(2):
            unit(i, u)
    for c, n in chains:
        c.leave(trips)
    unit(None, 2 * trips)


def at(i, per, off):
    return off if i is None else i * per + off


def ffn_up(k, name, w1, w2, c1, c2, tmp, lead, conv=None, aside=None):
    t0 = k.plan
    k.plan += KF
    M = k.M
    A, HID, T = view(M, A_A, KD, S), view(M, A_HID, KF, S), view(M, tmp, 4, S)
    w1 = w1.rearrange("(c p) n -> p c n", p=P)
    w2 = w2.rearrange("(c p) n -> p c n", p=P)
    free, gated, centred, tapped = (k.sem(f"{name}_{x}") for x in ("banks_free", "gated", "centred", "tapped"))

    def sync(k, sp):
        def unit(i, u):
            for w, c in ((w1, c1), (w2, c2)):
                k.sp_stream.load(w[:, :, c + 256 * u:][:, :, bass.ds(at(i, 512, 0), 256)], KD, 256)
        paired_units(k, sp, [(k.sp_stream, 4)], unit)

    def tensor(k, pe):
        pe.sem_inc(free, 2)

        def unit(i, u):
            pe.wait_ge(free, at(i, 2, u + 1))
            for g in range(2):
                wt = k.pe_stream.take(KD, 256)
                for b in range(2):
                    if u == g == b == 0:
                        lead.block(k, pe, k.bank[0], wt, lambda q: A[:, q, :])
                        continue
                    block_feature(pe, k.bank[4 * (u % 2) + 2 * g + b][:, :], wt, b * P, P, lambda q: A[:, q, :],
                                  KD).then_inc(k.half_done, 1)
        paired_units(k, pe, [(k.pe_stream, 4)], unit)

    def scalar(k, act):
        def unit(i, u):
            for b in range(2):
                act.wait_ge(k.half_done, at(i, 8, 2 * t0 + 4 * u + b + 1))
                if b == 0:
                    act.wait_ge(free, at(i, 2, u + 1))
                act.activation(T[:, 2 * (u % 2) + b, :], k.bank[4 * (u % 2) + b][:, :], ACT.Silu).then_inc(gated, 1)
        if aside:
            norm_scalar(k, act, aside)
        paired_units(k, act, [], unit)

    def vector(k, dve):
        def unit(i, u):
            for b in range(2):
                dve.wait_ge(k.half_done, at(i, 8, 2 * t0 + 4 * u + 2 + b + 1))
                dve.wait_ge(gated, at(i, 4, 2 * u + b + 1))
                bank = k.bank[4 * (u % 2) + 2 + b][:, :]
                dst = HID[:, bass.ds(at(i, 4, 2 * u + b), 1), :].rearrange("p a b -> p (a b)")
                ins = dve.tensor_tensor(dst, bank, T[:, 2 * (u % 2) + b, :], ALU.mult)
            ins.then_inc(free, 1)
        if aside:
            norm_add_vector(k, dve, aside)
        paired_units(k, dve, [], unit)

    def vec(i, u, b, half, what):
        return M[:, bass.ds(at(i, 4, O_VEC + conv[half][what] + 2 * u + b), 1)]

    def conv_scalar(k, act):
        def unit(i, u):
            for half in range(2):
                for b in range(2):
                    act.wait_ge(k.half_done, at(i, 8, 2 * t0 + 4 * u + 2 * half + b + 1))
                    if half == 0 and b == 0:
                        act.wait_ge(free, at(i, 2, u + 2))
                    act.activation(T[:, 2 * half + b, :], k.bank[4 * (u % 2) + 2 * half + b][:, :], ACT.Identity,
                                   scale=vec(i, u, b, half, "tap1"), bias=vec(i, u, b, half, "bias")).then_inc(centred, 1)
            for b in range(2):
                act.wait_ge(tapped, at(i, 4, 2 * u + b + 1))
                act.activation(T[:, 2 + b, :], T[:, 2 + b, :], ACT.Silu).then_inc(gated, 1)
        paired_units(k, act, [], unit)

    def conv_vector(k, dve):
        def unit(i, u):
            for half in range(2):
                for b in range(2):
                    dve.wait_ge(centred, at(i, 8, 4 * u + 2 * half + b + 1))
                    bank, t = k.bank[4 * (u % 2) + 2 * half + b], T[:, 2 * half + b, :]
                    k.dve.link(dve.scalar_tensor_tensor(out=t[:, 1:S], in0=bank[:, 0:S - 1], scalar=vec(i, u, b, half, "tap0"),
                                                        in1=t[:, 1:S], op0=ALU.mult, op1=ALU.add))
                    ins = dve.scalar_tensor_tensor(out=t[:, 0:S - 1], in0=bank[:, 1:S], scalar=vec(i, u, b, half, "tap2"),
                                                   in1=t[:, 0:S - 1], op0=ALU.mult, op1=ALU.add)
                    if half == 1:
                        ins.then_inc(tapped, 1)
                    else:
                        k.dve.link(ins)
            for b in range(2):
                dve.wait_ge(gated, at(i, 4, 2 * u + b + 1))
                dst = HID[:, bass.ds(at(i, 4, 2 * u + b), 1), :].rearrange("p a b -> p (a b)")
                ins = dve.tensor_tensor(dst, T[:, b, :], T[:, 2 + b, :], ALU.mult)
            ins.then_inc(free, 1)
        paired_units(k, dve, [(k.dve, 12)], unit)

    return Phase(name, sync=sync, tensor=tensor, vector=conv_vector if conv else vector,
                 scalar=conv_scalar if conv else scalar)


def ffn_down(k, name, w, post, aside=None):
    t0 = k.plan
    k.plan += 16
    HID, Y = view(k.M, A_HID, KF, S), view(k.M, A_Y, KD, S)
    w = w.rearrange("(h c p) n -> p h c n", h=2, p=P)
    free = k.sem(f"{name}_free")
    KH = KF // 2

    def sync(k, sp):
        with sp.Fori(0, KD // 2) as i:
            k.sp_stream.enter(i, 4)
            for b in range(2):
                for h in range(2):
                    k.sp_stream.load(w[:, h, :, b * P:][:, :, bass.ds(i * 256, P)], KH, P)
        k.sp_stream.leave(KD // 2)

    def tensor(k, pe):
        if aside:
            norm_tensor(k, pe, aside, k.bank[7])
        pe.sem_inc(free, 2)
        with pe.Fori(0, KD // 2) as i:
            k.pe_stream.enter(i, 4)
            for b in range(2):
                pe.wait_ge(free, i * 2 + (b + 1))
                for h in range(2):
                    wt = k.pe_stream.take(KH, P)
                    for q in range(KH):
                        mm = pe.matmul(k.bank[b][:, :], wt[:, q, :], HID[:, KH * h + q, :],
                                       start=h == 0 and q == 0, stop=h == 1 and q == KH - 1)
                        if q in (5, KH - 1):
                            mm.then_inc(k.half_done, 1)
        k.pe_stream.leave(KD // 2)

    def vector(k, dve):
        if aside:
            norm_root_vector(k, dve, aside, k.bank[7])
            norm_scale_vector(k, dve, aside)
        k.dve.link(dve.memset(post.acc, 0.0))
        with dve.Fori(0, KD // 2) as i:
            for b in range(2):
                dve.wait_ge(k.half_done, i * 8 + (2 * t0 + 4 * b + 4))
                dve.tensor_copy(Y[:, bass.ds(i * 2 + b, 1), :].rearrange("p a b -> p (a b)"),
                                k.bank[b][:, :]).then_inc(free, 1)
                square_vector(k, dve, post, b, i)

    def scalar(k, act):
        if aside:
            norm_root_scalar(k, act, aside)
        with act.Fori(0, KD // 2) as i:
            for b in range(2):
                square_scalar(k, act, post, (free, 2), b, i)

    return Phase(name, sync=sync, tensor=tensor, vector=vector, scalar=scalar)


def first_block_phases(k, stop):
    M = k.M
    k.plan = 0
    k.ws_in, k.bf_in = k.sem("spatial_in"), k.sem("b_forget_in")
    k.bf = M[0:12, O_SML + 200:O_SML + 201]
    k.scrap = M[0:1, O_SML + 202:O_SML + 203]
    A, B, Y, MN = view(M, A_A, KD, S), view(M, A_B, KD, S), view(M, A_Y, KD, S), view(M, A_MN, KD, NM)
    g = lambda name, base: (lambda c: col(k, name, base + c))

    ad = Adaptive(k)
    ph = []
    for L in range(2):
        if L == 0:
            mix = make_norm(k, "mix_norm0", k.H, S, [(g("ln_mix_pre", 0), A, None)], A_SCR)
            ph.append(ad.part(k, norm_phase(k, "input_norm", [mix]), (0,)))
            memory = make_norm(k, "mem_norm0", k.memT, NM, [(g("ln_mem", 0), MN, None)], A_TMP)
            ph.append(input_projection_a(k, memory, Lead(ph[-1], mix)))
            ph += [beside(spatial_prepare(k), mem_projection(k, L), 1), spatial_gate(k)]
        else:
            ph += [input_projection_b(k, Lead(ph[-1], nxt)), forget_phase(k), fox_attention(k)]
        ph.append(mem_attention(k, L))
        if stop == f"mix{L}":
            return ph
        post = make_norm(k, f"mix_post{L}", Y, S, [], A_SCR)
        ph.append(output_projection(k, f"output_projection{L}", k.a["w_out"][L], post))
        pre = make_norm(k, f"ffn_pre{L}", k.H, S, [(g("ln_ffn_pre", 8 * L), A, None)], A_HID, after=post)
        ph.append(ad.part(k, norm_phase(k, f"ffn_norm{L}", [pre], post=(post, g("ln_mix_post", 8 * L))), (0, 3)))
        lead = Lead(ph[-1], pre)
        if stop == f"hmix{L}":
            return ph
        if L == 0:
            aside = make_norm(k, "mem_norm1", k.memT, NM, [(g("ln_mem", 8), k.memT, None)], A_B)
        else:
            aside = make_norm(k, "ctx_norm", k.ctxT, NC_CTX, [(lambda c: derived_col(k, "gc", c), k.ctxT, lambda c: mod_col(k, c, 1))], A_B)
        ph.append(ffn_up(k, f"ffn_up{L}", k.a["w_ffn_gate"][L], k.a["w_ffn_up"][L], 0, 0, A_TMP, lead, aside=aside))
        post = make_norm(k, f"ffn_post{L}", Y, S, [], A_SCR)
        ph.append(ffn_down(k, f"ffn_down{L}", k.a["w_ffn_down"][L], post, aside))
        if L == 0:
            nxt = make_norm(k, "mix_norm1", k.H, S, [(g("ln_shared", 0), B, None), (g("ln_mix_pre", 8), A, None)], A_MIX, after=post)
            ph.append(beside(norm_phase(k, f"layer_norm{L}", [nxt], post=(post, g("ln_ffn_post", 8 * L))), mem_projection(k, 1), 1))
        else:
            nxt = make_norm(k, "second_norm", k.H, S, [(lambda c: derived_col(k, "gx", c), A, lambda c: mod_col(k, c))], A_HID, after=post)
            ph.append(ad.part(k, norm_phase(k, f"layer_norm{L}", [nxt], post=(post, g("ln_ffn_post", 8 * L))), (0, 3)))
            k.adaptive, k.second_lead = ad, Lead(ph[-1], nxt)
        if stop == f"h{L}":
            return ph
    return ph


T_ALL = NC_CTX + S
TT = T_ALL // P
LAM_INIT = 0.8 - 0.6 * 1.0
LN_X_EPS = 64e-5
CH = 64
NPAIR = 8
DECAY = -float(np.exp(-0.5))

D_Q = A_Y
D_K = D_Q + 4 * S
D_V = D_K + 4 * T_ALL
D_ROPE = D_V + TT * 512
D_PT = D_ROPE + P + 2 * S
D_P = D_PT + 2 * TT * S
D_LAM = D_P + 4 * T_ALL
assert D_LAM + 256 <= WORDS
R_R = A_Y
R_K = R_R + 4 * T_ALL
R_V = R_K + 4 * T_ALL
R_KK = R_V + 4 * T_ALL
R_WA = R_KK + 4 * T_ALL
R_GL = R_WA + T_ALL
R_YB = R_GL + S
R_TMP = R_YB + 4 * S
R_ABD = A_A
R_BBD, R_KBD, R_VBD = R_ABD + 1024, R_ABD + 2048, R_ABD + 3072
R_S0 = R_ABD + 4096
R_BTK, R_KTK, R_VTK = R_S0 + 1024, R_S0 + 2048, R_S0 + 3072
assert R_VTK + 1024 <= A_MIX
R_AR = O_MEM
R_B, R_G2, R_QK, R_QB, R_LT, R_RHO = (O_MEM + 1024 + 512 * n for n in range(6))
R_X, R_Y, R_T = R_TMP, R_TMP + 1024, R_TMP + 2048
R_PRE = R_TMP + 3072
R_KTBD = R_TMP + 3584
R_KV = R_KTBD
R_LOFF = R_KTBD + 1024
R_S = R_LOFF + 1024
assert R_S + 1024 <= WORDS
R_MASK = O_RING
MASKS = {}
_off = 0
for _n, _w in (("head", 2), ("x1", 2 * P), ("y1", 2 * P), ("incl", 2 * CH), ("neg", 2 * CH),
               ("strict", 2 * P), ("level", 5 * 2 * P), ("reset", 512), ("headsum", P)):
    MASKS[_n] = _off
    _off += _w
N_MASK = _off
R_W2 = R_MASK + N_MASK
R_KD = R_W2 + 1024
R_A2 = R_KD + 1024
R_AL = R_A2 + 1024
R_SIG = R_AL + T_ALL
assert R_SIG + 1024 <= O_MEM
R_SA = R_KD

MOD_DERIVED = ("gx", "gc", "gf", "pm", "pf")


class Adaptive:

    def __init__(self, k):
        self.done = 0
        self.rows_out, self.turned = k.sem("mod_rows_out"), k.sem("mod_turned")
        self.rows = view(k.M, A_TMP, 1024)[0:2, :]
        self.silu = k.sem("cond_silu")
        self.SIL, self.MOD = view(k.M, O_MOD + 144, KD, 2), view(k.M, O_MOD, 48, 2)
        self.w = k.a["w_mod_2"][0].rearrange("(c p) n -> p c n", p=P)

    def part(self, k, phase, split):
        g, t0, rows = self.done, k.plan, self.rows
        self.done += 1
        k.plan += 4
        sync0, vector0, scalar0 = phase.sync, phase.vector, phase.scalar
        steps = phase.tensor if isinstance(phase.tensor, list) else [phase.tensor]
        assert len(split) == len(steps)
        out = k.psum[0:2, 512 * 5:512 * 7]
        turned = k.bank[5][:, 0:16].rearrange("p (n two) -> p n two", two=2)

        def sync(k, sp):
            for t in range(4):
                c = 1024 * g + 256 * t
                k.sp_stream.load(self.w[:, :, c:c + 256], KD, 256)
            if sync0:
                sync0(k, sp)

        def tensor(k, pe):
            if g == 0:
                pe.wait_ge(self.silu, 1)
            first = 0
            for n, step in zip(split + (4 - sum(split),), steps + [None]):
                for t in range(first, first + n):
                    wt = k.pe_stream.take(KD, 256)
                    for q in range(KD):
                        mm = pe.matmul(out[:, 256 * t:256 * t + 256], self.SIL[:, q, :], wt[:, q, :], start=q == 0, stop=q == KD - 1)
                        if q in (3, KD - 1):
                            mm.then_inc(k.half_done, 1)
                first += n
                if step:
                    step(k, pe)
            pe.wait_ge(self.rows_out, g + 1)
            for n in range(8):
                mm = pe.transpose(turned[:, n, :], rows[:, n * P:(n + 1) * P], k.ident[0:2, 0:2])
            mm.then_inc(self.turned, 1)

        def scalar(k, act):
            if g == 0:
                for n, name in enumerate(("c_2", "c_ctx_2")):
                    ins = act.activation(self.SIL[:, :, n:n + 1], k.M[:, O_VEC + VCOL[name]:O_VEC + VCOL[name] + KD].rearrange(
                        "p (c o) -> p c o", o=1), ACT.Silu)
                ins.then_inc(self.silu, 1)
            if scalar0:
                scalar0(k, act)
            act.wait_ge(k.half_done, 2 * (t0 + 4))
            act.activation(rows, out, ACT.Copy).then_inc(self.rows_out, 1)

        def vector(k, dve):
            if vector0:
                vector0(k, dve)
            dve.wait_ge(self.turned, g + 1)
            bias = k.M[:, O_VEC + VCOL["b_mod_2"] + 8 * g:O_VEC + VCOL["b_mod_2"] + 8 * g + 8].rearrange("p (c o) -> p c o", o=1)
            ins = dve.tensor_tensor(self.MOD[:, 8 * g:8 * g + 8, :], turned, bias.broadcast_to([P, 8, 2]), ALU.add)
            k.dve.link(ins)
            self.derive(k, dve, g)

        return Phase(phase.name, sync=sync, tensor=tensor, vector=vector, scalar=scalar, pool=phase.pool)

    def derive(self, k, dve, g):
        vec = lambda name, n=KD: k.M[:, O_VEC + VCOL[name]:O_VEC + VCOL[name] + n].rearrange("p (c o) -> p c o", o=1)
        for name, (v, c, which, plus) in (("gx", ("g_pre_mix_2", 8, 0, 1.0)), ("gc", ("g_pre_mix_2", 8, 1, 1.0)),
                                          ("gf", ("g_pre_ffn_2", 32, 0, 1.0)), ("pm", ("g_post_mix_2", 16, 0, 0.0)),
                                          ("pf", ("g_post_ffn_2", 40, 0, 0.0))):
            if c != 8 * g:
                continue
            o = O_MOD + 96 + 8 * MOD_DERIVED.index(name)
            dve.scalar_tensor_tensor(out=k.M[:, o:o + KD].rearrange("p (c o) -> p c o", o=1), in0=self.MOD[:, c:c + KD, which:which + 1],
                                     scalar=plus, in1=vec(v), op0=ALU.add, op1=ALU.mult)


def mod_col(k, c, which=0):
    o = O_MOD + 2 * c + which
    return k.M[:, o:o + 1]


def derived_col(k, name, c):
    o = O_MOD + 96 + 8 * MOD_DERIVED.index(name) + c
    return k.M[:, o:o + 1]


def diff_projection(k, lead):
    t0 = k.plan
    k.plan += 6
    M = k.M
    A, C = view(M, A_A, KD, S), k.ctxT
    Q, K, V = view(M, D_Q, 4, S), view(M, D_K, 4, T_ALL), view(M, D_V, TT, 512)
    w = k.a["w_in_2"][0].rearrange("(c p) n -> p c n", p=P)
    read = k.sem("diff_read")
    halves = [("q", b) for b in range(4)] + [("k", b) for b in range(4)] + [("v", c, t) for c in range(2) for t in range(2)]
    rot, cos, sin = M[:, D_ROPE:D_ROPE + P], M[:, D_ROPE + P:D_ROPE + P + S], M[:, D_ROPE + P + S:D_ROPE + P + 2 * S]
    T = view(M, D_PT, 8, S)
    L = view(M, D_LAM, 4, HEAD)
    prod = view(M, D_P, 2, HEAD)
    lam = view(M, O_SML + 100, 4)
    turned, dots, exps, roped = k.sem("rotated"), k.sem("lam_dots"), k.sem("lam_exps"), k.sem("roped")
    blocks = [Q[:, n, :] for n in range(4)] + [K[:, n, NC_CTX:] for n in range(4)]
    k.lam = lam[:, 3:4]
    pair = lambda h: h if h < 4 else (h - 4) % 3
    turned_at = {4: (0,), 5: (1,), 6: (2,), 7: (3,), 8: (4, 5), 9: (6,), 10: (7,)}
    tok = lambda t: (lambda q: C[:, q, t * P:(t + 1) * P]) if t < 2 else (lambda q: A[:, q, (t - 2) * P:(t - 1) * P])

    def sync(k, sp):
        load_columns(k, w, 1696, 3232)
        for s in k.phase_end.values():
            sp.wait_ge(s, k.phase_index["layer_norm1"] + 1)
        sp.dma_start(M[:, D_ROPE:D_ROPE + P + 2 * S], k.a["const_rope"]).then_inc(k.rope_in, 16)
        for n, name in enumerate(("lam_q1_2", "lam_k1_2", "lam_q2_2", "lam_k2_2")):
            sp.dma_start(view(M, D_LAM, 4, HEAD)[:, n, :], k.a[name].broadcast_to([P, HEAD])).then_inc(k.rope_in, 16)

    def last_user(h):
        return max(g for g in range(h) if pair(g) == pair(h))

    def tensor(k, pe):
        for h, half in enumerate(halves):
            if h % 2 == 0:
                wt = k.pe_stream.take(KD, 256)
            if h >= 4:
                pe.wait_ge(read, last_user(h) + 1)
            two = [k.bank[2 * pair(h)], k.bank[2 * pair(h) + 1]]
            if h == 0:
                lead.block(k, pe, two[0], wt, lambda q: A[:, q, :])
                continue
            if half[0] == "v":
                for n in range(3):
                    dst = two[n // 2][:, (n % 2) * 256:(n % 2 + 1) * 256]
                    mm = block_token(pe, dst, tok(3 * half[2] + n), wt, KD)
            else:
                c0 = (half[1] % 2) * P
                if half[0] == "k":
                    block_feature(pe, two[1][:, :NC_CTX], wt, c0, P, lambda q: C[:, q, :], KD)
                mm = block_feature(pe, two[0], wt, c0, P, lambda q: A[:, q, :], KD)
            mm.then_inc(k.half_done, 1)
            if h == 4:
                pe.wait_ge(k.rope_in, 16 * 5)
            for n in turned_at.get(h, ()):
                pe.wait_ge(read, 4 if n < 4 else n + 1)
                if n >= 2:
                    pe.wait_ge(roped, n - 1)
                pe.matmul(k.bank[6 + n % 2], rot, blocks[n], start=True, stop=True).then_inc(turned, 1)

    def vector(k, dve):
        for h, half in enumerate(halves):
            dve.wait_ge(k.half_done, 2 * t0 + h + 1)
            o = 1024 * pair(h)
            if half[0] == "q":
                ins = dve.tensor_scalar(Q[:, half[1], :], k.psum[:, o:o + S], HEAD ** -0.5, None, ALU.mult)
            elif half[0] == "k":
                dve.tensor_copy(K[:, half[1], NC_CTX:], k.psum[:, o:o + S])
                ins = dve.tensor_copy(K[:, half[1], :NC_CTX], k.psum[:, o + S:o + S + NC_CTX])
            else:
                _, c, t = half
                ins = dve.tensor_copy(V[:, 3 * t:3 * t + 3, c * 256:(c + 1) * 256],
                                      k.psum[:, o:o + 768].rearrange("p (a b) -> p a b", a=3))
            ins.then_inc(read, 1)
            if h == 3:
                dve.wait_ge(k.rope_in, 16 * 5)
                for n in range(2):
                    k.dve.link(dve.tensor_tensor(prod[:, n, :], L[:, 2 * n, :], L[:, 2 * n + 1, :], ALU.mult))
                dve.tensor_reduce(lam[:, 0:2], prod, AX_X, ALU.add).then_inc(dots, 1)
            for n in turned_at.get(h, ()):
                dve.wait_ge(turned, n + 1)
                k.dve.link(dve.tensor_tensor(T[:, n, :], k.bank[6 + n % 2], sin, ALU.mult))
                k.dve.link(dve.tensor_tensor(blocks[n], blocks[n], cos, ALU.mult))
                dve.tensor_tensor(blocks[n], blocks[n], T[:, n, :], ALU.add).then_inc(roped, 1)
        dve.wait_ge(exps, 1)
        k.dve.link(dve.tensor_tensor(lam[:, 2:3], lam[:, 0:1], lam[:, 1:2], ALU.subtract))
        dve.tensor_scalar(lam[:, 3:4], lam[:, 2:3], LAM_INIT, None, ALU.add)

    def scalar(k, act):
        act.wait_ge(dots, 1)
        act.activation(lam[:, 0:2], lam[:, 0:2], ACT.Exp).then_inc(exps, 1)

    return Phase("diff_projection", sync=sync, tensor=tensor, vector=vector, scalar=scalar)


def diff_attention(k):
    M = k.M
    Q, K, V = view(M, D_Q, 4, S), view(M, D_K, 4, T_ALL), view(M, D_V, TT, 512)
    MIX = view(M, A_MIX, KD, S)
    PT, PR = view(M, D_PT, 2, TT, S), view(M, D_P, 2, 2, T_ALL)
    small = view(M, O_SML, 2, 2, 2)
    units = [(h, i) for h in range(4) for i in range(4)]
    scored, maxed, raised, ready, turned, copied, valued, taken = (
        k.sem(f"diff_{x}") for x in ("scored", "maxed", "raised", "ready", "turned", "copied", "valued", "taken"))
    score = lambda m: k.psum[:, 1024 * m:1024 * m + T_ALL]
    TURN = 4

    def values(pe, h):
        pe.wait_ge(copied, 4 * h + 4)
        if h >= 2:
            pe.wait_ge(taken, h - 1)
        for j in range(TT):
            mm = pe.matmul(k.bank[6 + h % 2], V[:, j, h * P:(h + 1) * P], PT[:, h % 2, j, :], start=j == 0, stop=j == TT - 1)
        mm.then_inc(valued, 1)

    def tensor(k, pe):
        for u in range(len(units) + 1):
            if u < len(units):
                h, i = units[u]
                for m in range(2):
                    if u >= 1:
                        pe.wait_ge(raised, 2 * u - 1 + m)
                    r = slice(64 * m, 64 * m + 64)
                    pe.matmul(k.bank[2 * m], Q[r, h, i * P:(i + 1) * P], K[r, h, 0:512], start=True, stop=True)
                    pe.matmul(k.bank[2 * m + 1][:, :256], Q[r, h, i * P:(i + 1) * P], K[r, h, 512:768], start=True,
                              stop=True).then_inc(scored, 1)
            if u >= 1:
                v = u - 1
                h, i = units[v]
                pe.wait_ge(ready, v + 1)
                if v >= 1:
                    pe.wait_ge(copied, v)
                for j in range(TT):
                    mm = pe.transpose(k.bank[TURN + j // 4][:, (j % 4) * P:(j % 4 + 1) * P],
                                      PR[:, v % 2, 0, j * P:(j + 1) * P], k.ident)
                mm.then_inc(turned, 1)
                if i == 1 and h >= 1:
                    values(pe, h - 1)
        values(pe, 3)

    def vector(k, dve):
        for u in range(len(units) + 1):
            if u >= 1:
                v = u - 1
                h, i = units[v]
                sm, pr = small[:, v % 2], PR[:, v % 2]
                dve.wait_ge(raised, 2 * v + 2)
                k.dve.link(dve.reciprocal(sm[:, :, 1:2], sm[:, :, 1:2]))
                k.dve.link(dve.tensor_tensor(sm[:, 1, 1:2], sm[:, 1, 1:2], k.lam, ALU.mult))
                k.dve.link(dve.tensor_scalar(pr[:, 1, :], pr[:, 1, :], sm[:, 1, 1:2], None, ALU.mult))
                dve.scalar_tensor_tensor(out=pr[:, 0, :], in0=pr[:, 0, :], scalar=sm[:, 0, 1:2], in1=pr[:, 1, :],
                                         op0=ALU.mult, op1=ALU.subtract).then_inc(ready, 1)
            if u < len(units):
                for m in range(2):
                    dve.wait_ge(scored, 2 * u + m + 1)
                    k.dve.link(dve.tensor_reduce(small[:, u % 2, m, 0:1], score(m), AX_X, ALU.max))
                    dve.tensor_scalar(small[:, u % 2, m, 0:1], small[:, u % 2, m, 0:1], -1.0, None, ALU.mult).then_inc(maxed, 1)
            if u >= 1 and i == 3 and h >= 1:
                take(dve, h - 1)
        take(dve, 3)

    def take(dve, h):
        dve.wait_ge(valued, h + 1)
        dve.tensor_copy(MIX[:, 4 + h, :], k.bank[6 + h % 2]).then_inc(taken, 1)

    def scalar(k, act):
        for u in range(len(units) + 2):
            if u < len(units):
                if u >= 2:
                    act.wait_ge(turned, u - 1)
                for m in range(2):
                    act.wait_ge(maxed, 2 * u + m + 1)
                    act.activation(PR[:, u % 2, m, :], score(m), ACT.Exp, bias=small[:, u % 2, m, 0:1],
                                   accum_out=small[:, u % 2, m, 1:2]).then_inc(raised, 1)
            if u >= 1 and u - 1 < len(units):
                v = u - 1
                h, i = units[v]
                act.wait_ge(turned, v + 1)
                if h >= 2:
                    act.wait_ge(valued, h - 1)
                act.activation(PT[:, h % 2, :, i * P:(i + 1) * P],
                               k.psum[:, 512 * TURN:512 * TURN + T_ALL].rearrange("p (j q) -> p j q", q=P),
                               ACT.Copy).then_inc(copied, 1)

    return Phase("diff_attention", tensor=tensor, vector=vector, scalar=scalar)


def diff_post(k):
    M = k.M
    O = view(M, A_MIX, KD, S)[:, 4:8, :]
    SQ = view(M, D_PT, 4, S)
    squared, summed, inv, rooted = (k.sem(f"diffpost_{x}") for x in ("squared", "summed", "inverted", "rooted"))
    k.diffpost_inverted = inv
    g = M[:, O_SML + 110:O_SML + 111]

    def scalar(k, act):
        act.activation(SQ, O, ACT.Square).then_inc(squared, 1)
        act.wait_ge(inv, 1)
        act.activation(SQ, SQ, ACT.Sqrt).then_inc(rooted, 1)

    def tensor(k, pe):
        pe.wait_ge(squared, 1)
        for n in range(4):
            mm = pe.matmul(k.bank[n], k.means, SQ[:, n, :], start=True, stop=True)
        mm.then_inc(summed, 1)

    def vector(k, dve):
        dve.tensor_scalar(g, col(k, "subln_w_2"), 1.0 - LAM_INIT, None, ALU.mult)
        dve.wait_ge(summed, 1)
        k.dve.link(dve.tensor_scalar(SQ, k.psum[:, 0:4 * S].rearrange("p (a b) -> p a b", a=4), D / P, SUBLN_EPS,
                                     ALU.mult, ALU.add))
        dve.reciprocal(SQ, SQ).then_inc(inv, 1)
        dve.wait_ge(rooted, 1)
        dve.scalar_tensor_tensor(out=O, in0=O, scalar=g, in1=SQ, op0=ALU.mult, op1=ALU.mult)

    return Phase("diff_post", tensor=tensor, vector=vector, scalar=scalar)


def rwkv_projection(k):
    t0 = k.plan
    k.plan += 7
    M = k.M
    A, C = view(M, A_A, KD, S), k.ctxT
    RKV = view(M, R_R, 12, T_ALL)
    WA, GL = view(M, R_WA, T_ALL), view(M, R_GL, S)
    w = k.a["w_in_2"][0].rearrange("(c p) n -> p c n", p=P)
    free, centred = k.sem("rwkv_bank_free"), k.sem("rwkv_centred")
    K, KK = view(M, R_K, 4, T_ALL), view(M, R_KK, 4, T_ALL)
    SQ, N = view(M, R_TMP, 2, T_ALL), view(M, R_TMP + 2 * T_ALL, 2, T_ALL)
    HEADSUM = M[:, R_TMP + 4 * T_ALL:R_TMP + 4 * T_ALL + P]
    scaled, squared, summed, rooted, floored = (k.sem(f"kk_{x}") for x in ("scaled", "squared", "summed", "rooted", "done"))
    pair = lambda h: h % 4 if h < 8 else (h - 8) % 3
    last_user = lambda h: max(g for g in range(h) if pair(g) == pair(h))
    norm_of = lambda h: h - 8 if 8 <= h < 12 else None

    def part(h):
        if h < 12:
            return RKV[:, h, :], [col(k, f"rwkv_tap{t}", h) for t in range(3)], P, (h % 2) * P
        name, m, c0, dst = (("rwkv_wa_taps", 64, 0, WA), ("rwkv_g_taps", 96, 64, GL))[h - 12]
        return dst[0:m, :], [col(k, name, t)[0:m, :] for t in range(3)], m, c0

    def segments(h):
        o = 1024 * pair(h)
        return [(o, 0, S)] if h == 13 else [(o, NC_CTX, S), (o + S, 0, NC_CTX)]

    def sync(k, sp):
        load_columns(k, w, 0, 1536)
        load_columns(k, w, 1536, 1696)
        for s in k.phase_end.values():
            sp.wait_ge(s, k.phase_index["diff_post"] + 1)
        c = MASKS["headsum"]
        sp.dma_start(HEADSUM, k.a["const_rwkv"][:, c:c + P]).then_inc(k.headsum_in, 16)

    def tensor(k, pe):
        for h in range(14):
            if h % 2 == 0:
                wt = k.pe_stream.take(KD, 256 if h < 12 else 160)
            if h >= 4:
                pe.wait_ge(free, last_user(h) + 1)
            if h == 0:
                pe.wait_ge(k.diffpost_inverted, 1)
            _, _, m, c0 = part(h)
            two = [k.bank[2 * pair(h)], k.bank[2 * pair(h) + 1]]
            if h != 13:
                block_feature(pe, two[1][0:m, :NC_CTX], wt, c0, m, lambda q: C[:, q, :], KD)
            block_feature(pe, two[0][0:m, :], wt, c0, m, lambda q: A[:, q, :], KD).then_inc(k.half_done, 1)
            if h == 0:
                settle(k, pe, "diff_post")
            f = norm_of(h)
            if f is not None:
                if f == 0:
                    pe.wait_ge(k.headsum_in, 16)
                    pe.wait_ge(free, 8)
                else:
                    pe.wait_ge(rooted, f)
                pe.wait_ge(squared, f + 1)
                pe.matmul(k.bank[6], HEADSUM, SQ[:, f % 2, 0:512], start=True, stop=True)
                pe.matmul(k.bank[7][:, :256], HEADSUM, SQ[:, f % 2, 512:768], start=True, stop=True).then_inc(summed, 1)

    def scalar(k, act):
        for h in range(14):
            f = norm_of(h)
            if f is not None:
                act.wait_ge(scaled, f + 1)
                if f >= 2:
                    act.wait_ge(summed, f - 1)
                act.activation(SQ[:, f % 2, :], KK[:, f, :], ACT.Square).then_inc(squared, 1)
            act.wait_ge(k.half_done, 2 * t0 + h + 1)
            dst, taps, m, _ = part(h)
            for o, d0, n in segments(h):
                ins = act.activation(dst[:, d0:d0 + n], k.psum[0:m, o:o + n], ACT.Copy, scale=taps[1])
            ins.then_inc(centred, 1)
            f = norm_of(h)
            if f is not None:
                act.wait_ge(summed, f + 1)
                if f >= 2:
                    act.wait_ge(floored, f - 1)
                act.activation(N[:, f % 2, :], k.psum[:, 512 * 6:512 * 6 + T_ALL], ACT.Sqrt).then_inc(rooted, 1)

    def vector(k, dve):
        for h in range(14):
            dve.wait_ge(centred, h + 1)
            dst, taps, m, _ = part(h)
            for n, (o, d0, cnt) in enumerate(segments(h)):
                x, y = k.psum[0:m, o:o + cnt], dst[:, d0:d0 + cnt]
                k.dve.link(dve.scalar_tensor_tensor(out=y[:, 1:cnt], in0=x[:, 0:cnt - 1], scalar=taps[0], in1=y[:, 1:cnt],
                                                    op0=ALU.mult, op1=ALU.add))
                ins = dve.scalar_tensor_tensor(out=y[:, 0:cnt - 1], in0=x[:, 1:cnt], scalar=taps[2], in1=y[:, 0:cnt - 1],
                                               op0=ALU.mult, op1=ALU.add)
            ins.then_inc(free, 1)
            if 4 <= h < 8:
                dve.wait_ge(free, h + 1)
                dve.tensor_scalar(KK[:, h - 4, :], K[:, h - 4, :], col(k, "k_k_2", h - 4), None, ALU.mult).then_inc(scaled, 1)
            f = norm_of(h)
            if f is not None:
                dve.wait_ge(rooted, f + 1)
                n = N[:, f % 2, :]
                k.dve.link(dve.tensor_scalar(n, n, 1e-12, None, ALU.max))
                k.dve.link(dve.reciprocal(n, n))
                dve.tensor_tensor(KK[:, f, :], KK[:, f, :], n, ALU.mult).then_inc(floored, 1)

    return Phase("rwkv_projection", sync=sync, tensor=tensor, vector=vector, scalar=scalar)


def mask(k, name, off=0, n=None):
    o = R_MASK + MASKS[name] + off
    return k.M[:, o:o + n]


def rwkv_prepare(k):
    M = k.M
    WA = view(M, R_WA, T_ALL)

    def sync(k, sp):
        for s in k.phase_end.values():
            sp.wait_ge(s, k.phase_index["rwkv_projection"] + 1)
        sp.dma_start(M[:, R_MASK:R_MASK + N_MASK], k.a["const_rwkv"]).then_inc(k.rwkv_in, 16)
        for d, s in enumerate(("fwd", "bwd")):
            sp.dma_start(view(M, R_W2, 2, 512)[0:32, d, :], k.a[f"w2_{s}_2"][0]).then_inc(k.rwkv_in, 16)
            sp.dma_start(view(M, R_A2, 2, 512)[0:32, d, :], k.a[f"a2_{s}_2"][0]).then_inc(k.rwkv_in, 16)
        sp.dma_start(M[0:96, R_G2:R_G2 + 512], k.a["g2_2"][0]).then_inc(k.rwkv_in, 16)

    def scalar(k, act):
        act.activation(WA[0:32, :], WA[0:32, :], ACT.Tanh)

    def tensor(k, pe):
        pe.wait_ge(k.rwkv_in, 16 * 6)

    def vector(k, dve):
        dve.tensor_copy(M[0:32, R_AL:R_AL + T_ALL], WA[32:64, :])

    return Phase("rwkv_prepare", sync=sync, tensor=tensor, vector=vector, scalar=scalar)


LEVELS = 5
NCH_CTX = NC_CTX // CH
TURNS = 3
LINKS = 9
MAIN_ONLY = ("ydone", "yout", "rho")


def rwkv_loop(k):
    M = k.M
    v4 = lambda o, *d: view(M, o, *d)
    half = lambda ap, d: ap[:, 4 * d:4 * d + 4]
    src = {n: v4(o, 4, T_ALL) for n, o in (("R", R_R), ("K", R_K), ("V", R_V), ("KK", R_KK))}
    latent, factor = (v4(R_WA, T_ALL), v4(R_AL, T_ALL)), (v4(R_W2, 2, 512), v4(R_A2, 2, 512))
    SIG = v4(R_SIG, 2, NPAIR, CH)
    PRE, POST = v4(R_PRE, NPAIR, CH), SIG[:, 0]
    KD_, KKA = v4(R_KD, NPAIR, CH), v4(R_KD + 512, NPAIR, CH)
    TH = v4(O_SML + 120, NPAIR)
    PHN = v4(O_SML + 128, NPAIR)
    PH = v4(O_SML + 136, NPAIR)
    AR, B_ = v4(R_AR, NPAIR, 2, CH), v4(R_B, NPAIR, CH)
    ABD, BBD, KBD, VBD = (v4(o, NPAIR, 2, CH) for o in (R_ABD, R_BBD, R_KBD, R_VBD))
    BTK, KTK, VTK = (v4(o, NPAIR, P) for o in (R_BTK, R_KTK, R_VTK))
    QK, QB, LT, RHO = (v4(o, NPAIR, CH) for o in (R_QK, R_QB, R_LT, R_RHO))
    XY, T_ = v4(R_X, 2, NPAIR, P), v4(R_T, NPAIR, P)
    KTBD, LOFF = v4(R_KTBD, NPAIR, 2, CH), v4(R_LOFF, NPAIR, 2, CH)
    KV, SA, ST, S0 = (v4(o, NPAIR, P) for o in (R_KV, R_SA, R_S, R_S0))
    YF, YB = v4(A_MIX, KD, S), v4(R_YB, 4, S)
    flat = lambda ap: ap.rearrange("p a b -> p (a b)")
    bd = lambda ap, p: ap[:, p].rearrange("p a b -> p (a b)")
    wide = lambda ap: ap.unsqueeze(2)
    m3 = lambda name, d, w: k.M[:, R_MASK + MASKS[name] + d * w:R_MASK + MASKS[name] + (d + 1) * w]
    sems = {n: k.sem(f"rwkv_{n}") for n in (
        "latents", "shifted", "sigmoid", "summed", "exps", "bd_ab", "bd_k", "bd_v", "grams", "gram_l", "gram2", "lt", "xy0",
        "kq", "turned", "tcopied", "loff", "tdone", "tst", "xydone", "xy", "kvdone", "kvst",
        "rho", "s0", "sadone", "sast", "sdone", "s", "ydone", "yout")}

    def parts(run):
        run(-1, None, 0, False, False, True)
        run(0, 3, 0, False, False, True)
        run(3, None, 0, False, True, True)
        run(4, 7, 0, True, True, True)
        run(11, None, 0, True, False, False)

    def step(n, i):
        def value(name, per, nth, ahead):
            return at(i, per, (n + ahead - (NCH_CTX if name in MAIN_ONLY else 0)) * per + nth)

        def wait(eng, name, per=1, nth=1, ahead=0):
            eng.wait_ge(sems[name], value(name, per, nth, ahead))

        def tokens(d):
            m = n + 1
            if d == 0:
                start = at(i, CH, m * CH)
            else:
                start = at(i, -CH, (NCH_CTX - 1 - m) * CH if m < NCH_CTX else T_ALL - CH - (m - NCH_CTX) * CH)
            return bass.ds(start, CH)

        def out_tokens(d):
            m = n - NCH_CTX
            return bass.ds(at(i, CH, m * CH) if d == 0 else at(i, -CH, S - CH - m * CH), CH)

        return wait, tokens, out_tokens

    def runner(eng, emit, chain=None):
        def run(n, trips, _, main, nxt_main, more):
            if trips is None:
                emit(n, None, main, nxt_main, more)
                return
            with eng.Fori(0, trips) as i:
                if chain:
                    chain.enter(i, LINKS)
                emit(n, i, main, nxt_main, more)
            if chain:
                chain.leave(trips)
        return run

    def tensor(k, pe):
        def emit(n, i, main, nxt_main, more):
            wait, tokens, out_tokens = step(n, i)
            n_ar = 2 if nxt_main else 1

            def latents():
                for which in range(2):
                    for d in range(2):
                        for f in range(4):
                            mm = pe.matmul(k.bank[which][:, (4 * d + f) * CH:(4 * d + f + 1) * CH],
                                           factor[which][0:32, d, f * P:(f + 1) * P], latent[which][0:32, tokens(d)], start=True, stop=True)
                            if which == d == 1 and f == 3:
                                mm.then_inc(sems["latents"], 1)
                            yield

            def gram(what, banks):
                for p in range(NPAIR):
                    mm = pe.matmul(k.bank[banks[p // 4]][:, (p % 4) * P:(p % 4) * P + n_ar * CH], bd(what, p),
                                   AR[:, p, 0:n_ar, :].rearrange("p a b -> p (a b)"), start=True, stop=True)
                return mm

            def gram_l():
                for p in range(NPAIR):
                    mm = pe.matmul(k.bank[5][:, p * CH:(p + 1) * CH], bd(ABD, p), B_[:, p, :], start=True, stop=True)
                mm.then_inc(sems["gram_l"], 1)

            def turn(what):
                for p in range(NPAIR):
                    mm = pe.transpose(k.bank[p // 4][:, (p % 4) * P:(p % 4 + 1) * P], bd(what, p), k.ident)
                mm.then_inc(sems["turned"], 1)

            def product(banks, lhs, rhs, more_terms=()):
                terms = ((lhs, rhs),) + more_terms
                for p in range(NPAIR):
                    for t, (u, v) in enumerate(terms):
                        mm = pe.matmul(k.bank[banks[p // 4]][:, (p % 4) * P:(p % 4 + 1) * P], u(p), v(p),
                                       start=t == 0, stop=t == len(terms) - 1)
                return mm

            if n < 0:
                for _ in latents():
                    pass
                wait(pe, "bd_ab", ahead=1)
                gram(BBD, (4, 6)).then_inc(sems["grams"], 1)
                gram_l()
                wait(pe, "bd_k", ahead=1)
                gram(KBD, (2, 3)).then_inc(sems["gram2"], 1)
                return
            wait(pe, "s", nth=1)
            wait(pe, "bd_v")
            turn(VBD)
            for lv in range(LEVELS):
                last = lv == LEVELS - 1
                for d in range(2):
                    if lv == 0 and d == 0:
                        wait(pe, "xy0")
                        wait(pe, "kq")
                    wait(pe, "loff", 2 * LEVELS, 2 * lv + d + 1)
                    if lv > 0:
                        wait(pe, "xy", 2 * LEVELS, 2 * (lv - 1) + d + 1)
                    for p in range(4 * d, 4 * d + 4):
                        mm = pe.matmul(k.bank[2 + d][:, (p % 4) * P:(p % 4 + 1) * P], bd(LOFF, p), XY[:, 0, p, :],
                                       start=True, stop=True)
                    mm.then_inc(sems["tdone"], 1)
                if lv == 0:
                    wait(pe, "tcopied", TURNS, 1)
                    aside = latents() if more else iter(())
                elif lv < 3:
                    if lv > 1:
                        wait(pe, "tcopied", TURNS, lv)
                    elif more:
                        wait(pe, "shifted", ahead=1)
                    turn((BBD, KBD)[lv - 1])
                elif lv == 3:
                    wait(pe, "tcopied", TURNS, TURNS)
                    wait(pe, "s0")
                    product((0, 1), lambda p: bd(KTBD, p), lambda p: VTK[:, p, :],
                            ((lambda p: bd(ABD, p), lambda p: S0[:, p, :]),)).then_inc(sems["kvdone"], 1)
                for d in range(2):
                    wait(pe, "tst", 2 * LEVELS, 2 * lv + d + 1)
                    if lv == 0 and d == 1 and main:
                        wait(pe, "yout", ahead=-1, nth=2)
                    for p in range(4 * d, 4 * d + 4):
                        o = (p % 4) * P
                        if not last:
                            pe.matmul(k.bank[4 + 2 * d][:, o:o + P], XY[:, 1, p, :], T_[:, p, :], start=True, stop=True)
                        mm = pe.matmul(k.bank[5 + 2 * d][:, o:o + P], T_[:, p, :], XY[:, 1, p, :], start=True, stop=True)
                        if p % 4 == 3:
                            mm.then_inc(sems["xydone"], 1)
                        if lv == 0:
                            next(aside, None)
                            next(aside, None)
            if more:
                wait(pe, "bd_ab", ahead=1)
                gram(BBD, (4, 6)).then_inc(sems["grams"], 1)
            wait(pe, "xy", 2 * LEVELS, 2 * LEVELS)
            if more:
                gram_l()
            wait(pe, "kvst")
            product((0, 1), lambda p: XY[:, 1, p, :], lambda p: KV[:, p, :]).then_inc(sems["sadone"], 1)
            if more:
                wait(pe, "bd_k", ahead=1)
                gram(KBD, (2, 3)).then_inc(sems["gram2"], 1)
            wait(pe, "sast")
            product((0, 1), lambda p: KTK[:, p, :], lambda p: VTK[:, p, :],
                    ((lambda p: BTK[:, p, :], lambda p: SA[:, p, :]),)).then_inc(sems["sdone"], 1)
            if main:
                wait(pe, "rho")
                for p in range(NPAIR):
                    o = k.bank[7][:, p * CH:(p + 1) * CH]
                    pe.matmul(o, S0[:, p, :], RHO[:, p, :], start=True, stop=False)
                    pe.matmul(o, VTK[:, p, :], QK[:, p, :], start=False, stop=False)
                    mm = pe.matmul(o, SA[:, p, :], QB[:, p, :], start=False, stop=True)
                mm.then_inc(sems["ydone"], 1)

        parts(runner(pe, emit))

    def scalar(k, act):
        act.sem_inc(sems["yout"], 1)

        def emit(n, i, main, nxt_main, more):
            wait, tokens, out_tokens = step(n, i)

            def rates():
                wait(act, "shifted", ahead=1)
                act.activation(SIG, SIG, ACT.Sigmoid).then_inc(sems["sigmoid"], 1)

            def exps():
                wait(act, "summed", ahead=1)
                if main:
                    wait(act, "rho")
                for dst, fwd, bwd in ((AR[:, :, 0, :], (1, 1), (0, -1)), (B_, (0, -1), (1, 1)), (AR[:, :, 1, :], (0, 1), (1, -1))):
                    if dst is not B_ and fwd[0] == 0 and not nxt_main:
                        continue
                    for d, (g, sign) in enumerate((fwd, bwd)):
                        act.activation(half(dst, d), half((PRE, POST)[g], d), ACT.Exp, scale=sign * DECAY)
                act.activation(PHN, TH, ACT.Exp, scale=DECAY).then_inc(sems["exps"], 1)

            def copied(m, dst, scale):
                wait(act, "turned", TURNS, m + 1)
                ins = act.activation(dst.rearrange("p a b -> p (a b)"), k.psum[:, 0:1024], ACT.Copy, scale=scale)
                ins.then_inc(sems["tcopied"], 1)

            if n < 0:
                rates()
                exps()
            else:
                copied(0, VTK, 1.0)
                for lv in range(LEVELS):
                    for d in range(2):
                        wait(act, "tdone", 2 * LEVELS, 2 * lv + d + 1)
                        act.activation(half(T_, d), k.bank[2 + d].rearrange("p (a b) -> p a b", a=4), ACT.Copy).then_inc(sems["tst"], 1)
                    if 1 <= lv < 3:
                        copied(lv, (BTK, KTK)[lv - 1], -1.0 if lv == 1 else 1.0)
                    if lv == 0 and main:
                        act.activation(RHO, AR[:, :, 1, :], ACT.Copy).then_inc(sems["rho"], 1)
                    if lv == 1 and more:
                        rates()
                    if lv == 2 and more:
                        exps()
                    if lv == 3:
                        wait(act, "kvdone")
                        act.activation(flat(KV), k.psum[:, 0:1024], ACT.Copy).then_inc(sems["kvst"], 1)
                if more:
                    wait(act, "bd_k", ahead=1)
                wait(act, "sadone")
                act.activation(flat(SA), k.psum[:, 0:1024], ACT.Copy).then_inc(sems["sast"], 1)
            if main:
                wait(act, "ydone")
                for d, Y in enumerate((YF, YB)):
                    ins = act.activation(Y[:, 0:4, out_tokens(d)],
                                         k.bank[7][:, 256 * d:256 * d + 256].rearrange("p (a b) -> p a b", a=4), ACT.Copy)
                ins.then_inc(sems["yout"], 1)

        parts(runner(act, emit))

    def vector(k, dve):
        dve.memset(ST, 0.0).then_inc(sems["s"], 1)

        def emit(n, i, main, nxt_main, more):
            wait, tokens, out_tokens = step(n, i)
            head = m3("head", 0, 2).unsqueeze(1).unsqueeze(3)
            full, hfull = [P, NPAIR, 2, CH], [P, 4, 2, CH]
            gram = lambda b, w: k.psum[:, 512 * b:512 * b + 512].rearrange("p (a w t) -> p a w t", a=4, w=2)[:, :, w, :]
            row = lambda name, d: m3(name, d, CH).unsqueeze(1).broadcast_to([P, 4, CH])

            def shift():
                offs = M[:, O_VEC + VCOL["w0_fwd_2"]:O_VEC + VCOL["w0_fwd_2"] + 16].rearrange("p (d w f o) -> p w d f o", d=2, w=2, o=1)
                wait(dve, "latents", ahead=1)
                for w in range(2):
                    for d in range(2):
                        ins = dve.tensor_tensor(half(SIG[:, w], d), k.bank[w][:, 256 * d:256 * d + 256].rearrange("p (a b) -> p a b", a=4),
                                                offs[:, w, d].broadcast_to([P, 4, CH]), ALU.add)
                ins.then_inc(sems["shifted"], 1)

            def cumulate():
                wait(dve, "sigmoid", ahead=1)
                k.dve.link(dve.tensor_tensor_scan(flat(PRE), mask(k, "reset", 0, 512), flat(POST), 0.0, ALU.mult, ALU.add))
                k.dve.link(dve.tensor_scalar(TH.unsqueeze(2), PRE[:, :, CH - 1:CH], 0.5, None, ALU.mult))
                k.dve.link(dve.tensor_tensor(PRE, PRE, TH.unsqueeze(2).broadcast_to([P, NPAIR, CH]), ALU.subtract))
                dve.tensor_tensor(POST, PRE, POST, ALU.subtract).then_inc(sems["summed"], 1)

            def rated():
                ka = M[:, O_VEC + VCOL["k_a_2"]:O_VEC + VCOL["k_a_2"] + 4].unsqueeze(2).broadcast_to([P, 4, CH])
                for d in range(2):
                    dve.tensor_tensor(half(KKA, d), src["KK"][:, :, tokens(d)], half(SIG[:, 1], d), ALU.mult)
                    ins = dve.scalar_tensor_tensor(out=half(KD_, d), in0=half(SIG[:, 1], d), scalar=-1.0, in1=ka, op0=ALU.add, op1=ALU.mult)
                k.dve.link(ins)
                for d in range(2):
                    ins = dve.scalar_tensor_tensor(out=half(KD_, d), in0=half(KD_, d), scalar=1.0, in1=src["K"][:, :, tokens(d)],
                                                   op0=ALU.add, op1=ALU.mult)
                k.dve.link(ins)

            def alpha_beta():
                wait(dve, "exps", ahead=1)
                for d in range(2):
                    dve.tensor_tensor(half(AR, d)[:, :, 0, :], half(AR, d)[:, :, 0, :], src["KK"][:, :, tokens(d)], ALU.mult)
                    if nxt_main:
                        dve.tensor_tensor(half(AR, d)[:, :, 1, :], half(AR, d)[:, :, 1, :], src["R"][:, :, tokens(d)], ALU.mult)
                dve.tensor_tensor(KD_, KD_, B_, ALU.mult)
                k.dve.link(dve.tensor_tensor(B_, KKA, B_, ALU.mult))

            def diagonal_ab():
                if n >= 0:
                    wait(dve, "kvdone")
                dve.tensor_tensor(ABD, AR[:, :, 0:1, :].broadcast_to(full), head.broadcast_to(full), ALU.mult)
                dve.tensor_tensor(BBD, wide(B_).broadcast_to(full), head.broadcast_to(full), ALU.mult).then_inc(sems["bd_ab"], 1)

            def diagonal_k():
                dve.tensor_tensor(KBD, wide(KD_).broadcast_to(full), head.broadcast_to(full), ALU.mult).then_inc(sems["bd_k"], 1)

            def next_xy():
                wait(dve, "grams", ahead=1)
                if n >= 0:
                    wait(dve, "loff", 2 * LEVELS, 2 * LEVELS)
                for d in range(2):
                    ins = dve.tensor_copy(half(LT, d), gram(4 + 2 * d, 0))
                ins.then_inc(sems["lt"], 1)
                blocks = lambda name, d: m3(name, d, P).rearrange("p (h t) -> p h t", h=2).unsqueeze(1).broadcast_to(hfull)
                as_heads = lambda w, d: half(XY[:, w], d).rearrange("p a (h t) -> p a h t", h=2)
                wait(dve, "gram_l", ahead=1)
                for d in range(2):
                    dve.tensor_tensor(as_heads(0, d), wide(k.bank[5][:, 256 * d:256 * d + 256].rearrange("p (a b) -> p a b", a=4)).broadcast_to(hfull),
                                      blocks("x1", d), ALU.mult)
                if n >= 0:
                    wait(dve, "sadone")
                for d in range(2):
                    ins = dve.tensor_tensor(as_heads(1, d), gram(4 + 2 * d, 0).unsqueeze(2).broadcast_to(hfull), blocks("y1", d), ALU.mult)
                k.dve.link(ins)
                both = XY.rearrange("p w a t -> p (w a) t")
                dve.tensor_tensor(both, both, k.ident.unsqueeze(1).broadcast_to([P, 2 * NPAIR, P]), ALU.add).then_inc(sems["xy0"], 1)

            def next_kq():
                wait(dve, "gram2", ahead=1)
                for d in range(2):
                    st = m3("strict", d, P).rearrange("p (h t) -> p h t", h=2).unsqueeze(1).broadcast_to(hfull)
                    ins = dve.tensor_tensor(half(KTBD, d), gram(2 + d, 0).unsqueeze(2).broadcast_to(hfull), st, ALU.mult)
                if main:
                    wait(dve, "ydone")
                if nxt_main:
                    for d in range(2):
                        dve.tensor_tensor(half(QB, d), gram(4 + 2 * d, 1), row("neg", d), ALU.mult)
                        ins = dve.tensor_tensor(half(QK, d), gram(2 + d, 1), row("incl", d), ALU.mult)
                ins.then_inc(sems["kq"], 1)

            def state():
                wait(dve, "sdone")
                k.dve.link(dve.tensor_tensor(flat(ST), flat(S0), k.psum[:, 0:1024], ALU.add))
                dve.tensor_tensor(ST, ST, PH.unsqueeze(2).broadcast_to([P, NPAIR, P]), ALU.mult).then_inc(sems["s"], 1)

            if n < 0:
                for part in (shift, cumulate, rated, alpha_beta, diagonal_ab, diagonal_k, next_xy, next_kq):
                    part()
                return
            wait(dve, "exps")
            wait(dve, "s")
            k.dve.link(dve.tensor_copy(PH, PHN))
            dve.tensor_tensor(S0, ST, PH.unsqueeze(2).broadcast_to([P, NPAIR, P]), ALU.mult).then_inc(sems["s0"], 1)
            beside = {0: (shift,), 1: (cumulate, rated), 2: (alpha_beta,), 3: (diagonal_ab,), 4: (diagonal_k,)}
            for lv in range(LEVELS):
                for d in range(2):
                    wait(dve, "xydone", 2 * LEVELS, 2 * lv + d + 1)
                    w = 0 if lv < LEVELS - 1 else 1
                    xy = XY[:, w:, 4 * d:4 * d + 4, :]
                    new = k.psum[:, (4 + 2 * d + w) * 512:(6 + 2 * d) * 512].rearrange("p (w a t) -> p w a t", w=2 - w, a=4)
                    dve.tensor_tensor(xy, xy, new, ALU.subtract).then_inc(sems["xy"], 1)
                for part in beside[lv] if more else ():
                    part()
            if more:
                next_xy()
            state()
            if more:
                next_kq()

        parts(runner(dve, emit, k.dve))

    def pool(k, pool):
        def emit(n, i, main, nxt_main, more):
            wait, tokens, out_tokens = step(n, i)
            hfull = [P, 4, 2, CH]
            head = m3("head", 0, 2).unsqueeze(1).unsqueeze(3).broadcast_to(hfull)

            def loff(lv, d):
                m = m3("level", 2 * lv + d, P).rearrange("p (h t) -> p h t", h=2).unsqueeze(1).broadcast_to(hfull)
                pool.tensor_tensor(half(LOFF, d), wide(half(LT, d)).broadcast_to(hfull), m, ALU.mult).then_inc(sems["loff"], 1)

            def diagonal_v():
                if n >= 0:
                    wait(pool, "turned", TURNS, 1)
                for d in range(2):
                    ins = pool.tensor_tensor(half(VBD, d), wide(src["V"][:, :, tokens(d)]).broadcast_to(hfull), head, ALU.mult)
                ins.then_inc(sems["bd_v"], 1)

            if n >= 0:
                for lv in range(LEVELS):
                    for d in range(2):
                        if lv > 0:
                            wait(pool, "tdone", 2 * LEVELS, 2 * (lv - 1) + d + 1)
                            loff(lv, d)
                if more:
                    diagonal_v()
            else:
                diagonal_v()
            if more:
                wait(pool, "lt", ahead=1)
                for d in range(2):
                    loff(0, d)

        parts(runner(pool, emit))

    return Phase("rwkv_loop", tensor=tensor, vector=vector, scalar=scalar, pool=pool)


def rwkv_output(k):
    M = k.M
    R, K, V = view(M, R_R, 4, T_ALL), view(M, R_K, 4, T_ALL), view(M, R_V, 4, T_ALL)
    AL, GL, A2 = view(M, R_AL, T_ALL), view(M, R_GL, S), view(M, R_A2, 2, 512)
    Y, YB = view(M, A_MIX, 4, S), view(M, R_YB, 4, S)
    SQ, AF, AB, T = view(M, A_A, 4, S), view(M, A_A + 2048, 4, S), view(M, A_A + 4096, 4, S), view(M, A_A + 6144, 4, S)
    G2 = M[0:96, R_G2:R_G2 + 512]
    lo, hi = k.psum[:, 0:2048].rearrange("p (a b) -> p a b", a=4), k.psum[:, 2048:4096].rearrange("p (a b) -> p a b", a=4)
    a, b = k.sem("rwkv_out_product"), k.sem("rwkv_out_vector")
    c = k.sem("rwkv_out_scalar")
    cc = lambda name, f: col(k, name, f)

    def tensor(k, pe):
        headsum = mask(k, "headsum", 0, P)

        def each(base, lhsT, rhs):
            for f in range(4):
                mm = pe.matmul(k.bank[base + f], lhsT(f), rhs(f), start=True, stop=True)
            mm.then_inc(a, 1)

        each(4, lambda f: A2[0:32, 0, f * P:(f + 1) * P], lambda f: AL[0:32, NC_CTX:])
        pe.wait_ge(b, 1)
        each(0, lambda f: headsum, lambda f: Y[:, f, :])
        pe.wait_ge(c, 1)
        each(4, lambda f: A2[0:32, 1, f * P:(f + 1) * P], lambda f: AL[0:32, NC_CTX:])
        pe.wait_ge(b, 2)
        pe.wait_ge(c, 3)
        each(0, lambda f: headsum, lambda f: SQ[:, f, :])
        pe.wait_ge(b, 3)
        each(4, lambda f: headsum, lambda f: T[:, f, :])
        pe.wait_ge(b, 4)
        pe.wait_ge(c, 4)
        each(0, lambda f: G2[:, f * P:(f + 1) * P], lambda f: GL[0:96, :])

    def scalar(k, act):
        def rate(dst, name):
            for f in range(4):
                ins = act.activation(dst[:, f, :], k.bank[4 + f], ACT.Sigmoid, bias=cc(name, f))
            ins.then_inc(c, 1)

        act.wait_ge(a, 1)
        rate(AF, "a0_fwd_2")
        act.wait_ge(a, 3)
        rate(AB, "a0_bwd_2")
        act.wait_ge(b, 2)
        act.activation(SQ, Y, ACT.Square).then_inc(c, 1)
        act.activation(GL[0:96, :], GL[0:96, :], ACT.Sigmoid).then_inc(c, 1)
        act.wait_ge(b, 5)
        act.activation(SQ, SQ, ACT.Sqrt).then_inc(c, 1)

    def vector(k, dve):
        dve.tensor_tensor(Y, Y, YB, ALU.add).then_inc(b, 1)
        dve.wait_ge(b, 1)
        dve.wait_ge(a, 2)
        dve.scalar_tensor_tensor(out=Y, in0=lo, scalar=-1.0 / HEAD, in1=Y, op0=ALU.mult, op1=ALU.add).then_inc(b, 1)
        dve.wait_ge(c, 2)
        k.dve.link(dve.tensor_tensor(AF, AF, AB, ALU.add))
        k.dve.link(dve.tensor_scalar(AF, AF, 0.5, -1.0, ALU.mult, ALU.add))
        for f in range(4):
            ins = dve.tensor_scalar(AF[:, f, :], AF[:, f, :], cc("k_a_2", f), 1.0, ALU.mult, ALU.add)
        k.dve.link(ins)
        k.dve.link(dve.tensor_tensor(AF, AF, K[:, :, NC_CTX:], ALU.mult))
        for f in range(4):
            ins = dve.scalar_tensor_tensor(out=T[:, f, :], in0=R[:, f, NC_CTX:], scalar=cc("r_k_2", f), in1=AF[:, f, :],
                                           op0=ALU.mult, op1=ALU.mult)
        ins.then_inc(b, 1)
        dve.wait_ge(a, 4)
        dve.tensor_scalar(SQ, lo, 1.0 / HEAD, LN_X_EPS, ALU.mult, ALU.add).then_inc(b, 1)
        dve.wait_ge(b, 4)
        dve.reciprocal(SQ, SQ).then_inc(b, 1)
        dve.wait_ge(a, 5)
        k.dve.link(dve.tensor_tensor(AB, hi, V[:, :, NC_CTX:], ALU.mult))
        dve.wait_ge(c, 5)
        for f in range(4):
            ins = dve.scalar_tensor_tensor(out=Y[:, f, :], in0=Y[:, f, :], scalar=cc("ln_x_w_2", f), in1=SQ[:, f, :],
                                           op0=ALU.mult, op1=ALU.mult)
        k.dve.link(ins)
        for f in range(4):
            ins = dve.scalar_tensor_tensor(out=Y[:, f, :], in0=Y[:, f, :], scalar=cc("ln_x_b_2", f), in1=AB[:, f, :],
                                           op0=ALU.add, op1=ALU.add)
        k.dve.link(ins)
        dve.wait_ge(a, 6)
        dve.tensor_tensor(Y, Y, lo, ALU.mult)

    def sync(k, sp):
        for s in k.phase_end.values():
            sp.wait_ge(s, k.phase_index["rwkv_output"] + 1)

    return Phase("rwkv_output", tensor=tensor, vector=vector, scalar=scalar, sync=sync)


def second_block_phases(k, stop):
    M = k.M
    k.rope_in, k.rwkv_in, k.headsum_in = k.sem("rope_in"), k.sem("rwkv_in"), k.sem("headsum_in")
    A, Y = view(M, A_A, KD, S), view(M, A_Y, KD, S)
    ph = []
    ph += [diff_projection(k, k.second_lead), diff_attention(k)]
    k.adaptive.rows = k.memT.rearrange("p a b -> p (a b)")[0:2, 0:1024]
    ph.append(k.adaptive.part(k, diff_post(k), (0,)))
    ph[-1].soft = True
    ph += [rwkv_projection(k), rwkv_prepare(k), rwkv_loop(k), rwkv_output(k)]
    if stop == "mix2":
        return ph
    post = make_norm(k, "mix_post2", Y, S, [], A_SCR)
    ph.append(output_projection(k, "output_projection2", k.a["w_out_2"][0], post))
    pre = make_norm(k, "ffn_pre2", k.H, S, [(lambda c: derived_col(k, "gf", c), A, lambda c: mod_col(k, 24 + c))], A_HID, after=post)
    ph.append(k.adaptive.part(k, norm_phase(k, "ffn_norm2", [pre], post=(post, lambda c: derived_col(k, "pm", c))), (0, 3)))
    lead = Lead(ph[-1], pre)
    if stop == "hmix2":
        return ph
    conv = [{"tap0": VCOL["ffn_tap0"] + off, "tap1": VCOL["ffn_tap1"] + off, "tap2": VCOL["ffn_tap2"] + off,
             "bias": VCOL["ffn_conv_b_2"] + off} for off in (0, KF)]
    w = k.a["w_up_2"][0]
    ph.append(ffn_up(k, "ffn_up2", w, w, 0, D_FF, A_TMP, lead, conv))
    post = make_norm(k, "ffn_post2", Y, S, [], A_SCR)
    ph.append(ffn_down(k, "ffn_down2", k.a["w_down_2"][0], post))
    ph.append(norm_phase(k, "layer_norm2", [], post=(post, lambda c: derived_col(k, "pf", c))))
    return ph


def final_phase(k, out):
    X = view(k.M, A_A, 4, D)
    turned, copied = k.sem("out_turned"), k.sem("out_copied")
    o = out[0].rearrange("(t p) d -> t p d", p=P)

    def tensor(k, pe):
        for n in range(8):
            if n >= 4:
                pe.wait_ge(copied, n - 3)
            for j in range(4):
                f = (n % 2) * 4 + j
                mm = pe.transpose(k.bank[n % 4][:, j * P:(j + 1) * P], k.H[:, f, (n // 2) * P:(n // 2 + 1) * P], k.ident)
            mm.then_inc(turned, 1)

    def vector(k, dve):
        for n in range(8):
            dve.wait_ge(turned, n + 1)
            dve.tensor_copy(X[:, n // 2, (n % 2) * 512:(n % 2 + 1) * 512], k.bank[n % 4][:, :]).then_inc(copied, 1)

    def sync(k, sp):
        for t in range(4):
            sp.wait_ge(copied, 2 * t + 2)
            sp.dma_start(o[t], X[:, t, :]).then_inc(k.out_sent, 16)
        sp.wait_ge(k.out_sent, 64)

    return Phase("final", sync=sync, tensor=tensor, vector=vector)


_INS = ['x', 'mem', 'ln_mix_pre', 'ln_mix_post', 'ln_ffn_pre', 'ln_ffn_post', 'ln_mem', 'w_mem_kv', 'w_out',
        'w_ffn_gate', 'w_ffn_up', 'w_ffn_down', 'w_in_a', 'w_spatial', 'b_spatial', 'ln_v_g', 'ln_v_b', 'ln_shared',
        'w_shared_kv', 'b_forget', 'w_in_b', 'c_2', 'ctx_2', 'c_ctx_2', 'w_mod_2', 'b_mod_2', 'g_pre_mix_2',
        'g_post_mix_2', 'g_pre_ffn_2', 'g_post_ffn_2', 'w_in_2', 'rwkv_conv_2', 'w0_fwd_2', 'w2_fwd_2', 'a0_fwd_2',
        'a2_fwd_2', 'w0_bwd_2', 'w2_bwd_2', 'a0_bwd_2', 'a2_bwd_2', 'g2_2', 'k_k_2', 'k_a_2', 'r_k_2', 'ln_x_w_2',
        'ln_x_b_2', 'lam_q1_2', 'lam_k1_2', 'lam_q2_2', 'lam_k2_2', 'subln_w_2', 'w_out_2', 'w_up_2', 'ffn_conv_2',
        'ffn_conv_b_2', 'w_down_2']


def shape_constants():
    p = np.arange(P)
    ident = np.eye(P, dtype=np.float32)
    means = np.full((P, P), 1.0 / D, np.float32)
    causal = np.where(p[None, :] <= p[:, None], 0.0, NEG).astype(np.float32)
    lower = (p[None, :] >= p[:, None]).astype(np.float32)
    inv = (np.float32(10000.0) ** (-np.arange(16, dtype=np.float32) / np.float32(16))).astype(np.float32)
    t = np.arange(S)
    ang = np.concatenate([(t // 64).astype(np.float32)[:, None] * inv, (t % 64).astype(np.float32)[:, None] * inv], 1)
    table = ang.T[p % 32].astype(np.float32)
    rot = np.zeros((P, P), np.float32)
    for m in range(P):
        if m % 64 < 32:
            rot[m + 32, m] = -1.0
        else:
            rot[m - 32, m] = 1.0
    a, hd = p % CH, p // CH
    b = np.arange(CH)
    same2 = a[:, None] // 2 == b[None, :] // 2
    later = [b[None, :] > a[:, None], b[None, :] < a[:, None]]
    earlier = [b[None, :] < a[:, None], b[None, :] > a[:, None]]
    eye = a[:, None] == b[None, :]
    head = hd[:, None] == np.arange(2)[None, :]
    spread = lambda m: (head[:, :, None] & m[:, None, :]).reshape(P, P)
    levels = []
    for lv in range(LEVELS):
        size = 4 << lv
        for d in range(2):
            same = (a[:, None] // size == b[None, :] // size) & (a[:, None] // (size // 2) != b[None, :] // (size // 2))
            levels.append(spread(same & later[d]))
    parts = {"head": head, "x1": np.concatenate([-1.0 * spread(same2 & earlier[d]) for d in range(2)], 1),
             "y1": np.concatenate([-1.0 * spread(same2 & later[d]) for d in range(2)], 1),
             "incl": np.concatenate([later[d] | eye for d in range(2)], 1),
             "neg": np.concatenate([-1.0 * (later[d] | eye) for d in range(2)], 1),
             "strict": np.concatenate([spread(later[d]) for d in range(2)], 1), "level": np.concatenate(levels, 1),
             "reset": np.tile((np.arange(512) % CH != 0)[None, :], (P, 1)), "headsum": hd[:, None] == hd[None, :]}
    rwkv = np.concatenate([parts[n].astype(np.float32) for n in MASKS], 1)
    return {"const_base": np.concatenate([ident, means, causal, lower], 1),
            "const_rope": np.concatenate([rot, np.cos(table), np.sin(table)], 1), "const_rwkv": rwkv}


def kernel(**inputs):
    import concourse.bacc as _bacc
    from concourse.bass_utils import run_bass_kernel_spmd as _run

    nc = _bacc.Bacc("TRN2", target_bir_lowering=False, num_devices=1)
    arrays, aps = {}, {}
    for name, a in list((n, inputs[n]) for n in _INS) + list(shape_constants().items()):
        a = np.ascontiguousarray(a)
        arrays[f"in_{name}_dram"] = a
        aps[name] = nc.dram_tensor(f"in_{name}_dram", a.shape, mybir.dt.from_np(a.dtype), kind="ExternalInput").ap()
    out = nc.dram_tensor("out_0_dram", (1, S, D), F32, kind="ExternalOutput").ap()
    build(nc, aps, out)
    r = _run(nc, [arrays], core_ids=[0])
    return r.results[0]["out_0_dram"]
```
